# Optimizing a Trainium2 kernel written in Bass

```python
import math
import jax, jax.numpy as jnp
from jax import lax
import numpy as np

D_MODEL = 1024
BATCH = 1
SEQ = 256
DEPTH = 2

N_EVEN = (DEPTH + 1) // 2
N_ODD = DEPTH // 2
HEAD_DIM = 64
A_Q_HEADS = D_MODEL // 128
A_KV_HEADS = A_Q_HEADS // 4
A_GROUP = A_Q_HEADS // A_KV_HEADS
A_WIDTH = A_Q_HEADS * HEAD_DIM
KV_WIDTH = A_KV_HEADS * HEAD_DIM
WINDOW = 128
BLOCK = 128
ROPE_THETA = 10000.0
NEG_INF = -1e30
B_GROUPS = D_MODEL // 128
B_GROUP_DIM = 64
B_WIDTH = B_GROUPS * B_GROUP_DIM
CHUNK = 128
IN_WIDTH = A_WIDTH + 2 * KV_WIDTH + 2 * B_WIDTH
MIX_WIDTH = A_WIDTH + B_WIDTH
S5_GROUP = 16
S5_GROUPS = D_MODEL // S5_GROUP
S5_STATE = 64
D_FF = ((8 * D_MODEL // 3 + 127) // 128) * 128
N_EXPERTS = 8
TOP_K = 2
ALPHA = (2.0 * DEPTH) ** 0.25
BETA = (8.0 * DEPTH) ** -0.25
LN_EPS = 1e-5

kernel_name = 'hybrid_window_gqa_gmlp_s5_moe_encoder'

def layer_norm(x, g, b):
    xf = x.astype(jnp.float32)
    mu = xf.mean(-1, keepdims=True)
    var = jnp.square(xf - mu).mean(-1, keepdims=True)
    return ((xf - mu) * lax.rsqrt(var + LN_EPS) * g.astype(jnp.float32) + b.astype(jnp.float32)).astype(x.dtype)

def rope_tables(seq):
    pos = jnp.arange(seq, dtype=jnp.float32)
    inv_freq = ROPE_THETA ** (-jnp.arange(0, HEAD_DIM, 2, dtype=jnp.float32) / HEAD_DIM)
    ang = pos[:, None] * inv_freq[None, :]
    return jnp.cos(ang), jnp.sin(ang)

def apply_rope(x, cos, sin):
    xf = x.astype(jnp.float32)
    x1, x2 = jnp.split(xf, 2, axis=-1)
    c = cos[None, :, None, :]
    s = sin[None, :, None, :]
    return jnp.concatenate([x1 * c - x2 * s, x2 * c + x1 * s], axis=-1).astype(x.dtype)

def window_attention(q, k, v, sink):
    Bsz, S = q.shape[0], q.shape[1]
    nb = S // BLOCK
    qb = q.reshape(Bsz, nb, BLOCK, A_KV_HEADS, A_GROUP, HEAD_DIM)

    def neighbours(t):
        tp = jnp.pad(t, ((0, 0), (BLOCK, BLOCK), (0, 0), (0, 0))).reshape(Bsz, nb + 2, BLOCK, A_KV_HEADS, HEAD_DIM)
        return jnp.concatenate([tp[:, :-2], tp[:, 1:-1], tp[:, 2:]], axis=2)

    kb, vb = neighbours(k), neighbours(v)
    scores = jnp.einsum('bnqhgd,bnshd->bnhgqs', qb, kb, preferred_element_type=jnp.float32) * (HEAD_DIM ** -0.5)
    blk = jnp.arange(nb)[:, None]
    qpos = blk * BLOCK + jnp.arange(BLOCK)[None, :]
    kpos = blk * BLOCK - BLOCK + jnp.arange(3 * BLOCK)[None, :]
    kp = kpos[:, None, :]
    valid = (jnp.abs(kp - qpos[:, :, None]) <= WINDOW) & (kp >= 0) & (kp < S)
    scores = jnp.where(valid[None, :, None, None], scores, NEG_INF)
    sink_l = sink.astype(jnp.float32).reshape(1, 1, A_KV_HEADS, A_GROUP, 1, 1)
    m = jnp.maximum(scores.max(-1, keepdims=True), sink_l)
    p = jnp.exp(scores - m)
    denom = p.sum(-1, keepdims=True) + jnp.exp(sink_l - m)
    probs = (p / denom).astype(v.dtype)
    out = jnp.einsum('bnhgqs,bnshd->bnqhgd', probs, vb)
    return out.reshape(Bsz, S, A_WIDTH)

def spatial_gating(z_u, z_v, w_s, b_s, ln_g, ln_b):
    Bsz, S = z_u.shape[0], z_u.shape[1]
    u = jax.nn.gelu(z_u)
    v = layer_norm(jax.nn.gelu(z_v), ln_g, ln_b)
    vc = v.reshape(Bsz, S // CHUNK, CHUNK, B_GROUPS, B_GROUP_DIM)
    sv = jnp.einsum('gpq,bnqgd->bnpgd', w_s, vc) + b_s.T[None, None, :, :, None]
    return (u * sv.reshape(Bsz, S, B_GROUPS, B_GROUP_DIM)).reshape(Bsz, S, B_WIDTH)

def mixer_ab(x, w_in, sink, w_s, b_s, sgu_g, sgu_b, w_out, cos, sin):
    Bsz, S, _ = x.shape
    h = x @ w_in
    q, k, v, z_u, z_v = jnp.split(h, [A_WIDTH, A_WIDTH + KV_WIDTH, A_WIDTH + 2 * KV_WIDTH,
                                      A_WIDTH + 2 * KV_WIDTH + B_WIDTH], axis=-1)
    q = apply_rope(q.reshape(Bsz, S, A_Q_HEADS, HEAD_DIM), cos, sin)
    k = apply_rope(k.reshape(Bsz, S, A_KV_HEADS, HEAD_DIM), cos, sin)
    v = v.reshape(Bsz, S, A_KV_HEADS, HEAD_DIM)
    a_out = window_attention(q, k, v, sink)
    b_out = spatial_gating(z_u.reshape(Bsz, S, B_GROUPS, B_GROUP_DIM), z_v.reshape(Bsz, S, B_GROUPS, B_GROUP_DIM),
                           w_s, b_s, sgu_g, sgu_b)
    return jnp.concatenate([a_out, b_out], axis=-1) @ w_out

def _ssm_combine(left, right):
    a_l, b_l = left
    a_r, b_r = right
    return a_r * a_l, a_r * b_l + b_r

def mixer_c(x, lam_re, lam_im, log_dt, b_re, b_im, c_re, c_im, d_skip, w_val, w_gate):
    Bsz, S, _ = x.shape
    u = x.astype(jnp.float32).reshape(Bsz, S, S5_GROUPS, S5_GROUP)
    uc = u.astype(jnp.complex64)
    y = d_skip.astype(jnp.float32) * u
    for direction, reverse in ((0, False), (1, True)):
        lam = lax.complex(lam_re[direction].astype(jnp.float32), lam_im[direction].astype(jnp.float32))
        dt = jnp.exp(log_dt[direction].astype(jnp.float32))[:, None]
        lam_bar = jnp.exp(lam * dt)
        bmat = lax.complex(b_re[direction].astype(jnp.float32), b_im[direction].astype(jnp.float32))
        b_bar = ((lam_bar - 1.0) / lam)[..., None] * bmat
        bu = jnp.einsum('gpc,bsgc->bsgp', b_bar, uc)
        a = jnp.broadcast_to(lam_bar, (1, S, S5_GROUPS, S5_STATE))
        _, states = lax.associative_scan(_ssm_combine, (a, bu), reverse=reverse, axis=1)
        cmat = lax.complex(c_re[direction].astype(jnp.float32), c_im[direction].astype(jnp.float32))
        y = y + jnp.einsum('gcp,bsgp->bsgc', cmat, states).real
    y = jax.nn.gelu(y.reshape(Bsz, S, D_MODEL)).astype(x.dtype)
    return (y @ w_val) * jax.nn.sigmoid(y @ w_gate)

def swiglu(x, w_gate, w_up, w_down):
    return (jax.nn.silu(x @ w_gate) * (x @ w_up)) @ w_down

def moe_swiglu(x, router_w, w_gate, w_up, w_down):
    Bsz, S, D = x.shape
    t = x.reshape(-1, D)
    logits = jnp.dot(t, router_w, preferred_element_type=jnp.float32)
    top_val, top_idx = lax.top_k(logits, TOP_K)
    top_w = jax.nn.softmax(top_val, axis=-1)
    combine = jnp.einsum('tk,tke->te', top_w, jax.nn.one_hot(top_idx, N_EXPERTS, dtype=jnp.float32))
    out = jnp.zeros_like(t)
    for e in range(N_EXPERTS):
        out = out + combine[:, e:e + 1].astype(t.dtype) * swiglu(t, w_gate[e], w_up[e], w_down[e])
    return out.reshape(Bsz, S, D)

def setup_inputs(seed: int = 0) -> dict:
    key = jax.random.key(seed)
    ks = iter(jax.random.split(key, 32))

    def nrm(shape, scale):
        return scale * jax.random.normal(next(ks), shape, jnp.float32)

    x = nrm((BATCH, SEQ, D_MODEL), 1.0)
    ln_g = 1.0 + nrm((DEPTH, 2, D_MODEL), 0.02)
    ln_b = nrm((DEPTH, 2, D_MODEL), 0.02)
    mix_w_in = nrm((N_EVEN, D_MODEL, IN_WIDTH), D_MODEL ** -0.5)
    attn_sink = nrm((N_EVEN, A_Q_HEADS), 0.5)
    sgu_w = nrm((N_EVEN, B_GROUPS, CHUNK, CHUNK), 0.5 * CHUNK ** -0.5)
    sgu_b = 1.0 + nrm((N_EVEN, B_GROUPS, CHUNK), 0.02)
    sgu_ln_g = 1.0 + nrm((N_EVEN, B_GROUPS, B_GROUP_DIM), 0.02)
    sgu_ln_b = nrm((N_EVEN, B_GROUPS, B_GROUP_DIM), 0.02)
    mix_w_out = nrm((N_EVEN, MIX_WIDTH, D_MODEL), BETA * MIX_WIDTH ** -0.5)
    ffn_w_gate = nrm((N_EVEN, D_MODEL, D_FF), D_MODEL ** -0.5)
    ffn_w_up = nrm((N_EVEN, D_MODEL, D_FF), D_MODEL ** -0.5)
    ffn_w_down = nrm((N_EVEN, D_FF, D_MODEL), BETA * D_FF ** -0.5)
    n = jnp.arange(S5_STATE, dtype=jnp.float32)
    s5_lam_re = -0.5 + nrm((N_ODD, 2, S5_GROUPS, S5_STATE), 0.01)
    s5_lam_im = math.pi * n + nrm((N_ODD, 2, S5_GROUPS, S5_STATE), 0.01)
    s5_log_dt = jax.random.uniform(next(ks), (N_ODD, 2, S5_GROUPS), jnp.float32, math.log(1e-3), math.log(1e-1))
    s5_b_re = nrm((N_ODD, 2, S5_GROUPS, S5_STATE, S5_GROUP), (2 * S5_GROUP) ** -0.5)
    s5_b_im = nrm((N_ODD, 2, S5_GROUPS, S5_STATE, S5_GROUP), (2 * S5_GROUP) ** -0.5)
    s5_c_re = nrm((N_ODD, 2, S5_GROUPS, S5_GROUP, S5_STATE), S5_STATE ** -0.5)
    s5_c_im = nrm((N_ODD, 2, S5_GROUPS, S5_GROUP, S5_STATE), S5_STATE ** -0.5)
    s5_d = nrm((N_ODD, S5_GROUPS, S5_GROUP), 1.0)
    glu_w_val = nrm((N_ODD, D_MODEL, D_MODEL), BETA * D_MODEL ** -0.5)
    glu_w_gate = nrm((N_ODD, D_MODEL, D_MODEL), D_MODEL ** -0.5)
    router_w = nrm((N_ODD, D_MODEL, N_EXPERTS), D_MODEL ** -0.5)
    moe_w_gate = nrm((N_ODD, N_EXPERTS, D_MODEL, D_FF), D_MODEL ** -0.5)
    moe_w_up = nrm((N_ODD, N_EXPERTS, D_MODEL, D_FF), D_MODEL ** -0.5)
    moe_w_down = nrm((N_ODD, N_EXPERTS, D_FF, D_MODEL), BETA * D_FF ** -0.5)
    return {'x': x, 'ln_g': ln_g, 'ln_b': ln_b, 'mix_w_in': mix_w_in, 'attn_sink': attn_sink,
            'sgu_w': sgu_w, 'sgu_b': sgu_b, 'sgu_ln_g': sgu_ln_g, 'sgu_ln_b': sgu_ln_b, 'mix_w_out': mix_w_out,
            'ffn_w_gate': ffn_w_gate, 'ffn_w_up': ffn_w_up, 'ffn_w_down': ffn_w_down,
            's5_lam_re': s5_lam_re, 's5_lam_im': s5_lam_im, 's5_log_dt': s5_log_dt,
            's5_b_re': s5_b_re, 's5_b_im': s5_b_im, 's5_c_re': s5_c_re, 's5_c_im': s5_c_im, 's5_d': s5_d,
            'glu_w_val': glu_w_val, 'glu_w_gate': glu_w_gate, 'router_w': router_w,
            'moe_w_gate': moe_w_gate, 'moe_w_up': moe_w_up, 'moe_w_down': moe_w_down}

def reference(x, ln_g, ln_b, mix_w_in, attn_sink, sgu_w, sgu_b, sgu_ln_g, sgu_ln_b, mix_w_out,
              ffn_w_gate, ffn_w_up, ffn_w_down, s5_lam_re, s5_lam_im, s5_log_dt,
              s5_b_re, s5_b_im, s5_c_re, s5_c_im, s5_d, glu_w_val, glu_w_gate, router_w,
              moe_w_gate, moe_w_up, moe_w_down):
    cos, sin = rope_tables(x.shape[1])
    for layer in range(DEPTH):
        i = layer // 2
        if layer % 2 == 0:
            mixed = mixer_ab(x, mix_w_in[i], attn_sink[i], sgu_w[i], sgu_b[i], sgu_ln_g[i], sgu_ln_b[i],
                             mix_w_out[i], cos, sin)
            x = layer_norm(ALPHA * x + mixed, ln_g[layer, 0], ln_b[layer, 0])
            ffn = swiglu(x, ffn_w_gate[i], ffn_w_up[i], ffn_w_down[i])
            x = layer_norm(ALPHA * x + ffn, ln_g[layer, 1], ln_b[layer, 1])
        else:
            mixed = mixer_c(x, s5_lam_re[i], s5_lam_im[i], s5_log_dt[i], s5_b_re[i], s5_b_im[i],
                            s5_c_re[i], s5_c_im[i], s5_d[i], glu_w_val[i], glu_w_gate[i])
            x = layer_norm(ALPHA * x + mixed, ln_g[layer, 0], ln_b[layer, 0])
            ffn = moe_swiglu(x, router_w[i], moe_w_gate[i], moe_w_up[i], moe_w_down[i])
            x = layer_norm(ALPHA * x + ffn, ln_g[layer, 1], ln_b[layer, 1])
    return x


_drawn_inputs = setup_inputs


def setup_inputs(seed=0):
    import zlib

    import numpy as np

    out = dict(_drawn_inputs(seed))
    spreads = {}
    factors = {'attn_sink': 64.0,
     'sgu_b': 21.37,
     'sgu_ln_g': 34.209,
     'sgu_ln_b': 53.728,
     's5_lam_re': 64.0,
     's5_lam_im': 25.312,
     's5_log_dt': 25.209,
     's5_b_re': 25.367,
     's5_b_im': 29.817,
     's5_c_re': 34.976,
     's5_c_im': 33.169}
    for name, (base, spread) in spreads.items():
        noise = np.random.default_rng([zlib.crc32(name.encode()), seed]).standard_normal(out[name].shape)
        drawn = base * np.exp(spread * noise) if base else spread * noise
        out[name] = __import__('jax').numpy.asarray(drawn.astype(out[name].dtype))
    for name, factor in factors.items():
        out[name] = (out[name] * factor).astype(out[name].dtype)
    return out
```

```python
import math
from contextlib import ExitStack

import numpy as np

import concourse.bass as bass
from concourse import mybir

P = 128
D = 1024
KT = D // P
SEQ = 256
MT = SEQ // P
HQ, HKV, HD = 8, 2, 64
QK = (HQ + HKV) * HD
V0 = QK
U0 = V0 + HKV * HD
Z0 = U0 + 512
IN_W = Z0 + 512
PROJ_N = IN_W // 4
G = 8
FF = 2816
FC = 256
SUB = FC // P
NCH = FF // FC
NE = 8
MOE_CH = NCH * NE
GLU_CH = D // FC
R = 3
SLOT = KT * 2 * FC + SUB * D
GLU_BASE = NCH
MOE_BASE = NCH + GLU_CH
MOE_TURNS = (MOE_CH - (R + 1)) // R - 1
assert MOE_CH == (R + 1) + R * (MOE_TURNS + 1)
ALPHA = (2.0 * 2) ** 0.25
EPS = 1e-5
NEG = -1e30
L, NC, CG, PS = 8, 32, 16, 64
PR = 4
NT = KT * PR * 2
MAGIC = 1.5 * 2.0**23

F32 = mybir.dt.float32
I32 = mybir.dt.int32
U32 = mybir.dt.uint32
ALU = mybir.AluOpType
ACT = mybir.ActivationFunctionType
AX = mybir.AxisListType
DEBUG = ()


class Steps:

    def __init__(self, eng, sem):
        self.eng, self.sem, self.n, self.offset = eng, sem, 0, 0

    def __call__(self, ins):
        self.n += 1
        ins.then_inc(self.sem, 1)
        self.eng.wait_ge(self.sem, self.offset + self.n)

    def loop(self, i, per_turn):
        self.start, self.per_turn = self.n, per_turn
        self.offset = i * per_turn

    def end_loop(self, turns):
        assert self.n - self.start == self.per_turn, (self.n - self.start, self.per_turn)
        self.n = self.start + self.per_turn * turns
        self.offset = 0


def build(nc, a, out):
    with ExitStack() as ctx:

        def sem(name):
            return ctx.enter_context(nc.semaphore(name))

        def sbuf(name, shape, dt=F32):
            return ctx.enter_context(nc.sbuf_tensor(name, [P] + list(shape), dt))

        ring = sbuf("ring", [R * SLOT])
        x_tok = sbuf("x_tok", [MT, D])
        xT = sbuf("xT", [KT, SEQ])
        res = sbuf("res", [MT, D])
        lnp = sbuf("lnp", [2, D])
        ident = sbuf("ident", [P])
        sg = sbuf("sg", [MT, FC])
        h = sbuf("h", [MT, FC])
        hT = sbuf("hT", [MT, SUB, P])
        stats = sbuf("stats", [MT, 2, 6])
        mv = sbuf("mv", [MT, 2])
        ln_s = sbuf("ln_s", [MT, 4])
        a8 = sbuf("a8", [2, 2, 2, KT * PR])
        wr_sb = sbuf("wr_sb", [KT, NE])
        comb = sbuf("comb", [MT, NE])
        combx = sbuf("combx", [MT, NE, NCH])
        rt = sbuf("rt", [MT, 64])
        top_i = sbuf("top_i", [MT, 8], U32)
        iota8 = sbuf("iota8", [NE])
        pw_i = sbuf("pw_i", [NT], I32)
        ARENA = 23200
        arena = sbuf("arena", [ARENA])
        ps = ctx.enter_context(nc.psum_tensor("ps", [P, 8, 512], F32))

        class Region:
            def __init__(self):
                self.at = 0

            def __call__(self, *shape):
                n = int(np.prod(shape))
                v = arena[:, self.at:self.at + n]
                self.at += n
                assert self.at <= ARENA, self.at
                names = "abcdef"[:len(shape)]
                if len(shape) > 1:
                    v = v.rearrange(f"z ({' '.join(names)}) -> z {' '.join(names)}",
                                    **{n_: s for n_, s in zip(names[1:], shape[1:])})
                return v

        r = Region()
        Bp, Cp, Cq = r(2, KT, 2, PR, CG), r(2, KT, 2, PR, CG), r(2, KT, 2, PR, CG)
        lamdt = r(3, NT)
        pa = r(2, NT, L + 1)
        p2, p1 = r(2, KT, 2, PR, L + 1), r(2, KT, 2, PR, L)
        ta, tb = r(2 * PR, L + 1, CG), r(2 * PR, L + 1, CG)
        w2 = r(2, 2 * PR, L + 1, CG)
        w1t = r(2, 2 * PR, L, CG)
        w1 = r(16, P)
        Bz = r(2, 2 * PR, 2, CG)
        kext = r(2 * L - 1, CG)
        Dd, Dp, eye16 = r(KT, CG), r(KT), r(CG)
        sm = r(24, NT)

        r = Region()
        hsb = r(MT, IN_W)
        qkr = r(MT, HQ + HKV, 2, HD // 2)
        kd = r(MT, HKV, 2, HD)
        qT, kT = r(4, SEQ), r(HKV, SEQ)
        pr_ = r(HQ, MT, SEQ)
        pT = r(HQ, 2, SEQ)
        mixT = r(KT, SEQ)
        sguT, sgub = r(G, P), r(G)
        sgln = r(2, 512)
        bout = r(MT, 512)
        mask = r(MT, SEQ)
        cs = r(MT, 2, HD // 2)
        sink = r(HQ)
        mxs, den = r(HQ, MT), r(4, HQ * MT)
        rtmp = r(2, HQ + HKV, HD // 2)
        gst = r(4, MT * G)
        gsq = pr_[:, 0:4, :, :].rearrange("z a b c -> z (a b c)")[:, 0:1024]

        r = Region()
        xg = r(2, 8, L, CG)
        yk = xg.rearrange("z a b c d -> z a (b c d)").rearrange("z a (i f) -> z a i f", i=L)
        xl = res[:].rearrange("z a (j f) -> z a j f", j=L)
        U = r(64, NC)
        wb = r(2, 2 * 2 * PR * (L + 1) * CG)
        Tb = r(2, 8, P)
        S = r(2, NC + 1, 2, KT * PR)
        Sz = r(2, 2, KT * PR, 2, NC)
        prod = sg[:].rearrange("z a b -> z (a b)")

        def dram(name, shape):
            return nc.dram_tensor(name, shape, F32, kind="Internal").ap()

        w1_d = dram("w1_d", (KT, P, 16 * P))
        w2_d = dram("w2_d", (KT, P, 2 * 2 * PR * (L + 1) * CG))
        kext_d = dram("kext_d", (KT, P, (2 * L - 1) * CG))
        x2_d = dram("x2_d", (SEQ, D))

        names = """const_in x_in win_in wout_in lamdt_in s5_in eye_in
            act_step dve_step pool_step
            s5_ready s5_free bz_ready w1t_ps w1_sb kgen_ps kext_sb s5_bz s5_w1t s5_w2 s5_kx w1_out kx_out
            a_done x0T_ps x0T_sb proj_ps proj_sb rope_ok qkT_ps qkT_sb sc_ps sc_sb mx_ok exp_ok p_ok
            pT_ps pT_sb pv_ps pv_sb gelu_ok vn_ok sv_ps bo_ok bT_ps bT_sb op_ps attn_ok
            ln_in ln_var ln_std ln_out xT_ps xT_sb ln_p
            ffn_gu ffn_silu ffn_h ffn_tr ffn_hT ffn_down
            glu_ps glu_sig glu_z
            moe_gu moe_silu moe_h moe_tr moe_hT moe_down
            x2_out xg_ok xk_in0 xk_in1 uT_ps u_sb wk_in0 wk_in1 tk_in0 tk_in1 s_ps s_sb scan_ok scan_p sz_ok y_ps y_g yt_ps yt_sb
            rt_ps comb_ok fin out_sent dbg wk_used""".split()
        s = {n: sem(n) for n in names}
        slot_full = [sem(f"slot_full{i}") for i in range(R)]
        W_used = {"ffn": s["ffn_down"], "glu": s["glu_ps"], "moe": s["moe_down"]}

        def bank(i, n=512):
            return ps[:, i, 0:n]

        def slot_views(k):
            base = k * SLOT
            gu = ring[:, base:base + KT * 2 * FC].rearrange("z (k n) -> z k n", k=KT)
            dn = ring[:, base + KT * 2 * FC:base + SLOT].rearrange("z (s n) -> z s n", s=SUB)
            return gu, dn

        w_in_v = ring[:, 0:KT * IN_W].rearrange("z (k n) -> z k n", k=KT)
        w_out_v = ring[:, 0:KT * D].rearrange("z (k n) -> z k n", k=KT)

        dbg_list = [d for d in DEBUG if d in a.get("_dbg", {})]

        block = ctx.enter_context(nc.Block())

        @block.sync
        def _(sp):
            sp.dma_start(lamdt, a["s5_lamdt"]).then_inc(s["lamdt_in"], 16)
            sp.dma_start(ident[:], a["ident"]).then_inc(s["eye_in"], 16)
            for dst, n in ((Bp, "s5_b"), (Cp, "s5_c")):
                sp.dma_start(dst.rearrange("z a b c d e -> z (a b c d e)"), a[n]).then_inc(s["s5_in"], 16)
            sp.dma_start(Dp, a["s5_d"]).then_inc(s["s5_in"], 16)
            sp.dma_start(eye16, a["eye16"]).then_inc(s["s5_in"], 16)
            sp.dma_start(x_tok[:], a["x"].rearrange("(m p) d -> p m d", p=P)).then_inc(s["x_in"], 16)
            sp.dma_start(ring[:, 0:KT * IN_W], a["w_in"]).then_inc(s["win_in"], 16)
            sp.dma_start(wr_sb[:].rearrange("z k e -> z (k e)"), a["w_router"]).then_inc(s["eye_in"], 16)
            sp.dma_start(iota8[:], a["iota8"]).then_inc(s["eye_in"], 16)
            sp.wait_ge(s["a_done"], 1)
            for dst, n in ((sguT.rearrange("z a b -> z (a b)"), "sguT"), (sgub, "sgub"),
                           (mask.rearrange("z a b -> z (a b)"), "mask"),
                           (cs.rearrange("z a b c -> z (a b c)"), "cossin"),
                           (sink, "sink"), (sgln.rearrange("z a b -> z (a b)"), "sgln")):
                src = a[n] if a[n].shape[0] == P else a[n].to_broadcast([P, a[n].shape[1]])
                sp.dma_start(dst, src).then_inc(s["const_in"], 16)
            sp.wait_ge(s["proj_ps"], 8)
            sp.dma_start(ring[:, 0:KT * D], a["w_out"]).then_inc(s["wout_in"], 16)

            def load_chunk(slot, src, size=SLOT):
                sp.dma_start(ring[:, slot * SLOT:slot * SLOT + size], src).then_inc(slot_full[slot], 16)

            for c in [2] + [c for c in range(NCH) if c != 2]:
                if c in (0, 1):
                    sp.wait_ge(s["op_ps"], 2)
                if c >= R:
                    sp.wait_ge(s["ffn_down"], c - R + 1)
                load_chunk(c % R, a["ffn_w"][c])
            for c in range(GLU_CH):
                item = GLU_BASE + c
                if c < R:
                    sp.wait_ge(s["ffn_down"], item - R + 1)
                else:
                    sp.wait_ge(s["glu_ps"], 2 * (c - R + 1))
                load_chunk(item % R, a["glu_w"][c], KT * 2 * FC)
            for c in range(R + 1):
                if c < R:
                    sp.wait_ge(s["glu_ps"], 2 * (GLU_CH - R + c + 1))
                else:
                    sp.wait_ge(s["moe_down"], c - R + 1)
                load_chunk((MOE_BASE + c) % R, a["moe_w"][c])
            with sp.Fori(0, MOE_TURNS + 1) as turn:
                c = turn * R + (R + 1)
                for j in range(R):
                    sp.wait_ge(s["moe_down"], c + (j - R + 1))
                    load_chunk((MOE_BASE + R + 1 + j) % R,
                               a["moe_w"][bass.ds(c + j, 1)].rearrange("o p n -> (o p) n"))
            sp.wait_ge(s["fin"], 2)
            sp.dma_start(out.rearrange("(m p) d -> p m d", p=P), x_tok[:]).then_inc(s["out_sent"], 16)
            sp.wait_ge(s["out_sent"], 16)

        def s5_loads(pool):
            pool.wait_ge(s["x2_out"], 16)
            xk = x2_d.rearrange("(n j) (k f) -> k n j f", j=L, f=P)
            for k in range(KT):
                pool.dma_start(xl[NC * (k % 4):NC * (k % 4 + 1), k // 4], xk[k]).then_inc(s[f"xk_in{k // 4}"], 16)
            for k in range(2 * KT):
                if 2 <= k < KT + 2:
                    pool.wait_ge(s["wk_used"], k - 1)
                elif k >= KT + 2:
                    pool.wait_ge(s["y_ps"], k - KT - 1)
                src = w1_d[k] if k < KT else w2_d[k - KT]
                pool.dma_start(wb[:, k % 2, 0:src.shape[1]], src).then_inc(s[f"wk_in{k % 2}"], 16)
                if k >= KT:
                    kk = k - KT
                    for j in range(L):
                        src = kext_d[kk][:, (L - 1 - j) * CG:(2 * L - 1 - j) * CG].rearrange("(g c) n -> c g n", c=CG)
                        pool.dma_start(Tb[j * CG:(j + 1) * CG, kk % 2], src).then_inc(s[f"tk_in{kk % 2}"], 16)

        @block.gpsimd
        def _(pool):
            with pool.Fori(0, KT) as k:
                pool.wait_ge(s["s5_w2"], k + 1)
                pool.dma_start(w2_d[bass.ds(k, 1)].rearrange("o p n -> (o p) n"),
                               w2.rearrange("z a b c d -> z (a b c d)")).then_inc(s["s5_free"], 16)
                pool.wait_ge(s["w1_sb"], 4 * k + 4)
                pool.dma_start(w1_d[bass.ds(k, 1)].rearrange("o p n -> (o p) n"),
                               w1.rearrange("z a b -> z (a b)")).then_inc(s["w1_out"], 16)
                pool.wait_ge(s["kext_sb"], k + 1)
                pool.dma_start(kext_d[bass.ds(k, 1)].rearrange("o p n -> (o p) n"),
                               kext.rearrange("z a b -> z (a b)")).then_inc(s["kx_out"], 16)
            pool.wait_ge(s["s5_free"], 16 * KT)
            pool.wait_ge(s["w1_out"], 16 * KT)
            pool.wait_ge(s["kx_out"], 16 * KT)
            for n in range(4):
                if n:
                    pool.wait_ge(s["ln_out"], 2 * n)
                if n == 2:
                    pool.dma_start(x2_d.rearrange("(m p) d -> p m d", p=P), x_tok[:]).then_inc(s["x2_out"], 16)
                for j, what in enumerate(("ln_g", "ln_b")):
                    pool.dma_start(lnp[:, j, :], a[what][n:n + 1, :].to_broadcast([P, D])).then_inc(s["ln_p"], 16)
                if n == 2:
                    s5_loads(pool)

        def swiglu_pe(pe, key, slot, use, q, first, second, last):
            gu, dn = slot_views(slot)
            prev = slot_views((slot - 1) % R)[1]
            for m in range(MT):
                if m == 0:
                    pe.wait_ge(slot_full[slot], use)
                if not first:
                    pe.wait_ge(s[key + "_h"], 2 * q - 1 + m)
                for k in range(KT):
                    mm = pe.matmul(bank(4 + m), xT[:, k, m * P:(m + 1) * P], gu[:, k, :],
                                   start=k == 0, stop=k == KT - 1)
                mm.then_inc(s[key + "_gu"], 1)
                if not first:
                    if m == 0:
                        swiglu_turn(pe, key, q - 1, 1, False)
                    else:
                        swiglu_down(pe, key, q - 1, prev, second, False)
            swiglu_turn(pe, key, q, 0, first)
            if last:
                swiglu_turn(pe, key, q, 1, first)
                swiglu_down(pe, key, q, dn, False, True)

        def swiglu_turn(pe, key, q, m, first):
            pe.wait_ge(s[key + "_h"], 2 * q + m + 1)
            if not first:
                pe.wait_ge(s[key + "_hT"], 2 * q - 1 + m)
            for t in range(SUB):
                mm = pe.transpose(ps[:, 6 + m, t * P:(t + 1) * P], h[:, m, t * P:(t + 1) * P], ident[:])
            mm.then_inc(s[key + "_tr"], 1)

        def swiglu_down(pe, key, q, dn, start, stop):
            pe.wait_ge(s[key + "_hT"], 2 * q + 2)
            for m in range(MT):
                for n in range(2):
                    for t in range(SUB):
                        mm = pe.matmul(bank(2 * m + n), hT[:, m, t, :], dn[:, t, n * 512:(n + 1) * 512],
                                       start=start and t == 0, stop=stop and t == SUB - 1)
            mm.then_inc(s[key + "_down"], 1)

        def swiglu_act(act, key, q, first, last):
            for m in range(MT):
                act.wait_ge(s[key + "_gu"], 2 * q + m + 1)
                if not first:
                    act.wait_ge(s[key + "_h"], 2 * q - 1 + m)
                act.activation(sg[:, m, :], ps[:, 4 + m, 0:FC], ACT.Silu).then_inc(s[key + "_silu"], 1)
                if m == 0 and not first:
                    swiglu_copy(act, key, q - 1, 1, False)
            swiglu_copy(act, key, q, 0, first)
            if last:
                swiglu_copy(act, key, q, 1, False)

        def swiglu_copy(act, key, q, m, first):
            act.wait_ge(s[key + "_tr"], 2 * q + m + 1)
            if not first:
                act.wait_ge(s[key + "_down"], q)
            act.copy(hT[:, m].rearrange("z a b -> z (a b)"), ps[:, 6 + m, 0:FC]).then_inc(s[key + "_hT"], 1)

        def swiglu_dve(dve, key, q, first, scale):
            for m in range(MT):
                dve.wait_ge(s[key + "_silu"], 2 * q + m + 1)
                if not first:
                    dve.wait_ge(s[key + "_tr"], 2 * q - 1 + m)
                dve.scalar_tensor_tensor(h[:, m, :], sg[:, m, :], scale(m), ps[:, 4 + m, FC:2 * FC],
                                         ALU.mult, ALU.mult).then_inc(s[key + "_h"], 1)

        def turn_y(pe, k):
            pe.wait_ge(s["y_g"], 4 * (k + 1))
            if k >= 2:
                pe.wait_ge(s["yt_sb"], k - 1)
            for i in range(L):
                mm = pe.transpose(ps[:, k % 2, i * NC:(i + 1) * NC], yk[0:NC, k % 2, i, :], ident[0:NC, 0:NC])
            mm.then_inc(s["yt_ps"], 1)

        @block.tensor
        def _(pe):
            pe.wait_ge(s["eye_in"], 48)
            def s5_tables_pe(k, first):
                pe.wait_ge(s["s5_w2"], k + 1)
                pe.wait_ge(s["s5_bz"], k + 1)
                if not first:
                    pe.wait_ge(s["s5_kx"], k)
                for d in range(2):
                    for p in range(PR):
                        for ri in range(2):
                            mm = pe.matmul(ps[32 * p:32 * p + 32, 4 + d, 0:P],
                                           Bz[:, ri, d * PR + p].rearrange("z a b -> z (a b)"),
                                           w2[:, ri, d * PR + p, d:d + L, :].rearrange("z a b -> z (a b)"),
                                           start=ri == 0, stop=ri == 1)
                mm.then_inc(s["kgen_ps"], 1)
                pe.wait_ge(s["s5_w1t"], k + 1)
                if not first:
                    pe.wait_ge(s["w1_sb"], 4 * k)
                for t in range(16):
                    mm = pe.transpose(ps[:, t // 4, (t % 4) * P:(t % 4 + 1) * P],
                                      w1t[:, t // 8, t % 8].rearrange("z a b -> z (a b)"), ident[:])
                    if t % 4 == 3:
                        mm.then_inc(s["w1t_ps"], 1)

            s5_tables_pe(0, True)
            with pe.Fori(1, KT) as k:
                s5_tables_pe(k, False)

            def turn_x(ready, count):
                for t in range(4):
                    m, half = t // 2, t % 2
                    pe.wait_ge(s["ln_out" if ready is None else ready], (count + m + 1) if ready is None else 16)
                    if t >= 2:
                        pe.wait_ge(s["xT_sb"], pe_turns[0] * 4 + t - 1)
                    for j in range(4):
                        mm = pe.transpose(ps[:, 6 + t % 2, j * P:(j + 1) * P],
                                          x_tok[:, m, (4 * half + j) * P:(4 * half + j + 1) * P], ident[:])
                    mm.then_inc(s["xT_ps"], 1)
                pe_turns[0] += 1

            pe_turns = [0]
            turn_x("x_in", 0)
            pe.wait_ge(s["xT_sb"], 4)
            pe.wait_ge(s["win_in"], 16)
            pe.wait_ge(s["w1_sb"], 4 * KT)
            pe.wait_ge(s["s5_kx"], KT)
            for m in range(MT):
                for n in range(4):
                    for k in range(KT):
                        mm = pe.matmul(bank(4 * m + n, PROJ_N), xT[:, k, m * P:(m + 1) * P],
                                       w_in_v[:, k, n * PROJ_N:(n + 1) * PROJ_N], start=k == 0, stop=k == KT - 1)
                    mm.then_inc(s["proj_ps"], 1)
            pe.wait_ge(s["proj_sb"], 8)
            pe.wait_ge(s["rope_ok"], 2)
            for m in range(MT):
                for j in range(4):
                    pe.transpose(ps[:, j // 2, (j % 2) * SEQ + m * P:(j % 2) * SEQ + (m + 1) * P],
                                 qkr[:, m, 2 * j:2 * j + 2].rearrange("z a b c -> z (a b c)"), ident[:])
                for j in range(HKV):
                    mm = pe.transpose(ps[:, 2, j * SEQ + m * P:j * SEQ + (m + 1) * P],
                                      kd[:, m, j].rearrange("z a b -> z (a b)"), ident[:])
            mm.then_inc(s["qkT_ps"], 1)
            pe.wait_ge(s["qkT_sb"], 3)
            for hd in range(HQ):
                o = HD * (hd % 2)
                for m in range(MT):
                    mm = pe.matmul(ps[:, hd, m * SEQ:(m + 1) * SEQ], qT[o:o + HD, hd // 2, m * P:(m + 1) * P],
                                   kT[o:o + HD, hd // 4, :], start=True, stop=True)
                mm.then_inc(s["sc_ps"], 1)
            pe.wait_ge(s["vn_ok"], 1)
            pe.wait_ge(s["sc_sb"], 8)
            pe.wait_ge(s["const_in"], 96)
            for g in range(G):
                mm = pe.matmul(ps[:, g // 4, (g % 4) * P:(g % 4 + 1) * P], sguT[:, g, :],
                               hsb[:, :, Z0 + g * HD:Z0 + (g + 1) * HD], start=True, stop=True)
            mm.then_inc(s["sv_ps"], 1)
            for hd in range(HQ):
                pe.wait_ge(s["p_ok"], 1)
                if hd >= 4:
                    pe.wait_ge(s["pT_sb"], hd - 3)
                for m in range(MT):
                    for kt in range(2):
                        mm = pe.transpose(ps[:, 2 + hd % 4, kt * SEQ + m * P:kt * SEQ + (m + 1) * P],
                                          pr_[:, hd, m, kt * P:(kt + 1) * P], ident[:])
                mm.then_inc(s["pT_ps"], 1)
            pe.wait_ge(s["bo_ok"], 1)
            for m in range(MT):
                for j in range(4):
                    mm = pe.transpose(ps[:, j // 2, (j % 2) * SEQ + m * P:(j % 2) * SEQ + (m + 1) * P],
                                      bout[:, m, j * P:(j + 1) * P], ident[:])
            mm.then_inc(s["bT_ps"], 1)
            for hd in range(HQ):
                pe.wait_ge(s["pT_sb"], hd + 1)
                o = HD * (hd % 2)
                for kt in range(2):
                    v = hsb[:, kt, V0 + (hd // 4) * HD:V0 + (hd // 4 + 1) * HD]
                    mm = pe.matmul(ps[o:o + HD, 6 + hd // 4, (hd // 2 % 2) * SEQ:(hd // 2 % 2 + 1) * SEQ],
                                   v, pT[:, hd, kt, :], start=kt == 0, stop=kt == 1)
            mm.then_inc(s["pv_ps"], 1)
            pe.wait_ge(s["wout_in"], 16)
            pe.wait_ge(s["attn_ok"], 4)
            for m in range(MT):
                for n in range(2):
                    for k in range(KT):
                        mm = pe.matmul(bank(2 * m + n), mixT[:, k, m * P:(m + 1) * P],
                                       w_out_v[:, k, n * 512:(n + 1) * 512], start=k == 0, stop=k == KT - 1)
                mm.then_inc(s["op_ps"], 1)
            turn_x(None, 0)
            pe.wait_ge(s["xT_sb"], 8)
            for c in range(NCH):
                swiglu_pe(pe, "ffn", c % R, 16 * (c // R + 1), c,
                          c == 0, c == 1, c == NCH - 1)
            for k in range(KT):
                pe.wait_ge(s["xg_ok"], k // 4 + 1)
                if k == 0:
                    pe.wait_ge(s["ln_out"], 4)
                if k >= 2:
                    pe.wait_ge(s["u_sb"], k - 1)
                o = NC * (k % 4)
                for g in range(8):
                    mm = pe.transpose(ps[:, 4 + k % 2, g * NC:(g + 1) * NC],
                                      xg[o:o + NC, k // 4, g].rearrange("z a b -> z (a b)"),
                                      ident[o:o + NC, o:o + NC])
                mm.then_inc(s["uT_ps"], 1)
            for k in range(KT):
                pe.wait_ge(s["u_sb"], k + 1)
                pe.wait_ge(s[f"wk_in{k % 2}"], 16 * (k // 2 + 1))
                if k >= 2:
                    pe.wait_ge(s["s_sb"], 2 * k - 2)
                for ri in range(2):
                    for d in range(2):
                        for p in range(PR):
                            t = (ri * 2 + d) * PR + p
                            for g2 in range(2):
                                mm = pe.matmul(ps[64 * g2:64 * g2 + 64, 6 + k % 2, ((d * 2 + ri) * PR + p) * NC:((d * 2 + ri) * PR + p + 1) * NC],
                                               wb[:, k % 2, t * P + 64 * g2:t * P + 64 * g2 + 64],
                                               U[:, 8 * k + 2 * p + g2, :], start=True, stop=True)
                mm.then_inc(s["wk_used"], 1)
            for k in range(KT):
                if k >= 2:
                    pe.wait_ge(s["y_g"], 4 * (k - 1))
                elif k == 0:
                    pe.wait_ge(s["sz_ok"], 8)
                pe.wait_ge(s[f"tk_in{k % 2}"], 16 * L * (k // 2 + 1))
                pe.wait_ge(s[f"wk_in{k % 2}"], 16 * ((k + KT) // 2 + 1))
                w2v = wb[:, k % 2].rearrange("z (r d p l) -> z r d p l", r=2, d=2, p=PR)
                for p in range(PR):
                    o = 64 * (p % 2)
                    col = slice((p // 2) * P, (p // 2 + 1) * P)
                    for d in range(2):
                        for ri in range(2):
                            lo = CG if d == 0 else 0
                            pe.matmul(ps[o:o + 64, 4 + k % 2, col],
                                      Sz[:, d, ri, k * PR + p].rearrange("z a b -> z (a b)"),
                                      w2v[:, ri, d, p, lo:lo + P], start=d + ri == 0, stop=False,
                                      skip_group_check=True)
                    for g2 in range(2):
                        mm = pe.matmul(ps[o + 32 * g2:o + 32 * g2 + 32, 4 + k % 2, col],
                                       U[:, 8 * k + 2 * p + g2, :], Tb[:, k % 2, 2 * p + g2, :],
                                       start=False, stop=True, skip_group_check=True)
                mm.then_inc(s["y_ps"], 1)
                if k >= 1:
                    turn_y(pe, k - 1)
            turn_y(pe, KT - 1)
            pe.wait_ge(s["yt_sb"], KT)
            for c in range(GLU_CH):
                item = GLU_BASE + c
                pe.wait_ge(slot_full[item % R], 16 * (item // R + 1))
                gu, _ = slot_views(item % R)
                for m in range(MT):
                    if c:
                        pe.wait_ge(s["glu_z"], 2 * c - 1 + m)
                    for k in range(KT):
                        mm = pe.matmul(bank(m), xT[:, k, m * P:(m + 1) * P], gu[:, k, :],
                                       start=k == 0, stop=k == KT - 1)
                    mm.then_inc(s["glu_ps"], 1)
            turn_x(None, 4)
            pe.wait_ge(s["xT_sb"], 12)
            for m in range(MT):
                for k in range(KT):
                    mm = pe.matmul(ps[:, 5, m * 8:m * 8 + 8], xT[:, k, m * P:(m + 1) * P], wr_sb[:, k, :],
                                   start=k == 0, stop=k == KT - 1)
            mm.then_inc(s["rt_ps"], 1)
            pe.wait_ge(s["comb_ok"], 1)
            for c in range(R + 1):
                item = MOE_BASE + c
                swiglu_pe(pe, "moe", item % R, 16 * (item // R + 1), c,
                          c == 0, c == 1, False)
            with pe.Fori(0, MOE_TURNS) as turn:
                for j in range(R):
                    item = MOE_BASE + R + 1 + j
                    swiglu_pe(pe, "moe", item % R, turn * 16 + 16 * (item // R + 1), turn * R + (R + 1 + j),
                              False, False, False)
            for c in range(MOE_CH - R, MOE_CH):
                item = MOE_BASE + c
                swiglu_pe(pe, "moe", item % R, 16 * (item // R + 1), c, False, False, c == MOE_CH - 1)

        def copy_y(act, k):
            act.wait_ge(s["yt_ps"], k + 1)
            act.copy(xT[:, k, :].rearrange("z (n i) -> z i n", i=L),
                     ps[:, k % 2, 0:SEQ].rearrange("z (i n) -> z i n", i=L)).then_inc(s["yt_sb"], 1)

        @block.scalar
        def _(act):
            def s5_tables_act(k, first):
                if not first:
                    act.wait_ge(s["w1_out"], 16 * k)
                for t in range(4):
                    act.wait_ge(s["w1t_ps"], 4 * k + t + 1)
                    act.copy(w1[:, 4 * t:4 * t + 4].rearrange("z a b -> z (a b)"), bank(t)).then_inc(s["w1_sb"], 1)

            s5_tables_act(0, True)
            with act.Fori(1, KT) as k:
                s5_tables_act(k, False)

            def copy_xT(turn):
                for t in range(4):
                    m, half = t // 2, t % 2
                    act.wait_ge(s["xT_ps"], 4 * turn + t + 1)
                    act.copy(xT[:, 4 * half:4 * half + 4, m * P:(m + 1) * P],
                             ps[:, 6 + t % 2, :].rearrange("z (a b) -> z a b", a=4)).then_inc(s["xT_sb"], 1)

            copy_xT(0)
            act.wait_ge(s["a_done"], 1)
            for m in range(MT):
                for n in range(4):
                    act.wait_ge(s["proj_ps"], 4 * m + n + 1)
                    act.copy(hsb[:, m, n * PROJ_N:(n + 1) * PROJ_N], bank(4 * m + n, PROJ_N)).then_inc(s["proj_sb"], 1)
            act.wait_ge(s["proj_sb"], 8)
            for m in range(MT):
                act.activation(hsb[:, m, U0:IN_W], hsb[:, m, U0:IN_W], ACT.Gelu_apprx_tanh).then_inc(s["gelu_ok"], 1)
            act.wait_ge(s["qkT_ps"], 1)
            for j in range(2):
                act.copy(qT[:, 2 * j:2 * j + 2].rearrange("z a b -> z (a b)"), bank(j)).then_inc(s["qkT_sb"], 1)
            act.copy(kT.rearrange("z a b -> z (a b)"), bank(2)).then_inc(s["qkT_sb"], 1)
            act.wait_ge(s["mx_ok"], 1)
            for hd in range(HQ):
                for m in range(MT):
                    act.activation(pr_[:, hd, m, :], pr_[:, hd, m, :], ACT.Exp, bias=den[:, 0, 2 * hd + m:2 * hd + m + 1],
                                   accum_out=den[:, 1, 2 * hd + m:2 * hd + m + 1]).then_inc(s["exp_ok"], 1)
            act.activation(den[:, 2, :], den[:, 2, :], ACT.Exp).then_inc(s["exp_ok"], 1)
            act.wait_ge(s["ln_var"], 1)
            act.activation(gst[:, 2, :], gst[:, 2, :], ACT.Sqrt).then_inc(s["ln_std"], 1)
            for hd in range(HQ):
                act.wait_ge(s["pT_ps"], hd + 1)
                act.copy(pT[:, hd].rearrange("z a b -> z (a b)"), bank(2 + hd % 4)).then_inc(s["pT_sb"], 1)
            act.wait_ge(s["bT_ps"], 1)
            for j in range(2):
                act.copy(mixT[:, 4 + 2 * j:6 + 2 * j].rearrange("z a b -> z (a b)"), bank(j)).then_inc(s["attn_ok"], 1)
            act.wait_ge(s["pv_ps"], 1)
            for j in range(2):
                act.copy(mixT[:, 2 * j:2 * j + 2].rearrange("z a b -> z (a b)"), bank(6 + j)).then_inc(s["attn_ok"], 1)

            def norm_sqrt(n):
                for m in range(MT):
                    act.wait_ge(s["ln_var"], 1 + 2 * n + m + 1)
                    act.activation(ln_s[:, m, 1:2], ln_s[:, m, 0:1], ACT.Sqrt).then_inc(s["ln_std"], 1)

            norm_sqrt(0)
            copy_xT(1)
            for c in range(NCH):
                swiglu_act(act, "ffn", c, c == 0, c == NCH - 1)
            norm_sqrt(1)
            for k in range(KT):
                act.wait_ge(s["uT_ps"], k + 1)
                act.copy(U[:, 8 * k:8 * k + 8].rearrange("z a b -> z (a b)"), ps[:, 4 + k % 2, 0:8 * NC]).then_inc(s["u_sb"], 1)
            for k in range(KT):
                act.wait_ge(s["wk_used"], k + 1)
                for d in range(2):
                    src = ps[:, 6 + k % 2, d * 256:(d + 1) * 256].rearrange("z (r p n) -> z n r p", r=2, p=PR)
                    act.copy(S[:, d, 1 - d:NC + 1 - d, :, k * PR:(k + 1) * PR], src).then_inc(s["s_sb"], 1)
            for k in range(KT):
                act.wait_ge(s["y_ps"], k + 1)
                if k >= 2:
                    act.wait_ge(s["yt_ps"], k - 1)
                elif k == 0:
                    act.wait_ge(s["uT_ps"], KT)
                for q in range(4):
                    src = ps[32 * q:32 * q + 32, 4 + k % 2, 0:2 * P].rearrange("z (h i c) -> z i h c", h=2, i=L)
                    dst = yk[0:NC, k % 2].rearrange("z i (h q c) -> z i h q c", h=2, q=4)[:, :, :, q, :]
                    act.activation(dst, src, ACT.Gelu_apprx_tanh).then_inc(s["y_g"], 1)
                if k >= 1:
                    copy_y(act, k - 1)
            copy_y(act, KT - 1)
            for c in range(GLU_CH):
                for m in range(MT):
                    act.wait_ge(s["glu_ps"], 2 * c + m + 1)
                    if c:
                        act.wait_ge(s["glu_z"], 2 * c - 1 + m)
                    act.activation(sg[:, m, :], ps[:, m, FC:2 * FC], ACT.Sigmoid).then_inc(s["glu_sig"], 1)
            norm_sqrt(2)
            copy_xT(2)
            act.wait_ge(s["rt_ps"], 2)
            act.activation(rt[:, :, 1:2], rt[:, :, 0:1], ACT.Exp).then_inc(s["rt_ps"], 1)
            for c in range(R + 1):
                swiglu_act(act, "moe", c, c == 0, False)
            with act.Fori(0, MOE_TURNS) as turn:
                for j in range(R):
                    swiglu_act(act, "moe", turn * R + (R + 1 + j), False, False)
            for c in range(MOE_CH - R, MOE_CH):
                swiglu_act(act, "moe", c, False, c == MOE_CH - 1)
            norm_sqrt(3)

        @block.vector
        def _(dve):
            step = Steps(dve, s["dve_step"])

            def tt(o, x, y, op):
                step(dve.tensor_tensor(o, x, y, op))

            def ts(o, x, s1, s2, op0, op1=None):
                step(dve.tensor_scalar(o, x, s1, s2, op0, op1) if op1 is not None
                     else dve.tensor_scalar(o, x, s1, None, op0))

            def stt(o, x, sc, y, op0, op1):
                step(dve.scalar_tensor_tensor(o, x, sc, y, op0, op1))

            MUL, ADD, SUB_ = ALU.mult, ALU.add, ALU.subtract

            free = iter(range(24))

            def small():
                return sm[:, next(free), :]

            q0, q1, q2, q3 = small(), small(), small(), small()

            def exp_parts(x, e, em1):
                ts(q0, x, -200.0, 200.0, ALU.max, ALU.min)
                ts(q1, q0, 1.0 / math.log(2.0), MAGIC, MUL, ADD)
                ts(q1, q1, MAGIC, None, SUB_)
                stt(q0, q1, -0.693359375, q0, MUL, ADD)
                stt(q0, q1, 2.12194440e-4, q0, MUL, ADD)
                ts(q2, q0, 1.0 / math.factorial(9), None, MUL)
                for n in range(8, 0, -1):
                    stt(q2, q2, 1.0 / math.factorial(n), q0, ADD, MUL)
                ts(q1, q1, 127.0, 0.0, ADD, ALU.max)
                step(dve.tensor_scalar(pw_i[:], q1, 255.0, None, ALU.min))
                step(dve.tensor_scalar(pw_i[:], pw_i[:], 23, None, ALU.logical_shift_left))
                pw = pw_i[:].bitcast(F32)
                stt(e, q2, 1.0, pw, ADD, MUL)
                if em1 is not None:
                    ts(q3, pw, -1.0, None, ADD)
                    tt(q0, q2, pw, MUL)
                    tt(em1, q0, q3, ADD)

            dve.wait_ge(s["lamdt_in"], 16)
            l_re, l_im, l_dt = lamdt[:, 0, :], lamdt[:, 1, :], lamdt[:, 2, :]
            dt_, la, lb, ea, em = small(), small(), small(), small(), small()
            exp_parts(l_dt, dt_, None)
            tt(la, l_re, dt_, MUL)
            tt(lb, l_im, dt_, MUL)
            exp_parts(la, ea, em)
            hh, h2, sh, ch, sb, oc = small(), small(), small(), small(), small(), small()
            ts(q0, lb, 1.0 / (2 * math.pi), MAGIC, MUL, ADD)
            ts(q0, q0, MAGIC, None, SUB_)
            stt(hh, q0, -6.28125, lb, MUL, ADD)
            stt(hh, q0, -1.93500518798828125e-3, hh, MUL, ADD)
            stt(hh, q0, -3.0199159819e-7, hh, MUL, ADD)
            ts(hh, hh, 0.5, None, MUL)
            tt(h2, hh, hh, MUL)
            f = math.factorial
            ts(sh, h2, 1.0 / f(13), None, MUL)
            for n, sign in ((11, -1), (9, 1), (7, -1), (5, 1), (3, -1)):
                stt(sh, sh, sign / f(n), h2, ADD, MUL)
            stt(sh, sh, 1.0, hh, ADD, MUL)
            ts(ch, h2, 1.0 / f(14) * -1, None, MUL)
            for n, sign in ((12, 1), (10, -1), (8, 1), (6, -1), (4, 1), (2, -1)):
                stt(ch, ch, sign / f(n), h2, ADD, MUL)
            ts(ch, ch, 1.0, None, ADD)
            stt(sb, sh, 2.0, ch, MUL, MUL)
            stt(oc, sh, 2.0, sh, MUL, MUL)
            br, bi, mr = small(), small(), small()
            tt(q0, ea, oc, MUL)
            tt(br, ea, q0, SUB_)
            tt(mr, em, q0, SUB_)
            tt(bi, ea, sb, MUL)
            cr, ci, nn = small(), small(), small()
            tt(q0, l_re, l_re, MUL)
            tt(q1, l_im, l_im, MUL)
            tt(q0, q0, q1, ADD)
            step(dve.reciprocal(nn, q0))
            tt(q0, mr, l_re, MUL)
            tt(q1, bi, l_im, MUL)
            tt(q0, q0, q1, ADD)
            tt(cr, q0, nn, MUL)
            tt(q0, bi, l_re, MUL)
            tt(q1, mr, l_im, MUL)
            tt(q0, q0, q1, SUB_)
            tt(ci, q0, nn, MUL)
            step(dve.memset(pa[:, 0, :, 0:1], 1.0))
            step(dve.memset(pa[:, 1, :, 0:1], 0.0))
            step(dve.tensor_copy(pa[:, 0, :, 1:2], br.unsqueeze(2)))
            step(dve.tensor_copy(pa[:, 1, :, 1:2], bi.unsqueeze(2)))
            for lo, n in ((1, 1), (2, 2), (4, 4)):
                sr, si = (pa[:, x, :, 1:1 + n] for x in (0, 1))
                mr_, mi_ = (pa[:, x, :, n:n + 1].to_broadcast([P, NT, n]) for x in (0, 1))
                dr, di = (pa[:, x, :, n + 1:2 * n + 1] for x in (0, 1))
                fa = ta.rearrange("z a b c -> z (a b c)")[:, 0:NT * n].rearrange("z (a b) -> z a b", b=n)
                fb = tb.rearrange("z a b c -> z (a b c)")[:, 0:NT * n].rearrange("z (a b) -> z a b", b=n)
                tt(fa, sr, mr_, MUL)
                tt(fb, si, mi_, MUL)
                tt(dr, fa, fb, SUB_)
                tt(fa, sr, mi_, MUL)
                tt(fb, si, mr_, MUL)
                tt(di, fa, fb, ADD)
            pav = pa.rearrange("z r (k d p) l -> z r k d p l", k=KT, d=2)
            for d in range(2):
                a8v = a8[:, d].rearrange("z a b (k p) -> z a b k p", k=KT)
                for o, i, x, sgn in ((0, 0, 0, 1.0), (0, 1, 1, -1.0), (1, 0, 1, 1.0), (1, 1, 0, 1.0)):
                    ts(a8v[:, o, i], pav[:, x, :, d, :, L], sgn, None, MUL)
            for x in range(2):
                for i in range(L + 1):
                    step(dve.tensor_copy(p2[:, x, :, 0, :, i], pav[:, x, :, 0, :, i]))
                    step(dve.tensor_copy(p2[:, x, :, 1, :, i], pav[:, x, :, 1, :, L - i]))
                for i in range(L):
                    step(dve.tensor_copy(p1[:, x, :, 0, :, i], pav[:, x, :, 0, :, L - 1 - i]))
                    step(dve.tensor_copy(p1[:, x, :, 1, :, i], pav[:, x, :, 1, :, i]))
            dve.wait_ge(s["s5_in"], 64)
            cflat = [c.rearrange("z x a b c d -> z x (a b c) d") for c in (Cp, Cq)]
            fa = ta.rearrange("z a b c -> z (a b c)")[:, 0:NT * CG].rearrange("z (a b) -> z a b", b=CG)
            fb = tb.rearrange("z a b c -> z (a b c)")[:, 0:NT * CG].rearrange("z (a b) -> z a b", b=CG)
            crb, cib = (v.unsqueeze(2).to_broadcast([P, NT, CG]) for v in (cr, ci))
            tt(fa, cflat[0][:, 0], crb, MUL)
            tt(fb, cflat[0][:, 1], cib, MUL)
            tt(cflat[1][:, 0], fa, fb, SUB_)
            tt(fa, cflat[0][:, 0], cib, MUL)
            tt(fb, cflat[0][:, 1], crb, MUL)
            tt(cflat[1][:, 1], fa, fb, ADD)
            step(dve.memset(Bz.rearrange("z a b c d -> z (a b c d)"), 0.0))
            for k in range(KT):
                ts(Dd[:, k, :], eye16, Dp[:, k:k + 1], None, MUL)

            def ksel(v, x, k, n):
                return v[:, x, bass.ds(k, 1)].rearrange("z o d p n -> z (o d p) n")

            def s5_tables_dve(k, first):
                C_, P_, B_, Q_ = ([ksel(v, x, k, 0) for x in (0, 1)] for v in (Cq, p2, Bp, p1))
                cb = [v.unsqueeze(2).to_broadcast([P, 2 * PR, L + 1, CG]) for v in C_]
                pb = [v.unsqueeze(3).to_broadcast([P, 2 * PR, L + 1, CG]) for v in P_]
                tt(ta, cb[0], pb[0], MUL)
                tt(tb, cb[1], pb[1], MUL)
                if not first:
                    dve.wait_ge(s["s5_free"], 16 * k)
                    dve.wait_ge(s["kgen_ps"], k)
                tt(w2[:, 0], ta, tb, SUB_)
                tt(ta, cb[0], pb[1], MUL)
                tt(tb, cb[1], pb[0], MUL)
                flat = lambda v: v.rearrange("z a b c -> z (a b c)")
                stt(flat(w2[:, 1]), flat(ta), -1.0, flat(tb), MUL, SUB_)
                dve.sem_inc(s["s5_w2"], 1)
                for x in range(2):
                    for g2 in range(2):
                        step(dve.tensor_copy(Bz[64 * g2:64 * g2 + 64, x, :, g2, :], B_[x][64 * g2:64 * g2 + 64]))
                dve.sem_inc(s["s5_bz"], 1)
                bb = [v.unsqueeze(2).to_broadcast([P, 2 * PR, L, CG]) for v in B_]
                qb = [v.unsqueeze(3).to_broadcast([P, 2 * PR, L, CG]) for v in Q_]
                va, vb = ta[:, :, 0:L, :], tb[:, :, 0:L, :]
                tt(va, bb[0], qb[0], MUL)
                tt(vb, bb[1], qb[1], MUL)
                if not first:
                    dve.wait_ge(s["w1t_ps"], 4 * k)
                tt(w1t[:, 0], va, vb, SUB_)
                tt(va, bb[0], qb[1], MUL)
                tt(vb, bb[1], qb[0], MUL)
                tt(w1t[:, 1], va, vb, ADD)
                dve.sem_inc(s["s5_w1t"], 1)
                dve.wait_ge(s["kgen_ps"], k + 1)
                if not first:
                    dve.wait_ge(s["kx_out"], 16 * k)
                kf = ps[:, 4, 0:P].rearrange("z (l c) -> z l c", c=CG)
                kb = ps[:, 5, 0:P].rearrange("z (l c) -> z l c", c=CG)
                step(dve.tensor_copy(kext[:, 0:L], kb))
                step(dve.tensor_copy(kext[:, L:2 * L - 1], kf[:, 1:L]))
                tt(kext[:, L - 1], kf[:, 0], kext[:, L - 1], ADD)
                step(dve.tensor_tensor(kext[:, L - 1], kext[:, L - 1],
                                       Dd[:, bass.ds(k, 1)].rearrange("z o c -> z (o c)"), ADD))
                dve.sem_inc(s["s5_kx"], 1)
                dve.sem_inc(s["kext_sb"], 1)

            before = step.n
            s5_tables_dve(0, True)
            per_turn = step.n - before
            with dve.Fori(1, KT) as k:
                step.loop(k - 1, per_turn)
                s5_tables_dve(k, False)
            step.end_loop(KT - 1)
            for n, v in (("s5_free", 16 * KT), ("w1_out", 16 * KT), ("kx_out", 16 * KT), ("w1t_ps", 4 * KT)):
                dve.wait_ge(s[n], v)
            dve.sem_inc(s["a_done"], 1)

            dve.wait_ge(s["const_in"], 96)
            dve.wait_ge(s["proj_sb"], 8)
            for m in range(MT):
                src = hsb[:, m, 0:QK].rearrange("z (h a b) -> z h a b", a=2, b=HD // 2)
                c_, s_ = (cs[:, m, x, :].unsqueeze(1).to_broadcast([P, HQ + HKV, HD // 2]) for x in (0, 1))
                x1, x2 = src[:, :, 0, :], src[:, :, 1, :]
                ra, rb = rtmp[:, 0], rtmp[:, 1]
                tt(ra, x1, c_, MUL)
                tt(rb, x2, s_, MUL)
                tt(qkr[:, m, :, 0, :], ra, rb, SUB_)
                tt(ra, x2, c_, MUL)
                tt(rb, x1, s_, MUL)
                tt(qkr[:, m, :, 1, :], ra, rb, ADD)
                kk = qkr[:, m, HQ:HQ + HKV].rearrange("z h a b -> z h (a b)")
                for x in range(2):
                    step(dve.tensor_copy(kd[:, m, :, x, :], kk))
                dve.sem_inc(s["rope_ok"], 1)
            dve.wait_ge(s["gelu_ok"], 2)
            vv = [hsb[:, m, Z0:IN_W].rearrange("z (g d) -> z g d", g=G) for m in range(MT)]
            sq = gsq.rearrange("z (m g d) -> z m g d", m=MT, g=G)
            mean, var, std = (gst[:, x, :] for x in (0, 1, 2))
            rs = gst[:, 3, :]
            for m in range(MT):
                step(dve.tensor_reduce(mean[:, m * G:(m + 1) * G], vv[m], AX.X, ADD))
            ts(mean, mean, 1.0 / HD, None, MUL)
            for m in range(MT):
                tt(vv[m], vv[m], mean[:, m * G:(m + 1) * G].unsqueeze(2).to_broadcast([P, G, HD]), SUB_)
                tt(sq[:, m], vv[m], vv[m], MUL)
                step(dve.tensor_reduce(var[:, m * G:(m + 1) * G], sq[:, m], AX.X, ADD))
            ts(var, var, 1.0 / HD, EPS, MUL, ADD)
            step(dve.tensor_copy(std, var))
            dve.sem_inc(s["ln_var"], 1)
            for hd in range(HQ):
                dve.wait_ge(s["sc_ps"], hd + 1)
                step(dve.scalar_tensor_tensor(pr_[:, hd].rearrange("z a b -> z (a b)"), bank(hd), HD ** -0.5,
                                              mask.rearrange("z a b -> z (a b)"), MUL, ADD))
                dve.sem_inc(s["sc_sb"], 1)
            step(dve.tensor_reduce(mxs.rearrange("z a b -> z (a b)"), pr_.rearrange("z a b c -> z (a b) c"), AX.X, ALU.max))
            sinkb = sink.unsqueeze(2).to_broadcast([P, HQ, MT])
            tt(mxs, mxs, sinkb, ALU.max)
            ts(den[:, 0, :], mxs.rearrange("z a b -> z (a b)"), -1.0, None, MUL)
            tt(den[:, 2, :].rearrange("z (a b) -> z a b", b=MT), sinkb, mxs, SUB_)
            dve.sem_inc(s["mx_ok"], 1)
            dve.wait_ge(s["ln_std"], 1)

            def refine(rs_, std_, var_, t_):
                step(dve.reciprocal(rs_, std_))
                tt(t_, rs_, rs_, MUL)
                tt(t_, t_, var_, MUL)
                ts(t_, t_, -0.5, 1.5, MUL, ADD)
                tt(rs_, rs_, t_, MUL)

            refine(rs, std, var, mean)
            for m in range(MT):
                tt(vv[m], vv[m], rs[:, m * G:(m + 1) * G].unsqueeze(2).to_broadcast([P, G, HD]), MUL)
                fv = hsb[:, m, Z0:IN_W]
                tt(fv, fv, sgln[:, 0, :], MUL)
                tt(fv, fv, sgln[:, 1, :], ADD)
            dve.sem_inc(s["vn_ok"], 1)
            dve.wait_ge(s["exp_ok"], 2 * HQ + 1)
            tt(den[:, 3, :], den[:, 1, :], den[:, 2, :], ADD)
            step(dve.reciprocal(den[:, 1, :], den[:, 3, :]))
            pf = pr_.rearrange("z a b c -> z (a b) c")
            tt(pf, pf, den[:, 1, :].unsqueeze(2).to_broadcast([P, HQ * MT, SEQ]), MUL)
            dve.sem_inc(s["p_ok"], 1)
            dve.wait_ge(s["sv_ps"], 1)
            for g in range(G):
                step(dve.scalar_tensor_tensor(
                    bout[:, :, g * HD:(g + 1) * HD],
                    ps[:, g // 4, (g % 4) * P:(g % 4 + 1) * P].rearrange("z (m d) -> z m d", m=MT), sgub[:, g:g + 1],
                    hsb[:, :, U0 + g * HD:U0 + (g + 1) * HD], ADD, MUL))
            dve.sem_inc(s["bo_ok"], 1)

            def norm(n, add_rest):
                for m in range(MT):
                    add_rest(m)
                    for x in range(2):
                        step(dve.bn_stats(stats[:, m, x, :], res[:, m, x * 512:(x + 1) * 512]))
                    step(dve.bn_aggr(mv[:, m, :], stats[:, m].rearrange("z a b -> z (a b)")))
                    ts(ln_s[:, m, 0:1], mv[:, m, 1:2], EPS, None, ADD)
                    dve.sem_inc(s["ln_var"], 1)
                for m in range(MT):
                    dve.wait_ge(s["ln_std"], 1 + 2 * n + m + 1)
                    refine(ln_s[:, m, 2:3], ln_s[:, m, 1:2], ln_s[:, m, 0:1], ln_s[:, m, 3:4])
                    dve.wait_ge(s["ln_p"], 32 * (n + 1))
                    ts(res[:, m], res[:, m], mv[:, m, 0:1], ln_s[:, m, 2:3], SUB_, MUL)
                    tt(res[:, m], res[:, m], lnp[:, 0], MUL)
                    step(dve.tensor_tensor(x_tok[:, m], res[:, m], lnp[:, 1], ADD))
                    dve.sem_inc(s["ln_out"], 1)

            def rest_of(sem_name, count):
                def add(m):
                    if m == 0 or sem_name == "op_ps":
                        dve.wait_ge(s[sem_name], count(m))
                    for n in range(2):
                        stt(res[:, m, n * 512:(n + 1) * 512], x_tok[:, m, n * 512:(n + 1) * 512], ALPHA,
                            bank(2 * m + n), MUL, ADD)
                return add

            dve.wait_ge(s["xT_ps"], 4)
            norm(0, rest_of("op_ps", lambda m: m + 1))
            for c in range(NCH):
                swiglu_dve(dve, "ffn", c, c == 0, lambda m: 1.0)
            norm(1, rest_of("ffn_down", lambda m: NCH))
            for x in range(2):
                dve.wait_ge(s[f"xk_in{x}"], 64)
                step(dve.tensor_copy(xg[:, x], xl[:, x].rearrange("z j (g c) -> z g j c", c=CG)))
                dve.sem_inc(s["xg_ok"], 1)
            step(dve.memset(Sz.rearrange("z a b c d e -> z (a b c d e)"), 0.0))
            step(dve.memset(S[:, 0, 0].rearrange("z a b -> z (a b)"), 0.0))
            step(dve.memset(S[:, 1, NC].rearrange("z a b -> z (a b)"), 0.0))
            dve.wait_ge(s["s_sb"], 2 * KT)
            T2 = KT * PR
            for i in range(1, NC):
                for d in range(2):
                    cur, prv = (i + 1, i) if d == 0 else (NC - 1 - i, NC - i)
                    pd = prod[:, d * 4 * T2:(d + 1) * 4 * T2].rearrange("z (o i t) -> z o i t", o=2, i=2)
                    tt(pd, a8[:, d], S[:, d, prv].unsqueeze(1).to_broadcast([P, 2, 2, T2]), MUL)
                    tt(S[:, d, cur], S[:, d, cur], pd[:, :, 0], ADD)
                    tt(S[:, d, cur], S[:, d, cur], pd[:, :, 1], ADD)
            for d in range(2):
                for ri in range(2):
                    for g2 in range(2):
                        src = S[64 * g2:64 * g2 + 64, d, d:NC + d, ri, :].rearrange("z n t -> z t n")
                        step(dve.tensor_copy(Sz[64 * g2:64 * g2 + 64, d, ri, :, g2, :], src))
                        dve.sem_inc(s["sz_ok"], 1)

            for c in range(GLU_CH):
                for m in range(MT):
                    dve.wait_ge(s["glu_sig"], 2 * c + m + 1)
                    if c == 0 and m == 0:
                        dve.wait_ge(s["yt_ps"], KT)
                    col = slice(c * FC, (c + 1) * FC)
                    step(dve.tensor_tensor(h[:, m, :], sg[:, m, :], ps[:, m, 0:FC], MUL))
                    dve.sem_inc(s["glu_z"], 1)
                    stt(res[:, m, col], x_tok[:, m, col], ALPHA, h[:, m, :], MUL, ADD)
            norm(2, lambda m: None)
            dve.wait_ge(s["rt_ps"], 1)
            lg, mx8 = rt[:, :, 8:16], rt[:, :, 16:24]
            tpf, m1, m2 = rt[:, :, 24:32], rt[:, :, 32:40], rt[:, :, 40:48]
            step(dve.tensor_copy(lg, ps[:, 5, 0:16].rearrange("z (m e) -> z m e", m=MT)))
            for m in range(MT):
                step(dve.max(mx8[:, m], lg[:, m]))
                step(dve.max_index(top_i[:, m], mx8[:, m], lg[:, m]))
                step(dve.tensor_copy(tpf[:, m], top_i[:, m]))
            tt(rt[:, :, 0:1], rt[:, :, 17:18], rt[:, :, 16:17], SUB_)
            dve.sem_inc(s["rt_ps"], 1)
            dve.wait_ge(s["rt_ps"], 3)
            ts(rt[:, :, 2:3], rt[:, :, 1:2], 1.0, None, ADD)
            step(dve.reciprocal(rt[:, :, 3:4], rt[:, :, 2:3]))
            tt(rt[:, :, 4:5], rt[:, :, 1:2], rt[:, :, 3:4], MUL)
            for m in range(MT):
                ts(m1[:, m], iota8[:], tpf[:, m, 0:1], rt[:, m, 3:4], ALU.is_equal, MUL)
                ts(m2[:, m], iota8[:], tpf[:, m, 1:2], rt[:, m, 4:5], ALU.is_equal, MUL)
            tt(comb[:], m1, m2, ADD)
            for m in range(MT):
                step(dve.tensor_copy(combx[:, m], comb[:, m].unsqueeze(2).to_broadcast([P, NE, NCH])))
            dve.sem_inc(s["comb_ok"], 1)
            cx = combx[:].rearrange("z m e c -> z m (e c)")
            for c in range(R + 1):
                swiglu_dve(dve, "moe", c, c == 0, lambda m: cx[:, m, c:c + 1])
            with dve.Fori(0, MOE_TURNS) as turn:
                for j in range(R):
                    swiglu_dve(dve, "moe", turn * R + (R + 1 + j), False,
                               lambda m: cx[:, m, bass.ds(turn * R + (R + 1 + j), 1)])
            for c in range(MOE_CH - R, MOE_CH):
                swiglu_dve(dve, "moe", c, False, lambda m: cx[:, m, c:c + 1])
            norm(3, rest_of("moe_down", lambda m: MOE_CH))
            dve.sem_inc(s["fin"], 2)


def layouts(inp):
    g = {k: np.asarray(v) for k, v in inp.items()}
    c = np.ascontiguousarray

    def by_k(w):
        return c(w.reshape(-1, P, w.shape[1]).transpose(1, 0, 2).reshape(P, -1))

    def swiglu_chunks(wg, wu, wd):
        e = wg.shape[0]
        gu = np.stack([w.reshape(e, KT, P, NCH, FC) for w in (wg, wu)], axis=4)
        gu = gu.transpose(0, 3, 2, 1, 4, 5).reshape(e * NCH, P, KT * 2 * FC)
        dn = wd.reshape(e, NCH, SUB, P, D).transpose(0, 1, 3, 2, 4).reshape(e * NCH, P, SUB * D)
        return c(np.concatenate([gu, dn], axis=2))

    o = {"x": c(g["x"][0])}
    o["w_in"], o["w_out"] = by_k(g["mix_w_in"][0]), by_k(g["mix_w_out"][0])
    o["w_router"] = by_k(g["router_w"][0])
    o["ln_g"], o["ln_b"] = c(g["ln_g"].reshape(4, D)), c(g["ln_b"].reshape(4, D))
    o["sguT"] = c(g["sgu_w"][0].transpose(2, 0, 1).reshape(P, G * P))
    o["sgub"] = c(g["sgu_b"][0].T)
    o["sgln"] = c(np.concatenate([g["sgu_ln_g"][0].reshape(1, -1), g["sgu_ln_b"][0].reshape(1, -1)], axis=1))
    o["sink"] = c(g["attn_sink"])
    o["ffn_w"] = swiglu_chunks(g["ffn_w_gate"], g["ffn_w_up"], g["ffn_w_down"])
    o["moe_w"] = swiglu_chunks(g["moe_w_gate"][0], g["moe_w_up"][0], g["moe_w_down"][0])
    glu = np.stack([g[n][0].reshape(KT, P, GLU_CH, FC) for n in ("glu_w_val", "glu_w_gate")], axis=3)
    o["glu_w"] = c(glu.transpose(2, 1, 0, 3, 4).reshape(GLU_CH, P, KT * 2 * FC))
    def groups(w):
        return w.reshape((2, KT, PR, 2) + w.shape[2:])
    o["s5_b"] = c(np.stack([groups(g[n][0]).transpose(3, 4, 1, 0, 2, 5) for n in ("s5_b_re", "s5_b_im")], axis=2).reshape(P, -1))
    o["s5_c"] = c(np.stack([groups(g[n][0]).transpose(3, 5, 1, 0, 2, 4) for n in ("s5_c_re", "s5_c_im")], axis=2).reshape(P, -1))
    ldt = np.broadcast_to(g["s5_log_dt"][0][:, :, None], (2, 64, PS))
    o["s5_lamdt"] = c(np.stack([groups(v).transpose(3, 4, 1, 0, 2) for v in (g["s5_lam_re"][0], g["s5_lam_im"][0], ldt)], axis=2).reshape(P, 3, NT))
    o["s5_d"] = c(g["s5_d"][0].reshape(KT, P).T)
    o["ident"] = np.eye(P, dtype=np.float32)
    o["eye16"] = c(np.tile(np.eye(CG, dtype=np.float32), (8, 1)))
    o["iota8"] = c(np.tile(np.arange(NE, dtype=np.float32), (P, 1)))
    pos = np.arange(SEQ, dtype=np.float32)
    inv = (10000.0 ** (-np.arange(0, HD, 2, dtype=np.float32) / HD)).astype(np.float32)
    ang = pos[:, None] * inv[None, :]
    o["cossin"] = c(np.stack([np.cos(ang), np.sin(ang)], 1).reshape(MT, P, 2, HD // 2).transpose(1, 0, 2, 3).reshape(P, -1))
    dist = np.abs(pos[:, None] - pos[None, :])
    o["mask"] = c(np.where(dist <= 128, 0.0, NEG).astype(np.float32).reshape(MT, P, SEQ).transpose(1, 0, 2).reshape(P, -1))
    return o


def kernel(**inputs):
    import concourse.bacc as _bacc
    from concourse import bass_utils as _bu

    nc = _bacc.Bacc("TRN2", target_bir_lowering=False, num_devices=1)
    arrays = layouts(inputs)
    aps = {n: nc.dram_tensor("in_" + n, v.shape, mybir.dt.from_np(v.dtype), kind="ExternalInput").ap() for n, v in arrays.items()}
    out = nc.dram_tensor("out", (SEQ, D), F32, kind="ExternalOutput").ap()
    build(nc, aps, out)
    got = _bu.run_bass_kernel_spmd(nc, [{"in_" + n: v for n, v in arrays.items()}], core_ids=[0])
    return got.results[0]["out"].reshape(1, SEQ, D)
```

```python
import math
from contextlib import ExitStack

import numpy as np

import concourse.bass as bass
from concourse import mybir

P = 128
D = 1024
KT = D // P
SEQ = 256
MT = SEQ // P
HQ, HKV, HD = 8, 2, 64
QK = (HQ + HKV) * HD
V0 = QK
U0 = V0 + HKV * HD
Z0 = U0 + 512
IN_W = Z0 + 512
PROJ_N = IN_W // 4
G = 8
FF = 2816
FC = 256
SUB = FC // P
NCH = FF // FC
NE = 8
GLU_CH = D // FC
ITEM = KT // 2 * 2 * FC
PER = 3
ITEMS = NCH * PER
R = 11
GLU_ITEMS = GLU_CH * 2
MOE_ITEM0 = ITEMS + GLU_ITEMS
assert ITEM == SUB * D and ITEMS % R == 0
NOV = 2 * SEQ // (P + 1)
TURNS = 1 + NE + NOV
ALPHA = (2.0 * 2) ** 0.25
EPS = 1e-5
NEG = -1e30
L, NC, CG, PS = 8, 32, 16, 64
PR = 4
NT = KT * PR * 2
MAGIC = 1.5 * 2.0**23

F32 = mybir.dt.float32
I32 = mybir.dt.int32
F32R = mybir.dt.float32r
U32 = mybir.dt.uint32
ALU = mybir.AluOpType
ACT = mybir.ActivationFunctionType
AX = mybir.AxisListType
DEBUG = ()


class Steps:

    def __init__(self, eng, sem):
        self.eng, self.sem, self.n, self.offset = eng, sem, 0, 0

    def __call__(self, ins):
        self.n += 1
        ins.then_inc(self.sem, 1)
        self.eng.wait_ge(self.sem, self.offset + self.n)

    def loop(self, i, per_turn):
        self.start, self.per_turn = self.n, per_turn
        self.offset = i * per_turn

    def end_loop(self, turns):
        assert self.n - self.start == self.per_turn, (self.n - self.start, self.per_turn)
        self.n = self.start + self.per_turn * turns
        self.offset = 0


def build(nc, a, out):
    with ExitStack() as ctx:

        def sem(name):
            return ctx.enter_context(nc.semaphore(name))

        def sbuf(name, shape, dt=F32):
            return ctx.enter_context(nc.sbuf_tensor(name, [P] + list(shape), dt))

        S5_SLOT = 8
        ARENA = 23168
        MEM = S5_SLOT * ITEM + ARENA
        mem = sbuf("mem", [MEM])
        base = nc.sbuf_base - 4 * MEM
        ring = mem[:, 0:R * ITEM].rearrange("z (s n) -> z s n", s=R)
        arena = mem[:, S5_SLOT * ITEM:MEM]

        def over_mem(name, at, shape):
            assert at >= R * ITEM and at + int(np.prod(shape)) <= MEM
            return nc.alloc_sbuf_tensor_at(name, [P] + list(shape), F32R, offset=base + 4 * at)

        wh = over_mem("wh", R * ITEM, [PER, ITEM])
        wl = over_mem("wl", R * ITEM + PER * ITEM, [PER, ITEM])
        xh = over_mem("xh", R * ITEM + 2 * PER * ITEM, [MT, KT, P])
        xl_ = over_mem("xl", R * ITEM + 2 * PER * ITEM + MT * KT * P, [MT, KT, P])
        x_tok = sbuf("x_tok", [MT, D])
        xT = sbuf("xT", [KT, SEQ])
        res = sbuf("res", [MT, D])
        lnp = sbuf("lnp", [2, D])
        ident = sbuf("ident", [P])
        sg = sbuf("sg", [MT, FC])
        h = sbuf("h", [MT, FC])
        hTh = sbuf("hTh", [MT, SUB, P], F32R)
        hTl = sbuf("hTl", [MT, SUB, P], F32R)
        stats = sbuf("stats", [MT, 2, 6])
        mv = sbuf("mv", [MT, 2])
        ln_s = sbuf("ln_s", [MT, 4])
        a8 = sbuf("a8", [2, 2, 2, KT * PR])
        wr_sb = sbuf("wr_sb", [KT, NE])
        rt = sbuf("rt", [MT, 64])
        sel = sbuf("sel", [MT, NE])
        comb = sbuf("comb", [MT, NE])
        posx, selx, combx = (sbuf(n, [MT, TURNS + 1]) for n in ("posx", "selx", "combx"))
        over = sbuf("over", [6, NE])
        over_i = sbuf("over_i", [4], I32)
        top_i = sbuf("top_i", [MT, 8], U32)
        iota8, iotaP = sbuf("iota8", [NE]), sbuf("iotaP", [P])
        tri, ones = sbuf("tri", [P]), sbuf("ones", [P])
        pw_i = sbuf("pw_i", [NT], I32)
        xTf = xT[:].rearrange("z a b -> z (a b)")
        pg = xTf[:, 0:2 * P].rearrange("z (m n) -> z m n", m=MT)
        pgc = xTf[:, 2 * P:4 * P].rearrange("z (m n) -> z m n", m=MT)
        scat = xTf[:, 4 * P:6 * P]
        ysb = xTf[:, 6 * P:6 * P + D]
        ps = ctx.enter_context(nc.psum_tensor("ps", [P, 8, 512], F32))

        class Region:
            def __init__(self):
                self.at = 0

            def __call__(self, *shape):
                n = int(np.prod(shape))
                v = arena[:, self.at:self.at + n]
                self.at += n
                assert self.at <= ARENA, self.at
                names = "abcdef"[:len(shape)]
                if len(shape) > 1:
                    v = v.rearrange(f"z ({' '.join(names)}) -> z {' '.join(names)}",
                                    **{n_: s for n_, s in zip(names[1:], shape[1:])})
                return v

        r = Region()
        Bp, Cp, Cq = r(2, KT, 2, PR, CG), r(2, KT, 2, PR, CG), r(2, KT, 2, PR, CG)
        lamdt = r(3, NT)
        pa = r(2, NT, L + 1)
        p2, p1 = r(2, KT, 2, PR, L + 1), r(2, KT, 2, PR, L)
        ta, tb = r(2 * PR, L + 1, CG), r(2 * PR, L + 1, CG)
        w2 = r(2, 2 * PR, L + 1, CG)
        w1t = r(2, 2 * PR, L, CG)
        w1 = r(16, P)
        Bz = r(2, 2 * PR, 2, CG)
        kext = r(2 * L - 1, CG)
        Dd, Dp, eye16 = r(KT, CG), r(KT), r(CG)
        sm = r(24, NT)

        r = Region()
        hsb = r(MT, IN_W)
        qkr = r(MT, HQ + HKV, 2, HD // 2)
        kd = r(MT, HKV, 2, HD)
        qT, kT = r(4, SEQ), r(HKV, SEQ)
        pr_ = r(HQ, MT, SEQ)
        pT = r(HQ, 2, SEQ)
        mixT = r(KT, SEQ)
        sguT, sgub = r(G, P), r(G)
        sgln = r(2, 512)
        bout = r(MT, 512)
        mask = r(MT, SEQ)
        cs = r(MT, 2, HD // 2)
        sink = r(HQ)
        mxs, den = r(HQ, MT), r(4, HQ * MT)
        rtmp = r(2, HQ + HKV, HD // 2)
        gst = r(4, MT * G)
        gsq = pr_[:, 0:4, :, :].rearrange("z a b c -> z (a b c)")[:, 0:1024]

        r = Region()
        xg = r(2, 8, L, CG)
        yk = xg.rearrange("z a b c d -> z a (b c d)").rearrange("z a (i f) -> z a i f", i=L)
        xl = res[:].rearrange("z a (j f) -> z a j f", j=L)
        U = r(64, NC)
        wb = r(2, 2 * 2 * PR * (L + 1) * CG)
        Tb = r(2, 8, P)
        S = r(2, NC + 1, 2, KT * PR)
        Sz = r(2, 2, KT * PR, 2, NC)
        prod = sg[:].rearrange("z a b -> z (a b)")

        def dram(name, shape):
            return nc.dram_tensor(name, shape, F32, kind="Internal").ap()

        w1_d = dram("w1_d", (KT, P, 16 * P))
        w2_d = dram("w2_d", (KT, P, 2 * 2 * PR * (L + 1) * CG))
        kext_d = dram("kext_d", (KT, P, (2 * L - 1) * CG))
        x2_d = dram("x2_d", (SEQ, D))

        names = """const_in x_in win_in wout_in lamdt_in s5_in eye_in
            act_step dve_step pool_step
            s5_ready s5_free bz_ready w1t_ps w1_sb kgen_ps kext_sb s5_bz s5_w1t s5_w2 s5_kx w1_out kx_out
            a_done x0T_ps x0T_sb proj_ps proj_sb rope_ok qkT_ps qkT_sb sc_ps sc_sb mx_ok exp_ok p_ok
            pT_ps pT_sb pv_ps pv_sb gelu_ok vn_ok sv_ps bo_ok bT_ps bT_sb op_ps attn_ok
            ln_in ln_var ln_std ln_out xT_ps xT_sb ln_p
            glu_ps glu_sig glu_z
            gu_used gu_hi gu_lo dn_hi dn_lo silu_ok h_ok tr_ps hT_hi hT_lo down_ok x1_lo
            hot_ok gath_ps xe_hi xe_lo scat_ps scat_sb ysb_ok put_ps acc_ok sel_ok rank_ps route_ok res_ok
            x2_out xg_ok xk_in0 xk_in1 uT_ps u_sb wk_in0 wk_in1 tk_in0 tk_in1 s_ps s_sb scan_ok scan_p sz_ok y_ps y_g yt_ps yt_sb
            rt_ps comb_ok fin out_sent dbg wk_used""".split()
        s = {n: sem(n) for n in names}
        slot_full = [sem(f"slot_full{i}") for i in range(R)]
        def bank(i, n=512):
            return ps[:, i, 0:n]

        w_in_v = mem[:, 0:KT * IN_W].rearrange("z (k n) -> z k n", k=KT)
        w_out_v = mem[:, 0:KT * D].rearrange("z (k n) -> z k n", k=KT)

        block = ctx.enter_context(nc.Block())

        @block.sync
        def _(sp):
            sp.dma_start(lamdt, a["s5_lamdt"]).then_inc(s["lamdt_in"], 16)
            sp.dma_start(ident[:], a["ident"]).then_inc(s["eye_in"], 16)
            for dst, n in ((Bp, "s5_b"), (Cp, "s5_c")):
                sp.dma_start(dst.rearrange("z a b c d e -> z (a b c d e)"), a[n]).then_inc(s["s5_in"], 16)
            sp.dma_start(Dp, a["s5_d"]).then_inc(s["s5_in"], 16)
            sp.dma_start(eye16, a["eye16"]).then_inc(s["s5_in"], 16)
            sp.dma_start(x_tok[:], a["x"].rearrange("(m p) d -> p m d", p=P)).then_inc(s["x_in"], 16)
            sp.dma_start(mem[:, 0:KT * IN_W], a["w_in"]).then_inc(s["win_in"], 16)
            sp.dma_start(wr_sb[:].rearrange("z k e -> z (k e)"), a["w_router"]).then_inc(s["eye_in"], 16)
            for dst, n in ((iota8, "iota8"), (iotaP, "iotaP"), (tri, "tri")):
                sp.dma_start(dst[:], a[n]).then_inc(s["eye_in"], 16)
            sp.wait_ge(s["a_done"], 1)
            for dst, n in ((sguT.rearrange("z a b -> z (a b)"), "sguT"), (sgub, "sgub"),
                           (mask.rearrange("z a b -> z (a b)"), "mask"),
                           (cs.rearrange("z a b c -> z (a b c)"), "cossin"),
                           (sink, "sink"), (sgln.rearrange("z a b -> z (a b)"), "sgln")):
                src = a[n] if a[n].shape[0] == P else a[n].to_broadcast([P, a[n].shape[1]])
                sp.dma_start(dst, src).then_inc(s["const_in"], 16)
            sp.wait_ge(s["proj_ps"], 8)
            sp.dma_start(mem[:, 0:KT * D], a["w_out"]).then_inc(s["wout_in"], 16)

            def load_item(slot, src):
                sp.dma_start(ring[:, slot, :], src).then_inc(slot_full[slot], 16)

            def wait_split(turn, i):
                n, j = turn * NCH + i // PER, i % PER
                if j < 2:
                    sp.wait_ge(s["gu_lo"], 2 * n + (j + 1))
                else:
                    sp.wait_ge(s["dn_lo"], n + 1)

            for i in (4, 5, 6, 7, 0, 1, 2, 3, 8, 9, 10):
                if i in (0, 8):
                    sp.wait_ge(s["op_ps"], 2)
                load_item(i, a["ffn_w"][i])
            for i in range(R, ITEMS):
                wait_split(0, i - R)
                load_item(i % R, a["ffn_w"][i])
            for i in range(GLU_ITEMS):
                wait_split(0, ITEMS - R + i)
                load_item((ITEMS + i) % R, a["glu_w"][i])
            for i in range(ITEMS):
                if i < R - GLU_ITEMS:
                    wait_split(0, ITEMS - R + GLU_ITEMS + i)
                if i == 0:
                    sp.wait_ge(s["yt_ps"], KT)
                elif R - GLU_ITEMS <= i < R:
                    sp.wait_ge(s["glu_ps"], 2 * ((i - (R - GLU_ITEMS)) // 2 + 1))
                elif i >= R:
                    wait_split(1, i - R)
                load_item((MOE_ITEM0 + i) % R, a["moe_w"][i])

            def load_expert(turn, e):
                for i in range(ITEMS):
                    wait_split(turn, i - R)
                    load_item((MOE_ITEM0 + i) % R,
                              a["moe_w"][bass.ds(e * ITEMS + i, 1)].rearrange("o p n -> (o p) n"))

            with sp.Fori(2, 1 + NE) as turn:
                load_expert(turn, turn - 1)
            sp.wait_ge(s["route_ok"], 1)
            n_over = sp.value_load(over_i[0:1, 0:1], min_val=0, max_val=NOV)
            with sp.Fori(0, NOV) as i:
                with sp.If(i < n_over):
                    e = sp.value_load(over_i[0:1, bass.ds(i + 1, 1)], min_val=0, max_val=NE - 1)
                    load_expert(i + (1 + NE), e)
            sp.wait_ge(s["fin"], 2)
            sp.dma_start(out.rearrange("(m p) d -> p m d", p=P), x_tok[:]).then_inc(s["out_sent"], 16)
            sp.wait_ge(s["out_sent"], 16)

        def s5_loads(pool):
            pool.wait_ge(s["x2_out"], 16)
            xk = x2_d.rearrange("(n j) (k f) -> k n j f", j=L, f=P)
            for k in range(KT):
                pool.dma_start(xl[NC * (k % 4):NC * (k % 4 + 1), k // 4], xk[k]).then_inc(s[f"xk_in{k // 4}"], 16)
            for k in range(2 * KT):
                if 2 <= k < KT + 2:
                    pool.wait_ge(s["wk_used"], k - 1)
                elif k >= KT + 2:
                    pool.wait_ge(s["y_ps"], k - KT - 1)
                src = w1_d[k] if k < KT else w2_d[k - KT]
                pool.dma_start(wb[:, k % 2, 0:src.shape[1]], src).then_inc(s[f"wk_in{k % 2}"], 16)
                if k >= KT:
                    kk = k - KT
                    for j in range(L):
                        src = kext_d[kk][:, (L - 1 - j) * CG:(2 * L - 1 - j) * CG].rearrange("(g c) n -> c g n", c=CG)
                        pool.dma_start(Tb[j * CG:(j + 1) * CG, kk % 2], src).then_inc(s[f"tk_in{kk % 2}"], 16)

        @block.gpsimd
        def _(pool):
            with pool.Fori(0, KT) as k:
                pool.wait_ge(s["s5_w2"], k + 1)
                pool.dma_start(w2_d[bass.ds(k, 1)].rearrange("o p n -> (o p) n"),
                               w2.rearrange("z a b c d -> z (a b c d)")).then_inc(s["s5_free"], 16)
                pool.wait_ge(s["w1_sb"], 4 * k + 4)
                pool.dma_start(w1_d[bass.ds(k, 1)].rearrange("o p n -> (o p) n"),
                               w1.rearrange("z a b -> z (a b)")).then_inc(s["w1_out"], 16)
                pool.wait_ge(s["kext_sb"], k + 1)
                pool.dma_start(kext_d[bass.ds(k, 1)].rearrange("o p n -> (o p) n"),
                               kext.rearrange("z a b -> z (a b)")).then_inc(s["kx_out"], 16)
            pool.wait_ge(s["s5_free"], 16 * KT)
            pool.wait_ge(s["w1_out"], 16 * KT)
            pool.wait_ge(s["kx_out"], 16 * KT)
            for n in range(4):
                if n:
                    pool.wait_ge(s["ln_out"], 2 * n)
                if n == 2:
                    pool.dma_start(x2_d.rearrange("(m p) d -> p m d", p=P), x_tok[:]).then_inc(s["x2_out"], 16)
                for j, what in enumerate(("ln_g", "ln_b")):
                    pool.dma_start(lnp[:, j, :], a[what][n:n + 1, :].to_broadcast([P, D])).then_inc(s["ln_p"], 16)
                if n == 2:
                    s5_loads(pool)

        def products(pe, o, lhs, rhs, start, stop):
            (lh, ll), (rh, rl) = lhs, rhs
            pe.matmul(o, ll, rh, start=start, stop=False)
            pe.matmul(o, lh, rl, start=False, stop=False)
            return pe.matmul(o, lh, rh, start=False, stop=stop)

        def gate_up(pe, n, tiles, first):
            for j in range(2):
                pe.wait_ge(s["gu_lo"], 2 * n + (j + 1))
                if j == 0 and not first:
                    pe.wait_ge(s["h_ok"], n)
                for m in tiles:
                    for k in range(KT // 2):
                        kk = j * KT // 2 + k
                        w = slice(k * 2 * FC, (k + 1) * 2 * FC)
                        mm = products(pe, bank(4 + m), (xh[:, m, kk, :], xl_[:, m, kk, :]),
                                      (wh[:, j, w], wl[:, j, w]), kk == 0, kk == KT - 1)
                mm.then_inc(s["gu_used"], 1)

        def turn_h(pe, n, tiles):
            pe.wait_ge(s["h_ok"], n + 1)
            for m in tiles:
                for t in range(SUB):
                    mm = pe.transpose(ps[:, 6, (m * SUB + t) * P:(m * SUB + t + 1) * P],
                                      h[:, m, t * P:(t + 1) * P], ident[:])
            mm.then_inc(s["tr_ps"], 1)

        def down(pe, n, tiles, start, stop):
            pe.wait_ge(s["hT_lo"], n + 1)
            pe.wait_ge(s["dn_lo"], n + 1)
            for m in tiles:
                for t in range(SUB):
                    for b in range(2):
                        w = slice(t * D + b * 512, t * D + (b + 1) * 512)
                        mm = products(pe, bank(2 * m + b), (hTh[:, m, t, :], hTl[:, m, t, :]),
                                      (wh[:, 2, w], wl[:, 2, w]), start and t == 0, stop and t == SUB - 1)
            mm.then_inc(s["down_ok"], 1)

        def swiglu_pe(pe, turn, tiles, first, before_down, before_last):
            n = turn * NCH
            gate_up(pe, n, tiles, first)
            turn_h(pe, n, tiles)
            gate_up(pe, n + 1, tiles, False)
            before_down()
            down(pe, n, tiles, True, False)
            turn_h(pe, n + 1, tiles)
            with pe.Fori(2, NCH) as c:
                gate_up(pe, c + n, tiles, False)
                down(pe, c + (n - 1), tiles, False, False)
                turn_h(pe, c + n, tiles)
            before_last()
            down(pe, n + (NCH - 1), tiles, False, True)

        def split_hi(act, n, j, slot, use, first):
            act.wait_ge(slot_full[slot], use)
            if not first:
                act.wait_ge(s["gu_used" if j < 2 else "down_ok"], 2 * n + (j - 1) if j < 2 else n)
            act.copy(wh[:, j, :], ring[:, slot, :]).then_inc(s["gu_hi" if j < 2 else "dn_hi"], 1)

        def swiglu_act(act, turn, tiles, first, item0, uses):
            n = turn * NCH
            for j in range(2):
                split_hi(act, n, j, (item0 + j) % R, uses(j), first)
            for c in range(NCH):
                for part in range(PER):
                    ahead = 1 if part < 2 else 0
                    if c + ahead < NCH:
                        i = (c + ahead) * PER + part
                        split_hi(act, n + (c + ahead), part, (item0 + i) % R, uses(i), first and c + ahead == 0)
                    if part == 0:
                        act.wait_ge(s["gu_used"], 2 * (n + c) + 2)
                        if c or not first:
                            act.wait_ge(s["h_ok"], n + c)
                        o = sg[:, 0:len(tiles), :]
                        act.activation(o, ps[:, 4:4 + len(tiles), 0:FC], ACT.Silu).then_inc(s["silu_ok"], 1)
                    elif part == 2:
                        act.wait_ge(s["tr_ps"], n + (c + 1))
                        act.copy(hTh[:, 0:len(tiles)].rearrange("z m t n -> z (m t n)"),
                                 ps[:, 6, 0:len(tiles) * FC]).then_inc(s["hT_hi"], 1)

        def split_lo(dve, n, j, slot):
            dve.wait_ge(s["gu_hi" if j < 2 else "dn_hi"], 2 * n + (j + 1) if j < 2 else n + 1)
            dve.tensor_tensor(wl[:, j, :], ring[:, slot, :], wh[:, j, :].bitcast(F32),
                              ALU.subtract).then_inc(s["gu_lo" if j < 2 else "dn_lo"], 1)

        def swiglu_dve(dve, turn, tiles, first, item0, between=None):
            n = turn * NCH
            for j in range(2):
                split_lo(dve, n, j, (item0 + j) % R)
            for c in range(NCH):
                for part in range(PER):
                    ahead = 1 if part < 2 else 0
                    if c + ahead < NCH:
                        split_lo(dve, n + (c + ahead), part, (item0 + (c + ahead) * PER + part) % R)
                    if part == 0:
                        dve.wait_ge(s["silu_ok"], n + (c + 1))
                        if c or not first:
                            dve.wait_ge(s["tr_ps"], n + c)
                        dve.tensor_tensor(h[:, 0:len(tiles), :], sg[:, 0:len(tiles), :],
                                          ps[:, 4:4 + len(tiles), FC:2 * FC], ALU.mult).then_inc(s["h_ok"], 1)
                    elif part == 2:
                        dve.wait_ge(s["hT_hi"], n + (c + 1))
                        w = len(tiles) * FC
                        dve.tensor_tensor(hTl[:, 0:len(tiles)].rearrange("z m t n -> z (m t n)"), ps[:, 6, 0:w],
                                          hTh[:, 0:len(tiles)].bitcast(F32).rearrange("z m t n -> z (m t n)"),
                                          ALU.subtract).then_inc(s["hT_lo"], 1)
                if c == 4 and between is not None:
                    between()

        def turn_y(pe, k):
            pe.wait_ge(s["y_g"], 4 * (k + 1))
            if k >= 2:
                pe.wait_ge(s["yt_sb"], k - 1)
            for i in range(L):
                mm = pe.transpose(ps[:, k % 2, i * NC:(i + 1) * NC], yk[0:NC, k % 2, i, :], ident[0:NC, 0:NC])
            mm.then_inc(s["yt_ps"], 1)

        @block.tensor
        def _(pe):
            pe.wait_ge(s["eye_in"], 80)
            def s5_tables_pe(k, first):
                pe.wait_ge(s["s5_w2"], k + 1)
                pe.wait_ge(s["s5_bz"], k + 1)
                if not first:
                    pe.wait_ge(s["s5_kx"], k)
                for d in range(2):
                    for p in range(PR):
                        for ri in range(2):
                            mm = pe.matmul(ps[32 * p:32 * p + 32, 4 + d, 0:P],
                                           Bz[:, ri, d * PR + p].rearrange("z a b -> z (a b)"),
                                           w2[:, ri, d * PR + p, d:d + L, :].rearrange("z a b -> z (a b)"),
                                           start=ri == 0, stop=ri == 1)
                mm.then_inc(s["kgen_ps"], 1)
                pe.wait_ge(s["s5_w1t"], k + 1)
                if not first:
                    pe.wait_ge(s["w1_sb"], 4 * k)
                for t in range(16):
                    mm = pe.transpose(ps[:, t // 4, (t % 4) * P:(t % 4 + 1) * P],
                                      w1t[:, t // 8, t % 8].rearrange("z a b -> z (a b)"), ident[:])
                    if t % 4 == 3:
                        mm.then_inc(s["w1t_ps"], 1)

            s5_tables_pe(0, True)
            with pe.Fori(1, KT) as k:
                s5_tables_pe(k, False)

            def turn_x(ready, count):
                for t in range(4):
                    m, half = t // 2, t % 2
                    pe.wait_ge(s["ln_out" if ready is None else ready], (count + m + 1) if ready is None else 16)
                    if t >= 2:
                        pe.wait_ge(s["xT_sb"], pe_turns[0] * 4 + t - 1)
                        if pe_turns[0] == 1:
                            pe.wait_ge(s["x1_lo"], t - 1)
                    for j in range(4):
                        mm = pe.transpose(ps[:, 6 + t % 2, j * P:(j + 1) * P],
                                          x_tok[:, m, (4 * half + j) * P:(4 * half + j + 1) * P], ident[:])
                    mm.then_inc(s["xT_ps"], 1)
                pe_turns[0] += 1

            pe_turns = [0]
            turn_x("x_in", 0)
            pe.wait_ge(s["xT_sb"], 4)
            pe.wait_ge(s["win_in"], 16)
            pe.wait_ge(s["w1_sb"], 4 * KT)
            pe.wait_ge(s["s5_kx"], KT)
            for m in range(MT):
                for n in range(4):
                    for k in range(KT):
                        mm = pe.matmul(bank(4 * m + n, PROJ_N), xT[:, k, m * P:(m + 1) * P],
                                       w_in_v[:, k, n * PROJ_N:(n + 1) * PROJ_N], start=k == 0, stop=k == KT - 1)
                    mm.then_inc(s["proj_ps"], 1)
            pe.wait_ge(s["proj_sb"], 8)
            pe.wait_ge(s["rope_ok"], 2)
            for m in range(MT):
                for j in range(4):
                    pe.transpose(ps[:, j // 2, (j % 2) * SEQ + m * P:(j % 2) * SEQ + (m + 1) * P],
                                 qkr[:, m, 2 * j:2 * j + 2].rearrange("z a b c -> z (a b c)"), ident[:])
                for j in range(HKV):
                    mm = pe.transpose(ps[:, 2, j * SEQ + m * P:j * SEQ + (m + 1) * P],
                                      kd[:, m, j].rearrange("z a b -> z (a b)"), ident[:])
            mm.then_inc(s["qkT_ps"], 1)
            pe.wait_ge(s["qkT_sb"], 3)
            for hd in range(HQ):
                o = HD * (hd % 2)
                for m in range(MT):
                    mm = pe.matmul(ps[:, hd, m * SEQ:(m + 1) * SEQ], qT[o:o + HD, hd // 2, m * P:(m + 1) * P],
                                   kT[o:o + HD, hd // 4, :], start=True, stop=True)
                mm.then_inc(s["sc_ps"], 1)
            pe.wait_ge(s["vn_ok"], 1)
            pe.wait_ge(s["sc_sb"], 8)
            pe.wait_ge(s["const_in"], 96)
            for g in range(G):
                mm = pe.matmul(ps[:, g // 4, (g % 4) * P:(g % 4 + 1) * P], sguT[:, g, :],
                               hsb[:, :, Z0 + g * HD:Z0 + (g + 1) * HD], start=True, stop=True)
            mm.then_inc(s["sv_ps"], 1)
            for hd in range(HQ):
                pe.wait_ge(s["p_ok"], 1)
                if hd >= 4:
                    pe.wait_ge(s["pT_sb"], hd - 3)
                for m in range(MT):
                    for kt in range(2):
                        mm = pe.transpose(ps[:, 2 + hd % 4, kt * SEQ + m * P:kt * SEQ + (m + 1) * P],
                                          pr_[:, hd, m, kt * P:(kt + 1) * P], ident[:])
                mm.then_inc(s["pT_ps"], 1)
            pe.wait_ge(s["bo_ok"], 1)
            for m in range(MT):
                for j in range(4):
                    mm = pe.transpose(ps[:, j // 2, (j % 2) * SEQ + m * P:(j % 2) * SEQ + (m + 1) * P],
                                      bout[:, m, j * P:(j + 1) * P], ident[:])
            mm.then_inc(s["bT_ps"], 1)
            for hd in range(HQ):
                pe.wait_ge(s["pT_sb"], hd + 1)
                o = HD * (hd % 2)
                for kt in range(2):
                    v = hsb[:, kt, V0 + (hd // 4) * HD:V0 + (hd // 4 + 1) * HD]
                    mm = pe.matmul(ps[o:o + HD, 6 + hd // 4, (hd // 2 % 2) * SEQ:(hd // 2 % 2 + 1) * SEQ],
                                   v, pT[:, hd, kt, :], start=kt == 0, stop=kt == 1)
            mm.then_inc(s["pv_ps"], 1)
            pe.wait_ge(s["wout_in"], 16)
            pe.wait_ge(s["attn_ok"], 4)
            for m in range(MT):
                for n in range(2):
                    for k in range(KT):
                        mm = pe.matmul(bank(2 * m + n), mixT[:, k, m * P:(m + 1) * P],
                                       w_out_v[:, k, n * 512:(n + 1) * 512], start=k == 0, stop=k == KT - 1)
                mm.then_inc(s["op_ps"], 1)
            turn_x(None, 0)
            pe.wait_ge(s["x1_lo"], 4)
            swiglu_pe(pe, 0, range(MT), True, lambda: None, lambda: None)
            for k in range(KT):
                pe.wait_ge(s["xg_ok"], k // 4 + 1)
                if k == 0:
                    pe.wait_ge(s["ln_out"], 4)
                if k >= 2:
                    pe.wait_ge(s["u_sb"], k - 1)
                o = NC * (k % 4)
                for g in range(8):
                    mm = pe.transpose(ps[:, 4 + k % 2, g * NC:(g + 1) * NC],
                                      xg[o:o + NC, k // 4, g].rearrange("z a b -> z (a b)"),
                                      ident[o:o + NC, o:o + NC])
                mm.then_inc(s["uT_ps"], 1)
            for k in range(KT):
                pe.wait_ge(s["u_sb"], k + 1)
                pe.wait_ge(s[f"wk_in{k % 2}"], 16 * (k // 2 + 1))
                if k >= 2:
                    pe.wait_ge(s["s_sb"], 2 * k - 2)
                for ri in range(2):
                    for d in range(2):
                        for p in range(PR):
                            t = (ri * 2 + d) * PR + p
                            for g2 in range(2):
                                mm = pe.matmul(ps[64 * g2:64 * g2 + 64, 6 + k % 2, ((d * 2 + ri) * PR + p) * NC:((d * 2 + ri) * PR + p + 1) * NC],
                                               wb[:, k % 2, t * P + 64 * g2:t * P + 64 * g2 + 64],
                                               U[:, 8 * k + 2 * p + g2, :], start=True, stop=True)
                mm.then_inc(s["wk_used"], 1)
            for k in range(KT):
                if k >= 2:
                    pe.wait_ge(s["y_g"], 4 * (k - 1))
                elif k == 0:
                    pe.wait_ge(s["sz_ok"], 8)
                pe.wait_ge(s[f"tk_in{k % 2}"], 16 * L * (k // 2 + 1))
                pe.wait_ge(s[f"wk_in{k % 2}"], 16 * ((k + KT) // 2 + 1))
                w2v = wb[:, k % 2].rearrange("z (r d p l) -> z r d p l", r=2, d=2, p=PR)
                for p in range(PR):
                    o = 64 * (p % 2)
                    col = slice((p // 2) * P, (p // 2 + 1) * P)
                    for d in range(2):
                        for ri in range(2):
                            lo = CG if d == 0 else 0
                            pe.matmul(ps[o:o + 64, 4 + k % 2, col],
                                      Sz[:, d, ri, k * PR + p].rearrange("z a b -> z (a b)"),
                                      w2v[:, ri, d, p, lo:lo + P], start=d + ri == 0, stop=False,
                                      skip_group_check=True)
                    for g2 in range(2):
                        mm = pe.matmul(ps[o + 32 * g2:o + 32 * g2 + 32, 4 + k % 2, col],
                                       U[:, 8 * k + 2 * p + g2, :], Tb[:, k % 2, 2 * p + g2, :],
                                       start=False, stop=True, skip_group_check=True)
                mm.then_inc(s["y_ps"], 1)
                if k >= 1:
                    turn_y(pe, k - 1)
            turn_y(pe, KT - 1)
            pe.wait_ge(s["yt_sb"], KT)
            for c in range(GLU_CH):
                for m in range(MT):
                    if c:
                        pe.wait_ge(s["glu_z"], 2 * c - 1 + m)
                    for k in range(KT):
                        item = ITEMS + 2 * c + k // (KT // 2)
                        if m == 0 and k % (KT // 2) == 0:
                            pe.wait_ge(slot_full[item % R], 16 * (item // R + 1))
                        kk = k % (KT // 2)
                        mm = pe.matmul(bank(m), xT[:, k, m * P:(m + 1) * P],
                                       ring[:, item % R, kk * 2 * FC:(kk + 1) * 2 * FC],
                                       start=k == 0, stop=k == KT - 1)
                    mm.then_inc(s["glu_ps"], 1)
            turn_x(None, 4)
            pe.wait_ge(s["xT_sb"], 12)
            for m in range(MT):
                for k in range(KT):
                    mm = pe.matmul(ps[:, 5, m * 8:m * 8 + 8], xT[:, k, m * P:(m + 1) * P], wr_sb[:, k, :],
                                   start=k == 0, stop=k == KT - 1)
            mm.then_inc(s["rt_ps"], 1)
            pe.wait_ge(s["sel_ok"], 1)
            pe.matmul(ps[:, 7, 0:NE], tri[:], sel[:, 0], start=True, stop=True)
            pe.matmul(ps[:, 7, NE:2 * NE], tri[:], sel[:, 1], start=True, stop=False)
            pe.matmul(ps[:, 7, NE:2 * NE], ones[:], sel[:, 0], start=False, stop=True)
            pe.matmul(ps[:, 7, 2 * NE:3 * NE], ones[:], sel[:, 0], start=True, stop=False)
            pe.matmul(ps[:, 7, 2 * NE:3 * NE], ones[:], sel[:, 1], start=False, stop=True).then_inc(s["rank_ps"], 1)
            def gather(turn, first):
                pe.wait_ge(s["hot_ok"], turn)
                for b, k0 in ((5, 0), (7, KT // 2)):
                    for k in range(k0, k0 + KT // 2):
                        for m in range(MT):
                            mm = pe.matmul(ps[:, b, (k - k0) * P:(k - k0 + 1) * P], x_tok[:, m, k * P:(k + 1) * P],
                                           pg[:, m, :], start=m == 0, stop=m == MT - 1)
                    mm.then_inc(s["gath_ps"], 1)

            def expert_pe(turn):
                pe.wait_ge(s["xe_lo"], 2 * turn)

                def before_down():
                    pe.wait_ge(s["acc_ok"], 2 * turn)

                def before_last():
                    for m in range(MT):
                        mm = pe.transpose(ps[:, 2, m * P:(m + 1) * P], pgc[:, m, :], ident[:])
                    mm.then_inc(s["scat_ps"], 1)
                    gather(turn + 1, False)

                swiglu_pe(pe, turn, [0], False, before_down, before_last)
                pe.wait_ge(s["scat_sb"], turn)
                pe.wait_ge(s["ysb_ok"], turn)
                for m, b0 in ((0, 2), (1, 0)):
                    for b in range(2):
                        mm = pe.matmul(bank(b0 + b), scat[:, m * P:(m + 1) * P], ysb[:, b * 512:(b + 1) * 512],
                                       start=True, stop=True)
                    mm.then_inc(s["put_ps"], 1)

            pe.wait_ge(s["route_ok"], 1)
            gather(1, True)
            with pe.Fori(1, 1 + NE) as turn:
                expert_pe(turn)
            n_over = pe.value_load(over_i[0:1, 0:1], min_val=0, max_val=NOV)
            with pe.Fori(0, NOV) as i:
                with pe.If(i < n_over):
                    expert_pe(i + (1 + NE))

        def copy_y(act, k):
            act.wait_ge(s["yt_ps"], k + 1)
            act.copy(xT[:, k, :].rearrange("z (n i) -> z i n", i=L),
                     ps[:, k % 2, 0:SEQ].rearrange("z (i n) -> z i n", i=L)).then_inc(s["yt_sb"], 1)

        @block.scalar
        def _(act):
            def s5_tables_act(k, first):
                if not first:
                    act.wait_ge(s["w1_out"], 16 * k)
                for t in range(4):
                    act.wait_ge(s["w1t_ps"], 4 * k + t + 1)
                    act.copy(w1[:, 4 * t:4 * t + 4].rearrange("z a b -> z (a b)"), bank(t)).then_inc(s["w1_sb"], 1)

            s5_tables_act(0, True)
            with act.Fori(1, KT) as k:
                s5_tables_act(k, False)

            def copy_xT(turn):
                for t in range(4):
                    m, half = t // 2, t % 2
                    act.wait_ge(s["xT_ps"], 4 * turn + t + 1)
                    act.copy(xh[:, m, 4 * half:4 * half + 4, :] if turn == 1 else
                             xT[:, 4 * half:4 * half + 4, m * P:(m + 1) * P],
                             ps[:, 6 + t % 2, :].rearrange("z (a b) -> z a b", a=4)).then_inc(s["xT_sb"], 1)

            copy_xT(0)
            act.wait_ge(s["a_done"], 1)
            for m in range(MT):
                for n in range(4):
                    act.wait_ge(s["proj_ps"], 4 * m + n + 1)
                    act.copy(hsb[:, m, n * PROJ_N:(n + 1) * PROJ_N], bank(4 * m + n, PROJ_N)).then_inc(s["proj_sb"], 1)
            act.wait_ge(s["proj_sb"], 8)
            for m in range(MT):
                act.activation(hsb[:, m, U0:IN_W], hsb[:, m, U0:IN_W], ACT.Gelu_apprx_tanh).then_inc(s["gelu_ok"], 1)
            act.wait_ge(s["qkT_ps"], 1)
            for j in range(2):
                act.copy(qT[:, 2 * j:2 * j + 2].rearrange("z a b -> z (a b)"), bank(j)).then_inc(s["qkT_sb"], 1)
            act.copy(kT.rearrange("z a b -> z (a b)"), bank(2)).then_inc(s["qkT_sb"], 1)
            act.wait_ge(s["mx_ok"], 1)
            for hd in range(HQ):
                for m in range(MT):
                    act.activation(pr_[:, hd, m, :], pr_[:, hd, m, :], ACT.Exp, bias=den[:, 0, 2 * hd + m:2 * hd + m + 1],
                                   accum_out=den[:, 1, 2 * hd + m:2 * hd + m + 1]).then_inc(s["exp_ok"], 1)
            act.activation(den[:, 2, :], den[:, 2, :], ACT.Exp).then_inc(s["exp_ok"], 1)
            act.wait_ge(s["ln_var"], 1)
            act.activation(gst[:, 2, :], gst[:, 2, :], ACT.Sqrt).then_inc(s["ln_std"], 1)
            for hd in range(HQ):
                act.wait_ge(s["pT_ps"], hd + 1)
                act.copy(pT[:, hd].rearrange("z a b -> z (a b)"), bank(2 + hd % 4)).then_inc(s["pT_sb"], 1)
            act.wait_ge(s["bT_ps"], 1)
            for j in range(2):
                act.copy(mixT[:, 4 + 2 * j:6 + 2 * j].rearrange("z a b -> z (a b)"), bank(j)).then_inc(s["attn_ok"], 1)
            act.wait_ge(s["pv_ps"], 1)
            for j in range(2):
                act.copy(mixT[:, 2 * j:2 * j + 2].rearrange("z a b -> z (a b)"), bank(6 + j)).then_inc(s["attn_ok"], 1)

            def norm_sqrt(n):
                for m in range(MT):
                    act.wait_ge(s["ln_var"], 1 + 2 * n + m + 1)
                    act.activation(ln_s[:, m, 1:2], ln_s[:, m, 0:1], ACT.Sqrt).then_inc(s["ln_std"], 1)

            norm_sqrt(0)
            copy_xT(1)
            swiglu_act(act, 0, range(MT), True, 0, lambda i: 16 * (i // R + 1))
            norm_sqrt(1)
            for k in range(KT):
                act.wait_ge(s["uT_ps"], k + 1)
                act.copy(U[:, 8 * k:8 * k + 8].rearrange("z a b -> z (a b)"), ps[:, 4 + k % 2, 0:8 * NC]).then_inc(s["u_sb"], 1)
            for k in range(KT):
                act.wait_ge(s["wk_used"], k + 1)
                for d in range(2):
                    src = ps[:, 6 + k % 2, d * 256:(d + 1) * 256].rearrange("z (r p n) -> z n r p", r=2, p=PR)
                    act.copy(S[:, d, 1 - d:NC + 1 - d, :, k * PR:(k + 1) * PR], src).then_inc(s["s_sb"], 1)
            for k in range(KT):
                act.wait_ge(s["y_ps"], k + 1)
                if k >= 2:
                    act.wait_ge(s["yt_ps"], k - 1)
                elif k == 0:
                    act.wait_ge(s["uT_ps"], KT)
                for q in range(4):
                    src = ps[32 * q:32 * q + 32, 4 + k % 2, 0:2 * P].rearrange("z (h i c) -> z i h c", h=2, i=L)
                    dst = yk[0:NC, k % 2].rearrange("z i (h q c) -> z i h q c", h=2, q=4)[:, :, :, q, :]
                    act.activation(dst, src, ACT.Gelu_apprx_tanh).then_inc(s["y_g"], 1)
                if k >= 1:
                    copy_y(act, k - 1)
            copy_y(act, KT - 1)
            for c in range(GLU_CH):
                for m in range(MT):
                    act.wait_ge(s["glu_ps"], 2 * c + m + 1)
                    if c:
                        act.wait_ge(s["glu_z"], 2 * c - 1 + m)
                    act.activation(sg[:, m, :], ps[:, m, FC:2 * FC], ACT.Sigmoid).then_inc(s["glu_sig"], 1)
            norm_sqrt(2)
            copy_xT(2)
            act.wait_ge(s["rt_ps"], 2)
            act.activation(rt[:, :, 1:2], rt[:, :, 0:1], ACT.Exp).then_inc(s["rt_ps"], 1)
            def xe_high(turn):
                for x, b in enumerate((5, 7)):
                    act.wait_ge(s["gath_ps"], 2 * turn + (x - 1))
                    act.copy(xh[:, 0, x * KT // 2:(x + 1) * KT // 2].rearrange("z k n -> z (k n)"),
                             bank(b)).then_inc(s["xe_hi"], 1)

            def expert_act(turn):
                swiglu_act(act, turn, [0], False, MOE_ITEM0,
                           lambda i: turn * (16 * ITEMS // R) + 16 * ((MOE_ITEM0 + i) // R + 1 - ITEMS // R))
                act.wait_ge(s["scat_ps"], turn)
                act.copy(scat, ps[:, 2, 0:2 * P]).then_inc(s["scat_sb"], 1)
                xe_high(turn + 1)
                act.wait_ge(s["down_ok"], (turn + 1) * NCH)
                act.copy(ysb.rearrange("z (b n) -> z b n", b=2), ps[:, 0:2, :]).then_inc(s["ysb_ok"], 1)

            act.wait_ge(s["route_ok"], 1)
            xe_high(1)
            with act.Fori(1, 1 + NE) as turn:
                expert_act(turn)
            n_over = act.value_load(over_i[0:1, 0:1], min_val=0, max_val=NOV)
            with act.Fori(0, NOV) as i:
                with act.If(i < n_over):
                    expert_act(i + (1 + NE))
            norm_sqrt(3)

        @block.vector
        def _(dve):
            step = Steps(dve, s["dve_step"])

            def tt(o, x, y, op):
                step(dve.tensor_tensor(o, x, y, op))

            def ts(o, x, s1, s2, op0, op1=None):
                step(dve.tensor_scalar(o, x, s1, s2, op0, op1) if op1 is not None
                     else dve.tensor_scalar(o, x, s1, None, op0))

            def stt(o, x, sc, y, op0, op1):
                step(dve.scalar_tensor_tensor(o, x, sc, y, op0, op1))

            MUL, ADD, SUB_ = ALU.mult, ALU.add, ALU.subtract

            free = iter(range(24))

            def small():
                return sm[:, next(free), :]

            q0, q1, q2, q3 = small(), small(), small(), small()

            def exp_parts(x, e, em1):
                ts(q0, x, -200.0, 200.0, ALU.max, ALU.min)
                ts(q1, q0, 1.0 / math.log(2.0), MAGIC, MUL, ADD)
                ts(q1, q1, MAGIC, None, SUB_)
                stt(q0, q1, -0.693359375, q0, MUL, ADD)
                stt(q0, q1, 2.12194440e-4, q0, MUL, ADD)
                ts(q2, q0, 1.0 / math.factorial(9), None, MUL)
                for n in range(8, 0, -1):
                    stt(q2, q2, 1.0 / math.factorial(n), q0, ADD, MUL)
                ts(q1, q1, 127.0, 0.0, ADD, ALU.max)
                step(dve.tensor_scalar(pw_i[:], q1, 255.0, None, ALU.min))
                step(dve.tensor_scalar(pw_i[:], pw_i[:], 23, None, ALU.logical_shift_left))
                pw = pw_i[:].bitcast(F32)
                stt(e, q2, 1.0, pw, ADD, MUL)
                if em1 is not None:
                    ts(q3, pw, -1.0, None, ADD)
                    tt(q0, q2, pw, MUL)
                    tt(em1, q0, q3, ADD)

            dve.wait_ge(s["lamdt_in"], 16)
            l_re, l_im, l_dt = lamdt[:, 0, :], lamdt[:, 1, :], lamdt[:, 2, :]
            dt_, la, lb, ea, em = small(), small(), small(), small(), small()
            exp_parts(l_dt, dt_, None)
            tt(la, l_re, dt_, MUL)
            tt(lb, l_im, dt_, MUL)
            exp_parts(la, ea, em)
            hh, h2, sh, ch, sb, oc = small(), small(), small(), small(), small(), small()
            ts(q0, lb, 1.0 / (2 * math.pi), MAGIC, MUL, ADD)
            ts(q0, q0, MAGIC, None, SUB_)
            stt(hh, q0, -6.28125, lb, MUL, ADD)
            stt(hh, q0, -1.93500518798828125e-3, hh, MUL, ADD)
            stt(hh, q0, -3.0199159819e-7, hh, MUL, ADD)
            ts(hh, hh, 0.5, None, MUL)
            tt(h2, hh, hh, MUL)
            f = math.factorial
            ts(sh, h2, 1.0 / f(13), None, MUL)
            for n, sign in ((11, -1), (9, 1), (7, -1), (5, 1), (3, -1)):
                stt(sh, sh, sign / f(n), h2, ADD, MUL)
            stt(sh, sh, 1.0, hh, ADD, MUL)
            ts(ch, h2, 1.0 / f(14) * -1, None, MUL)
            for n, sign in ((12, 1), (10, -1), (8, 1), (6, -1), (4, 1), (2, -1)):
                stt(ch, ch, sign / f(n), h2, ADD, MUL)
            ts(ch, ch, 1.0, None, ADD)
            stt(sb, sh, 2.0, ch, MUL, MUL)
            stt(oc, sh, 2.0, sh, MUL, MUL)
            br, bi, mr = small(), small(), small()
            tt(q0, ea, oc, MUL)
            tt(br, ea, q0, SUB_)
            tt(mr, em, q0, SUB_)
            tt(bi, ea, sb, MUL)
            cr, ci, nn = small(), small(), small()
            tt(q0, l_re, l_re, MUL)
            tt(q1, l_im, l_im, MUL)
            tt(q0, q0, q1, ADD)
            step(dve.reciprocal(nn, q0))
            tt(q0, mr, l_re, MUL)
            tt(q1, bi, l_im, MUL)
            tt(q0, q0, q1, ADD)
            tt(cr, q0, nn, MUL)
            tt(q0, bi, l_re, MUL)
            tt(q1, mr, l_im, MUL)
            tt(q0, q0, q1, SUB_)
            tt(ci, q0, nn, MUL)
            step(dve.memset(pa[:, 0, :, 0:1], 1.0))
            step(dve.memset(pa[:, 1, :, 0:1], 0.0))
            step(dve.tensor_copy(pa[:, 0, :, 1:2], br.unsqueeze(2)))
            step(dve.tensor_copy(pa[:, 1, :, 1:2], bi.unsqueeze(2)))
            for lo, n in ((1, 1), (2, 2), (4, 4)):
                sr, si = (pa[:, x, :, 1:1 + n] for x in (0, 1))
                mr_, mi_ = (pa[:, x, :, n:n + 1].to_broadcast([P, NT, n]) for x in (0, 1))
                dr, di = (pa[:, x, :, n + 1:2 * n + 1] for x in (0, 1))
                fa = ta.rearrange("z a b c -> z (a b c)")[:, 0:NT * n].rearrange("z (a b) -> z a b", b=n)
                fb = tb.rearrange("z a b c -> z (a b c)")[:, 0:NT * n].rearrange("z (a b) -> z a b", b=n)
                tt(fa, sr, mr_, MUL)
                tt(fb, si, mi_, MUL)
                tt(dr, fa, fb, SUB_)
                tt(fa, sr, mi_, MUL)
                tt(fb, si, mr_, MUL)
                tt(di, fa, fb, ADD)
            pav = pa.rearrange("z r (k d p) l -> z r k d p l", k=KT, d=2)
            for d in range(2):
                a8v = a8[:, d].rearrange("z a b (k p) -> z a b k p", k=KT)
                for o, i, x, sgn in ((0, 0, 0, 1.0), (0, 1, 1, -1.0), (1, 0, 1, 1.0), (1, 1, 0, 1.0)):
                    ts(a8v[:, o, i], pav[:, x, :, d, :, L], sgn, None, MUL)
            for x in range(2):
                for i in range(L + 1):
                    step(dve.tensor_copy(p2[:, x, :, 0, :, i], pav[:, x, :, 0, :, i]))
                    step(dve.tensor_copy(p2[:, x, :, 1, :, i], pav[:, x, :, 1, :, L - i]))
                for i in range(L):
                    step(dve.tensor_copy(p1[:, x, :, 0, :, i], pav[:, x, :, 0, :, L - 1 - i]))
                    step(dve.tensor_copy(p1[:, x, :, 1, :, i], pav[:, x, :, 1, :, i]))
            dve.wait_ge(s["s5_in"], 64)
            cflat = [c.rearrange("z x a b c d -> z x (a b c) d") for c in (Cp, Cq)]
            fa = ta.rearrange("z a b c -> z (a b c)")[:, 0:NT * CG].rearrange("z (a b) -> z a b", b=CG)
            fb = tb.rearrange("z a b c -> z (a b c)")[:, 0:NT * CG].rearrange("z (a b) -> z a b", b=CG)
            crb, cib = (v.unsqueeze(2).to_broadcast([P, NT, CG]) for v in (cr, ci))
            tt(fa, cflat[0][:, 0], crb, MUL)
            tt(fb, cflat[0][:, 1], cib, MUL)
            tt(cflat[1][:, 0], fa, fb, SUB_)
            tt(fa, cflat[0][:, 0], cib, MUL)
            tt(fb, cflat[0][:, 1], crb, MUL)
            tt(cflat[1][:, 1], fa, fb, ADD)
            step(dve.memset(Bz.rearrange("z a b c d -> z (a b c d)"), 0.0))
            for k in range(KT):
                ts(Dd[:, k, :], eye16, Dp[:, k:k + 1], None, MUL)

            def ksel(v, x, k, n):
                return v[:, x, bass.ds(k, 1)].rearrange("z o d p n -> z (o d p) n")

            def s5_tables_dve(k, first):
                C_, P_, B_, Q_ = ([ksel(v, x, k, 0) for x in (0, 1)] for v in (Cq, p2, Bp, p1))
                cb = [v.unsqueeze(2).to_broadcast([P, 2 * PR, L + 1, CG]) for v in C_]
                pb = [v.unsqueeze(3).to_broadcast([P, 2 * PR, L + 1, CG]) for v in P_]
                tt(ta, cb[0], pb[0], MUL)
                tt(tb, cb[1], pb[1], MUL)
                if not first:
                    dve.wait_ge(s["s5_free"], 16 * k)
                    dve.wait_ge(s["kgen_ps"], k)
                tt(w2[:, 0], ta, tb, SUB_)
                tt(ta, cb[0], pb[1], MUL)
                tt(tb, cb[1], pb[0], MUL)
                flat = lambda v: v.rearrange("z a b c -> z (a b c)")
                stt(flat(w2[:, 1]), flat(ta), -1.0, flat(tb), MUL, SUB_)
                dve.sem_inc(s["s5_w2"], 1)
                for x in range(2):
                    for g2 in range(2):
                        step(dve.tensor_copy(Bz[64 * g2:64 * g2 + 64, x, :, g2, :], B_[x][64 * g2:64 * g2 + 64]))
                dve.sem_inc(s["s5_bz"], 1)
                bb = [v.unsqueeze(2).to_broadcast([P, 2 * PR, L, CG]) for v in B_]
                qb = [v.unsqueeze(3).to_broadcast([P, 2 * PR, L, CG]) for v in Q_]
                va, vb = ta[:, :, 0:L, :], tb[:, :, 0:L, :]
                tt(va, bb[0], qb[0], MUL)
                tt(vb, bb[1], qb[1], MUL)
                if not first:
                    dve.wait_ge(s["w1t_ps"], 4 * k)
                tt(w1t[:, 0], va, vb, SUB_)
                tt(va, bb[0], qb[1], MUL)
                tt(vb, bb[1], qb[0], MUL)
                tt(w1t[:, 1], va, vb, ADD)
                dve.sem_inc(s["s5_w1t"], 1)
                dve.wait_ge(s["kgen_ps"], k + 1)
                if not first:
                    dve.wait_ge(s["kx_out"], 16 * k)
                kf = ps[:, 4, 0:P].rearrange("z (l c) -> z l c", c=CG)
                kb = ps[:, 5, 0:P].rearrange("z (l c) -> z l c", c=CG)
                step(dve.tensor_copy(kext[:, 0:L], kb))
                step(dve.tensor_copy(kext[:, L:2 * L - 1], kf[:, 1:L]))
                tt(kext[:, L - 1], kf[:, 0], kext[:, L - 1], ADD)
                step(dve.tensor_tensor(kext[:, L - 1], kext[:, L - 1],
                                       Dd[:, bass.ds(k, 1)].rearrange("z o c -> z (o c)"), ADD))
                dve.sem_inc(s["s5_kx"], 1)
                dve.sem_inc(s["kext_sb"], 1)

            before = step.n
            s5_tables_dve(0, True)
            per_turn = step.n - before
            with dve.Fori(1, KT) as k:
                step.loop(k - 1, per_turn)
                s5_tables_dve(k, False)
            step.end_loop(KT - 1)
            for n, v in (("s5_free", 16 * KT), ("w1_out", 16 * KT), ("kx_out", 16 * KT), ("w1t_ps", 4 * KT)):
                dve.wait_ge(s[n], v)
            dve.sem_inc(s["a_done"], 1)

            dve.wait_ge(s["const_in"], 96)
            dve.wait_ge(s["proj_sb"], 8)
            for m in range(MT):
                src = hsb[:, m, 0:QK].rearrange("z (h a b) -> z h a b", a=2, b=HD // 2)
                c_, s_ = (cs[:, m, x, :].unsqueeze(1).to_broadcast([P, HQ + HKV, HD // 2]) for x in (0, 1))
                x1, x2 = src[:, :, 0, :], src[:, :, 1, :]
                ra, rb = rtmp[:, 0], rtmp[:, 1]
                tt(ra, x1, c_, MUL)
                tt(rb, x2, s_, MUL)
                tt(qkr[:, m, :, 0, :], ra, rb, SUB_)
                tt(ra, x2, c_, MUL)
                tt(rb, x1, s_, MUL)
                tt(qkr[:, m, :, 1, :], ra, rb, ADD)
                kk = qkr[:, m, HQ:HQ + HKV].rearrange("z h a b -> z h (a b)")
                for x in range(2):
                    step(dve.tensor_copy(kd[:, m, :, x, :], kk))
                dve.sem_inc(s["rope_ok"], 1)
            dve.wait_ge(s["gelu_ok"], 2)
            vv = [hsb[:, m, Z0:IN_W].rearrange("z (g d) -> z g d", g=G) for m in range(MT)]
            sq = gsq.rearrange("z (m g d) -> z m g d", m=MT, g=G)
            mean, var, std = (gst[:, x, :] for x in (0, 1, 2))
            rs = gst[:, 3, :]
            for m in range(MT):
                step(dve.tensor_reduce(mean[:, m * G:(m + 1) * G], vv[m], AX.X, ADD))
            ts(mean, mean, 1.0 / HD, None, MUL)
            for m in range(MT):
                tt(vv[m], vv[m], mean[:, m * G:(m + 1) * G].unsqueeze(2).to_broadcast([P, G, HD]), SUB_)
                tt(sq[:, m], vv[m], vv[m], MUL)
                step(dve.tensor_reduce(var[:, m * G:(m + 1) * G], sq[:, m], AX.X, ADD))
            ts(var, var, 1.0 / HD, EPS, MUL, ADD)
            step(dve.tensor_copy(std, var))
            dve.sem_inc(s["ln_var"], 1)
            for hd in range(HQ):
                dve.wait_ge(s["sc_ps"], hd + 1)
                step(dve.scalar_tensor_tensor(pr_[:, hd].rearrange("z a b -> z (a b)"), bank(hd), HD ** -0.5,
                                              mask.rearrange("z a b -> z (a b)"), MUL, ADD))
                dve.sem_inc(s["sc_sb"], 1)
            step(dve.tensor_reduce(mxs.rearrange("z a b -> z (a b)"), pr_.rearrange("z a b c -> z (a b) c"), AX.X, ALU.max))
            sinkb = sink.unsqueeze(2).to_broadcast([P, HQ, MT])
            tt(mxs, mxs, sinkb, ALU.max)
            ts(den[:, 0, :], mxs.rearrange("z a b -> z (a b)"), -1.0, None, MUL)
            tt(den[:, 2, :].rearrange("z (a b) -> z a b", b=MT), sinkb, mxs, SUB_)
            dve.sem_inc(s["mx_ok"], 1)
            dve.wait_ge(s["ln_std"], 1)

            def refine(rs_, std_, var_, t_):
                step(dve.reciprocal(rs_, std_))
                tt(t_, rs_, rs_, MUL)
                tt(t_, t_, var_, MUL)
                ts(t_, t_, -0.5, 1.5, MUL, ADD)
                tt(rs_, rs_, t_, MUL)

            refine(rs, std, var, mean)
            for m in range(MT):
                tt(vv[m], vv[m], rs[:, m * G:(m + 1) * G].unsqueeze(2).to_broadcast([P, G, HD]), MUL)
                fv = hsb[:, m, Z0:IN_W]
                tt(fv, fv, sgln[:, 0, :], MUL)
                tt(fv, fv, sgln[:, 1, :], ADD)
            dve.sem_inc(s["vn_ok"], 1)
            dve.wait_ge(s["exp_ok"], 2 * HQ + 1)
            tt(den[:, 3, :], den[:, 1, :], den[:, 2, :], ADD)
            step(dve.reciprocal(den[:, 1, :], den[:, 3, :]))
            pf = pr_.rearrange("z a b c -> z (a b) c")
            tt(pf, pf, den[:, 1, :].unsqueeze(2).to_broadcast([P, HQ * MT, SEQ]), MUL)
            dve.sem_inc(s["p_ok"], 1)
            dve.wait_ge(s["sv_ps"], 1)
            for g in range(G):
                step(dve.scalar_tensor_tensor(
                    bout[:, :, g * HD:(g + 1) * HD],
                    ps[:, g // 4, (g % 4) * P:(g % 4 + 1) * P].rearrange("z (m d) -> z m d", m=MT), sgub[:, g:g + 1],
                    hsb[:, :, U0 + g * HD:U0 + (g + 1) * HD], ADD, MUL))
            dve.sem_inc(s["bo_ok"], 1)

            def norm(n, add_rest):
                for m in range(MT):
                    add_rest(m)
                    for x in range(2):
                        step(dve.bn_stats(stats[:, m, x, :], res[:, m, x * 512:(x + 1) * 512]))
                    step(dve.bn_aggr(mv[:, m, :], stats[:, m].rearrange("z a b -> z (a b)")))
                    ts(ln_s[:, m, 0:1], mv[:, m, 1:2], EPS, None, ADD)
                    dve.sem_inc(s["ln_var"], 1)
                for m in range(MT):
                    dve.wait_ge(s["ln_std"], 1 + 2 * n + m + 1)
                    refine(ln_s[:, m, 2:3], ln_s[:, m, 1:2], ln_s[:, m, 0:1], ln_s[:, m, 3:4])
                    dve.wait_ge(s["ln_p"], 32 * (n + 1))
                    ts(res[:, m], res[:, m], mv[:, m, 0:1], ln_s[:, m, 2:3], SUB_, MUL)
                    tt(res[:, m], res[:, m], lnp[:, 0], MUL)
                    step(dve.tensor_tensor(x_tok[:, m], res[:, m], lnp[:, 1], ADD))
                    dve.sem_inc(s["ln_out"], 1)

            def rest_of(sem_name, count):
                def add(m):
                    if m == 0 or sem_name == "op_ps":
                        dve.wait_ge(s[sem_name], count(m))
                    for n in range(2):
                        stt(res[:, m, n * 512:(n + 1) * 512], x_tok[:, m, n * 512:(n + 1) * 512], ALPHA,
                            bank(2 * m + n), MUL, ADD)
                return add

            dve.wait_ge(s["xT_ps"], 4)
            norm(0, rest_of("op_ps", lambda m: m + 1))
            def low_of(o, src, hi):
                return dve.tensor_tensor(o, src, hi.bitcast(F32), SUB_)

            for t in range(4):
                m, half = t // 2, t % 2
                dve.wait_ge(s["xT_sb"], 4 + t + 1)
                low_of(xl_[:, m, 4 * half:4 * half + 4, :].rearrange("z k n -> z (k n)"), bank(6 + t % 2),
                       xh[:, m, 4 * half:4 * half + 4, :].rearrange("z k n -> z (k n)")).then_inc(s["x1_lo"], 1)
            swiglu_dve(dve, 0, range(MT), True, 0)
            norm(1, rest_of("down_ok", lambda m: NCH))
            for x in range(2):
                dve.wait_ge(s[f"xk_in{x}"], 64)
                step(dve.tensor_copy(xg[:, x], xl[:, x].rearrange("z j (g c) -> z g j c", c=CG)))
                dve.sem_inc(s["xg_ok"], 1)
            step(dve.memset(Sz.rearrange("z a b c d e -> z (a b c d e)"), 0.0))
            step(dve.memset(S[:, 0, 0].rearrange("z a b -> z (a b)"), 0.0))
            step(dve.memset(S[:, 1, NC].rearrange("z a b -> z (a b)"), 0.0))
            dve.wait_ge(s["s_sb"], 2 * KT)
            T2 = KT * PR
            for i in range(1, NC):
                for d in range(2):
                    cur, prv = (i + 1, i) if d == 0 else (NC - 1 - i, NC - i)
                    pd = prod[:, d * 4 * T2:(d + 1) * 4 * T2].rearrange("z (o i t) -> z o i t", o=2, i=2)
                    tt(pd, a8[:, d], S[:, d, prv].unsqueeze(1).to_broadcast([P, 2, 2, T2]), MUL)
                    tt(S[:, d, cur], S[:, d, cur], pd[:, :, 0], ADD)
                    tt(S[:, d, cur], S[:, d, cur], pd[:, :, 1], ADD)
            for d in range(2):
                for ri in range(2):
                    for g2 in range(2):
                        src = S[64 * g2:64 * g2 + 64, d, d:NC + d, ri, :].rearrange("z n t -> z t n")
                        step(dve.tensor_copy(Sz[64 * g2:64 * g2 + 64, d, ri, :, g2, :], src))
                        dve.sem_inc(s["sz_ok"], 1)

            for c in range(GLU_CH):
                for m in range(MT):
                    dve.wait_ge(s["glu_sig"], 2 * c + m + 1)
                    if c == 0 and m == 0:
                        dve.wait_ge(s["yt_ps"], KT)
                    col = slice(c * FC, (c + 1) * FC)
                    step(dve.tensor_tensor(h[:, m, :], sg[:, m, :], ps[:, m, 0:FC], MUL))
                    dve.sem_inc(s["glu_z"], 1)
                    stt(res[:, m, col], x_tok[:, m, col], ALPHA, h[:, m, :], MUL, ADD)
            norm(2, lambda m: None)
            dve.wait_ge(s["rt_ps"], 1)
            lg, mx8 = rt[:, :, 8:16], rt[:, :, 16:24]
            tpf, m1, m2 = rt[:, :, 24:32], rt[:, :, 32:40], rt[:, :, 40:48]
            step(dve.tensor_copy(lg, ps[:, 5, 0:16].rearrange("z (m e) -> z m e", m=MT)))
            for m in range(MT):
                step(dve.max(mx8[:, m], lg[:, m]))
                step(dve.max_index(top_i[:, m], mx8[:, m], lg[:, m]))
                step(dve.tensor_copy(tpf[:, m], top_i[:, m]))
            tt(rt[:, :, 0:1], rt[:, :, 17:18], rt[:, :, 16:17], SUB_)
            dve.sem_inc(s["rt_ps"], 1)
            dve.wait_ge(s["rt_ps"], 3)
            ts(rt[:, :, 2:3], rt[:, :, 1:2], 1.0, None, ADD)
            step(dve.reciprocal(rt[:, :, 3:4], rt[:, :, 2:3]))
            tt(rt[:, :, 4:5], rt[:, :, 1:2], rt[:, :, 3:4], MUL)
            for m in range(MT):
                ts(m1[:, m], iota8[:], tpf[:, m, 0:1], None, ALU.is_equal)
                ts(m2[:, m], iota8[:], tpf[:, m, 1:2], None, ALU.is_equal)
                tt(sel[:, m], m1[:, m], m2[:, m], ADD)
            step(dve.memset(ones[:], 1.0))
            dve.sem_inc(s["sel_ok"], 1)
            for m in range(MT):
                ts(m1[:, m], m1[:, m], rt[:, m, 3:4], None, MUL)
                stt(comb[:, m], m2[:, m], rt[:, m, 4:5], m1[:, m], MUL, ADD)
            for v in (posx, selx, combx):
                step(dve.memset(v[:], 0.0))
            step(dve.tensor_copy(selx[:, :, 1:1 + NE], sel[:]))
            step(dve.tensor_copy(combx[:, :, 1:1 + NE], comb[:]))
            dve.wait_ge(s["rank_ps"], 1)
            pos = rt[:, :, 48:56]
            step(dve.tensor_copy(pos, ps[:, 7, 0:2 * NE].rearrange("z (m e) -> z m e", m=MT)))
            step(dve.tensor_copy(posx[:, :, 1:1 + NE], pos))
            cnt, rank, hot, tmp = (over[:, x, :] for x in range(4))
            ts(cnt, ps[:, 7, 2 * NE:3 * NE], float(P), None, ALU.is_gt)
            step(dve.memset(rank, 0.0))
            for e in range(1, NE):
                tt(rank[:, e:e + 1], rank[:, e - 1:e], cnt[:, e - 1:e], ADD)
            nf = over[:, 4, :]
            tt(nf[:, 0:1], rank[:, NE - 1:NE], cnt[:, NE - 1:NE], ADD)
            for i in range(NOV):
                stt(hot, rank, float(i), cnt, ALU.is_equal, MUL)
                tt(tmp, hot, iota8[:], MUL)
                step(dve.tensor_reduce(nf[:, 1 + i:2 + i], tmp, AX.X, ADD))
                for dst, src in ((posx, pos), (selx, sel[:]), (combx, comb[:])):
                    tt(m1, src, hot.unsqueeze(1).to_broadcast([P, MT, NE]), MUL)
                    step(dve.tensor_reduce(dst[:, :, 1 + NE + i:2 + NE + i], m1, AX.X, ADD))
            ts(posx[:, :, 1 + NE:TURNS], posx[:, :, 1 + NE:TURNS], -float(P), None, ADD)
            step(dve.tensor_copy(over_i[:], nf[:, 0:4]))

            def tokens_hot(turn):
                for m in range(MT):
                    at = bass.ds(turn, 1)
                    ins = dve.tensor_scalar(pg[:, m, :], iotaP[:], posx[:, m, at], selx[:, m, at],
                                            ALU.is_equal, MUL)
                ins.then_inc(s["hot_ok"], 1)

            def expert_dve(turn):
                def between():
                    at = bass.ds(turn, 1)
                    for m in range(MT):
                        dve.tensor_scalar(pgc[:, m, :], iotaP[:], posx[:, m, at], combx[:, m, at],
                                          ALU.is_equal, MUL)
                    dve.wait_ge(s["gath_ps"], 2 * turn)
                    tokens_hot(turn + 1)

                swiglu_dve(dve, turn, [0], False, MOE_ITEM0, between)
                for x, b in enumerate((5, 7)):
                    dve.wait_ge(s["xe_hi"], 2 * turn + (1 + x))
                    low_of(xl_[:, 0, x * KT // 2:(x + 1) * KT // 2].rearrange("z k n -> z (k n)"), bank(b),
                           xh[:, 0, x * KT // 2:(x + 1) * KT // 2].rearrange("z k n -> z (k n)")
                           ).then_inc(s["xe_lo"], 1)
                for m, b0 in ((0, 2), (1, 0)):
                    dve.wait_ge(s["put_ps"], 2 * turn + (m - 1))
                    dve.wait_ge(s["acc_ok"], 2 * turn + m)
                    dve.tensor_tensor(res[:, m].rearrange("z (b n) -> z b n", b=2), ps[:, b0:b0 + 2, :],
                                      res[:, m].rearrange("z (b n) -> z b n", b=2), ADD).then_inc(s["acc_ok"], 1)

            ts(res[:, 0], x_tok[:, 0], ALPHA, None, MUL)
            ts(res[:, 1], x_tok[:, 1], ALPHA, None, MUL)
            dve.sem_inc(s["acc_ok"], 2)
            tokens_hot(1)
            dve.wait_ge(s["hot_ok"], 1)
            dve.sem_inc(s["route_ok"], 1)
            for x, b in enumerate((5, 7)):
                dve.wait_ge(s["xe_hi"], 1 + x)
                low_of(xl_[:, 0, x * KT // 2:(x + 1) * KT // 2].rearrange("z k n -> z (k n)"), bank(b),
                       xh[:, 0, x * KT // 2:(x + 1) * KT // 2].rearrange("z k n -> z (k n)")).then_inc(s["xe_lo"], 1)
            with dve.Fori(1, 1 + NE) as turn:
                expert_dve(turn)
            n_over = dve.value_load(over_i[0:1, 0:1], min_val=0, max_val=NOV)
            with dve.Fori(0, NOV) as i:
                with dve.If(i < n_over):
                    expert_dve(i + (1 + NE))
            norm(3, lambda m: None)
            dve.sem_inc(s["fin"], 2)


def layouts(inp):
    g = {k: np.asarray(v) for k, v in inp.items()}
    c = np.ascontiguousarray

    def by_k(w):
        return c(w.reshape(-1, P, w.shape[1]).transpose(1, 0, 2).reshape(P, -1))

    def swiglu_chunks(wg, wu, wd):
        e = wg.shape[0]
        gu = np.stack([w.reshape(e, KT, P, NCH, FC) for w in (wg, wu)], axis=4)
        gu = gu.reshape(e, 2, KT // 2, P, NCH, 2, FC).transpose(0, 4, 1, 3, 2, 5, 6).reshape(e, NCH, 2, P, ITEM)
        dn = wd.reshape(e, NCH, 1, SUB, P, D).transpose(0, 1, 2, 4, 3, 5).reshape(e, NCH, 1, P, ITEM)
        return c(np.concatenate([gu, dn], axis=2)).reshape(e * ITEMS, P, ITEM)

    o = {"x": c(g["x"][0])}
    o["w_in"], o["w_out"] = by_k(g["mix_w_in"][0]), by_k(g["mix_w_out"][0])
    o["w_router"] = by_k(g["router_w"][0])
    o["ln_g"], o["ln_b"] = c(g["ln_g"].reshape(4, D)), c(g["ln_b"].reshape(4, D))
    o["sguT"] = c(g["sgu_w"][0].transpose(2, 0, 1).reshape(P, G * P))
    o["sgub"] = c(g["sgu_b"][0].T)
    o["sgln"] = c(np.concatenate([g["sgu_ln_g"][0].reshape(1, -1), g["sgu_ln_b"][0].reshape(1, -1)], axis=1))
    o["sink"] = c(g["attn_sink"])
    o["ffn_w"] = swiglu_chunks(g["ffn_w_gate"], g["ffn_w_up"], g["ffn_w_down"])
    o["moe_w"] = swiglu_chunks(g["moe_w_gate"][0], g["moe_w_up"][0], g["moe_w_down"][0])
    glu = np.stack([g[n][0].reshape(KT, P, GLU_CH, FC) for n in ("glu_w_val", "glu_w_gate")], axis=3)
    glu = glu.reshape(2, KT // 2, P, GLU_CH, 2, FC).transpose(3, 0, 2, 1, 4, 5)
    o["glu_w"] = c(glu).reshape(GLU_ITEMS, P, ITEM)
    def groups(w):
        return w.reshape((2, KT, PR, 2) + w.shape[2:])
    o["s5_b"] = c(np.stack([groups(g[n][0]).transpose(3, 4, 1, 0, 2, 5) for n in ("s5_b_re", "s5_b_im")], axis=2).reshape(P, -1))
    o["s5_c"] = c(np.stack([groups(g[n][0]).transpose(3, 5, 1, 0, 2, 4) for n in ("s5_c_re", "s5_c_im")], axis=2).reshape(P, -1))
    ldt = np.broadcast_to(g["s5_log_dt"][0][:, :, None], (2, 64, PS))
    o["s5_lamdt"] = c(np.stack([groups(v).transpose(3, 4, 1, 0, 2) for v in (g["s5_lam_re"][0], g["s5_lam_im"][0], ldt)], axis=2).reshape(P, 3, NT))
    o["s5_d"] = c(g["s5_d"][0].reshape(KT, P).T)
    o["ident"] = np.eye(P, dtype=np.float32)
    o["eye16"] = c(np.tile(np.eye(CG, dtype=np.float32), (8, 1)))
    o["iota8"] = c(np.tile(np.arange(NE, dtype=np.float32), (P, 1)))
    o["iotaP"] = c(np.tile(np.arange(P, dtype=np.float32), (P, 1)))
    o["tri"] = np.triu(np.ones((P, P), np.float32), 1)
    pos = np.arange(SEQ, dtype=np.float32)
    inv = (10000.0 ** (-np.arange(0, HD, 2, dtype=np.float32) / HD)).astype(np.float32)
    ang = pos[:, None] * inv[None, :]
    o["cossin"] = c(np.stack([np.cos(ang), np.sin(ang)], 1).reshape(MT, P, 2, HD // 2).transpose(1, 0, 2, 3).reshape(P, -1))
    dist = np.abs(pos[:, None] - pos[None, :])
    o["mask"] = c(np.where(dist <= 128, 0.0, NEG).astype(np.float32).reshape(MT, P, SEQ).transpose(1, 0, 2).reshape(P, -1))
    return o


def kernel(**inputs):
    import concourse.bacc as _bacc
    from concourse import bass_utils as _bu

    nc = _bacc.Bacc("TRN2", target_bir_lowering=False, num_devices=1)
    arrays = layouts(inputs)
    aps = {n: nc.dram_tensor("in_" + n, v.shape, mybir.dt.from_np(v.dtype), kind="ExternalInput").ap() for n, v in arrays.items()}
    out = nc.dram_tensor("out", (SEQ, D), F32, kind="ExternalOutput").ap()
    build(nc, aps, out)
    got = _bu.run_bass_kernel_spmd(nc, [{"in_" + n: v for n, v in arrays.items()}], core_ids=[0])
    return got.results[0]["out"].reshape(1, SEQ, D)
```

```python
import math
from contextlib import ExitStack

import numpy as np

import concourse.bass as bass
from concourse import mybir

P = 128
D = 1024
KT = D // P
SEQ = 256
MT = SEQ // P
HQ, HKV, HD = 8, 2, 64
QK = (HQ + HKV) * HD
V0 = QK
U0 = V0 + HKV * HD
Z0 = U0 + 512
IN_W = Z0 + 512
PROJ_N = IN_W // 4
G = 8
FF = 2816
FC = 256
SUB = FC // P
NCH = FF // FC
NE = 8
GLU_CH = D // FC
ITEM = KT // 2 * 2 * FC
PER = 3
ITEMS = NCH * PER
R = 11
GLU_ITEMS = GLU_CH * 2
MOE_ITEM0 = GLU_ITEMS
CHUNK_A = 2
assert CHUNK_A + KT == NCH - 1
assert ITEM == SUB * D and ITEMS % R == 0
NOV = 2 * SEQ // (P + 1)
TURNS = 1 + NE + NOV
ALPHA = (2.0 * 2) ** 0.25
EPS = 1e-5
NEG = -1e30
L, NC, CG, PS = 8, 32, 16, 64
PR = 4
NT = KT * PR * 2
HT = KT // 2 * PR
MAGIC = 1.5 * 2.0**23

F32 = mybir.dt.float32
I32 = mybir.dt.int32
F32R = mybir.dt.float32r
U32 = mybir.dt.uint32
ALU = mybir.AluOpType
ACT = mybir.ActivationFunctionType
AX = mybir.AxisListType
DEBUG = ()


class Steps:

    def __init__(self, eng, sem):
        self.eng, self.sem, self.n, self.offset = eng, sem, 0, 0

    def __call__(self, ins):
        self.n += 1
        ins.then_inc(self.sem, 1)
        self.eng.wait_ge(self.sem, self.offset + self.n)

    def passed(self, n):
        self.n += n
        self.eng.wait_ge(self.sem, self.offset + self.n)

    def loop(self, i, per_turn):
        self.start, self.per_turn = self.n, per_turn
        self.offset = i * per_turn

    def end_loop(self, turns):
        assert self.n - self.start == self.per_turn, (self.n - self.start, self.per_turn)
        self.n = self.start + self.per_turn * turns
        self.offset = 0


def build(nc, a, out):
    with ExitStack() as ctx:

        def sem(name):
            return ctx.enter_context(nc.semaphore(name))

        def sbuf(name, shape, dt=F32):
            return ctx.enter_context(nc.sbuf_tensor(name, [P] + list(shape), dt))

        S5_SLOT = 8
        ARENA = 23168
        MEM = S5_SLOT * ITEM + ARENA
        mem = sbuf("mem", [MEM])
        base = nc.sbuf_base - 4 * MEM
        ring = mem[:, 0:R * ITEM].rearrange("z (s n) -> z s n", s=R)

        def over_mem(name, at, shape):
            assert at + int(np.prod(shape)) <= MEM
            return nc.alloc_sbuf_tensor_at(name, [P] + list(shape), F32R, offset=base + 4 * at)

        wh = over_mem("wh", R * ITEM, [PER, ITEM])
        wl = over_mem("wl", R * ITEM + PER * ITEM, [PER, ITEM])
        xh = over_mem("xh", R * ITEM + 2 * PER * ITEM, [KT, P])
        xl_ = over_mem("xl", R * ITEM + 2 * PER * ITEM + KT * P, [KT, P])
        x_tok = sbuf("x_tok", [MT, D])
        xT = sbuf("xT", [KT, SEQ])
        xT_base = nc.sbuf_base - 4 * KT * SEQ
        res = sbuf("res", [MT, D])
        lnp = sbuf("lnp", [2, D])
        ident = sbuf("ident", [P])
        sg = sbuf("sg", [MT, FC])
        h = sbuf("h", [MT, FC])
        hTh = sbuf("hTh", [SUB, P], F32R)
        hTl = sbuf("hTl", [SUB, P], F32R)
        stats = sbuf("stats", [MT, 2, 6])
        mv = sbuf("mv", [MT, 2])
        ln_s = sbuf("ln_s", [MT, 4])
        a8 = sbuf("a8", [2, 2, 2, 2, HT])
        wr_sb = sbuf("wr_sb", [KT, NE])
        rt = sbuf("rt", [MT, 64])
        sel = sbuf("sel", [MT, NE])
        comb = sbuf("comb", [MT, NE])
        posx, selx, combx = (sbuf(n, [MT, TURNS + 1]) for n in ("posx", "selx", "combx"))
        over = sbuf("over", [6, NE])
        over_i = sbuf("over_i", [2 + NOV], I32)
        top_i = sbuf("top_i", [MT, 8], U32)
        iota8, iotaP = sbuf("iota8", [NE]), sbuf("iotaP", [P])
        tri, ones = sbuf("tri", [P]), sbuf("ones", [P])
        pw_i = sbuf("pw_i", [NT], I32)
        xTf = xT[:].rearrange("z a b -> z (a b)")
        pg = xTf[:, 0:2 * P].rearrange("z (m n) -> z m n", m=MT)
        pgc = xTf[:, 2 * P:4 * P].rearrange("z (m n) -> z m n", m=MT)
        scat = xTf[:, 4 * P:6 * P]
        ysb = xTf[:, 6 * P:6 * P + D]
        ps = ctx.enter_context(nc.psum_tensor("ps", [P, 8, 512], F32))

        class Region:
            def __init__(self, at=S5_SLOT * ITEM, end=MEM):
                self.at, self.end = at, end

            def __call__(self, *shape):
                n = int(np.prod(shape))
                v = mem[:, self.at:self.at + n]
                self.at += n
                assert self.at <= self.end, self.at
                names = "abcdef"[:len(shape)]
                if len(shape) > 1:
                    v = v.rearrange(f"z ({' '.join(names)}) -> z {' '.join(names)}",
                                    **{n_: s for n_, s in zip(names[1:], shape[1:])})
                return v

        WOUT0 = KT * (IN_W - D)
        r = Region(PER * ITEM, KT * IN_W)
        ta, tb = r(2 * PR, L + 1, CG), r(2 * PR, L + 1, CG)
        w1 = r(16, P)
        ffn_hTh = over_mem("ffn_hTh", r.at, [MT, SUB, P])
        ffn_hTl = over_mem("ffn_hTl", r.at + MT * FC, [MT, SUB, P])
        ffn_xl = over_mem("ffn_xl", r.at + 2 * MT * FC, [MT, KT, P])
        assert r.at + 2 * MT * FC + MT * D <= r.end
        ffn_xh = nc.alloc_sbuf_tensor_at("ffn_xh", [P, MT, KT, P], F32R, offset=xT_base)
        r = Region(KT * IN_W, S5_SLOT * ITEM)
        p2, coef = r(2, KT, 2, PR, L + 1), r(2, NT)
        P1_AT = MEM - 2 * NT * L
        p1 = Region(P1_AT)(2, KT, 2, PR, L)
        ffn_wh = over_mem("ffn_wh", S5_SLOT * ITEM, [PER, ITEM])
        ffn_wl = over_mem("ffn_wl", (S5_SLOT + PER) * ITEM, [PER, ITEM])
        r = Region((S5_SLOT + 2 * PER) * ITEM, P1_AT)
        Bp, Cp = r(2, KT, 2, PR, CG), r(2, KT, 2, PR, CG)
        w2 = r(2, 2 * PR, L + 1, CG)
        w1t = r(2, 2 * PR, L, CG)
        Bz = r(2, 2 * PR, 2, CG)
        kext = r(2 * L - 1, CG)
        Dd, Dp, eye16 = r(KT, CG), r(KT), r(CG)
        B_k, p1_k = r(2, 2 * PR, CG), r(2, 2 * PR, L)
        resf = res[:].rearrange("z a b -> z (a b)")
        tc, td = (resf[:, x * D:(x + 1) * D].rearrange("z (a b c) -> z a b c", a=2 * PR, b=L) for x in range(2))

        r = Region(end=P1_AT)
        hsb = r(MT, IN_W)
        qkr = r(MT, HQ + HKV, 2, HD // 2)
        kd = r(MT, HKV, 2, HD)
        qT, kT = r(4, SEQ), r(HKV, SEQ)
        pr_ = r(HQ, MT, SEQ)
        pT = r(HQ, 2, SEQ)
        mixT = r(KT, SEQ)
        sguT, sgub = r(G, P), r(G)
        sgln = r(2, 512)
        bout = r(MT, 512)
        mask = r(MT, SEQ)
        cs = r(MT, 2, HD // 2)
        sink = r(HQ)
        mxs, den = r(HQ, MT), r(4, HQ * MT)
        rtmp = r(2, HQ + HKV, HD // 2)
        gst = r(4, MT * G)
        start = [pT.rearrange("z a b c -> z (a b c)"), res[:].rearrange("z a b -> z (a b)")]
        lamdt = start[0][:, 0:3 * NT].rearrange("z (a b) -> z a b", a=3)
        pa = start[0][:, 3 * NT:3 * NT + 2 * NT * (L + 1)].rearrange("z (r t l) -> z r t l", r=2, t=NT)
        sm = start[1][:, 0:24 * NT].rearrange("z (a b) -> z a b", a=24)
        pow_a, pow_b = start[1][:, 24 * NT:28 * NT], start[1][:, 28 * NT:32 * NT]
        gsq = res[:].rearrange("z a b -> z (a b)")[:, 0:MT * G * HD]

        r = Region()
        xg = r(2, 8, L, CG)
        yk = xg.rearrange("z a b c d -> z a (b c d)").rearrange("z a (i f) -> z a i f", i=L)
        xl = res[:].rearrange("z a (j f) -> z a j f", j=L)
        U = r(64, NC)
        wb = r(2, 2 * 2 * PR * (L + 1) * CG)
        Tb = r(2, 8, P)
        S = r(2, 2, NC + 1, 2 * HT)
        Sz = r(2, 2, KT * PR, 2, NC)
        pd = sg[:].rearrange("z a b -> z (a b)")[:, 0:8 * HT].rearrange("z (d o t) -> z d o t", d=2, o=2)

        def dram(name, shape):
            return nc.dram_tensor(name, shape, F32, kind="Internal").ap()

        w1_d = dram("w1_d", (KT, P, 16 * P))
        w2_d = dram("w2_d", (KT, P, 2 * 2 * PR * (L + 1) * CG))
        t_d = dram("t_d", (KT, P, 8 * P))
        x2_d = dram("x2_d", (SEQ, D))

        names = """const_in x_in win_in0 win_in1 win_in2 win_in3 ident_in wout_in lamdt_in s5_in eye_in
            act_step dve_step pool_step
            s5_ready s5_free bz_ready w1t_ps w1_sb kgen_ps kext_sb s5_bz s5_w1t s5_w2 s5_kx w1_out t_out
            proj_ps proj_sb rope_ok qkT_ps qkT_sb sc_ps sc_sb mx_ok exp_ok p_ok
            pT_ps pT_sb pv_ps pv_sb gelu_ok vn_ok sv_ps bo_ok bT_ps bT_sb op_ps attn_ok
            ln_in ln_var ln_std ln_out xT_ps xT_sb ln_p
            glu_ps glu_sig glu_z
            ffn_gu_hi ffn_gu_lo ffn_dn_hi ffn_dn_lo ffn_used ffn_silu ffn_h ffn_tr
            ffn_hT_hi ffn_hT_lo ffn_down ffn_tile x1_lo
            gu_used gu_hi gu_lo dn_hi dn_lo silu_ok h_ok tr_ps hT_hi hT_lo down_ok
            hot_ok gath_ps xe_hi xe_lo scat_ps scat_sb ysb_ok put_ps acc_ok sel_ok rank_ps route_ok res_ok
            x2_out xg_ok xk_in0 xk_in1 uT_ps u_sb wk_in0 wk_in1 tk_in0 tk_in1 s_ps s_sb scan_ok scan_p sz_ok y_ps y_g yt_ps yt_sb
            rt_ps comb_ok fin out_sent dbg wk_used""".split()
        s = {n: sem(n) for n in names}
        slot_full = [sem(f"slot_full{i}") for i in range(R)]
        ffn_full = [sem(f"ffn_full{i}") for i in range(PER)]

        def bank(i, n=512):
            return ps[:, i, 0:n]

        w_in_v = mem[:, 0:KT * IN_W].rearrange("z (k n) -> z k n", k=KT)
        w_out_v = mem[:, WOUT0:KT * IN_W].rearrange("z (k n) -> z k n", k=KT)

        block = ctx.enter_context(nc.Block())

        def s5_loads(sp, load_glu):
            for k in range(2):
                sp.dma_start(wb[:, k, 0:16 * P], w1_d[k]).then_inc(s[f"wk_in{k}"], 16)
            for i in range(2, GLU_ITEMS // 2):
                load_glu(i)
            sp.wait_ge(s["x2_out"], 16)
            xk = x2_d.rearrange("(n j) (k f) -> k n j f", j=L, f=P)
            for k in range(KT):
                sp.dma_start(xl[NC * (k % 4):NC * (k % 4 + 1), k // 4], xk[k]).then_inc(s[f"xk_in{k // 4}"], 16)
            for i in range(GLU_ITEMS // 2, GLU_ITEMS):
                load_glu(i)
            for k in range(2, 2 * KT):
                if k < KT + 2:
                    sp.wait_ge(s["wk_used"], k - 1)
                else:
                    sp.wait_ge(s["y_ps"], k - KT - 1)
                src = w1_d[k] if k < KT else w2_d[k - KT]
                sp.dma_start(wb[:, k % 2, 0:src.shape[1]], src).then_inc(s[f"wk_in{k % 2}"], 16)
                if k >= KT:
                    kk = k - KT
                    sp.dma_start(Tb[:, kk % 2].rearrange("z g n -> z (g n)"), t_d[kk]).then_inc(s[f"tk_in{kk % 2}"], 16)

        @block.sync
        def _(sp):
            sp.dma_start(lamdt, a["s5_lamdt"]).then_inc(s["lamdt_in"], 16)
            sp.dma_start(ident[:], a["ident"]).then_inc(s["ident_in"], 16)
            sp.dma_start(x_tok[:], a["x"].rearrange("(m p) d -> p m d", p=P)).then_inc(s["x_in"], 16)
            for n in range(4):
                cols = slice(n * PROJ_N, (n + 1) * PROJ_N)
                sp.dma_start(w_in_v[:, :, cols], a["w_in"].rearrange("z (k n) -> z k n", k=KT)[:, :, cols]
                             ).then_inc(s[f"win_in{n}"], 16)
            sp.dma_start(wr_sb[:].rearrange("z k e -> z (k e)"), a["w_router"]).then_inc(s["eye_in"], 16)
            for dst, n in ((iota8, "iota8"), (iotaP, "iotaP"), (tri, "tri")):
                sp.dma_start(dst[:], a[n]).then_inc(s["eye_in"], 16)
            for dst, n in ((sguT.rearrange("z a b -> z (a b)"), "sguT"), (sgub, "sgub"),
                           (mask.rearrange("z a b -> z (a b)"), "mask"),
                           (cs.rearrange("z a b c -> z (a b c)"), "cossin"),
                           (sink, "sink"), (sgln.rearrange("z a b -> z (a b)"), "sgln")):
                src = a[n] if a[n].shape[0] == P else a[n].to_broadcast([P, a[n].shape[1]])
                sp.dma_start(dst, src).then_inc(s["const_in"], 16)
            sp.wait_ge(s["proj_ps"], 8)
            sp.dma_start(mem[:, WOUT0:KT * IN_W], a["w_out"]).then_inc(s["wout_in"], 16)

            def load_item(slot, src):
                sp.dma_start(ring[:, slot, :], src).then_inc(slot_full[slot], 16)

            def wait_split(turn, i):
                n, j = turn * NCH + i // PER, i % PER
                if j < 2:
                    sp.wait_ge(s["gu_lo"], 2 * n + (j + 1))
                else:
                    sp.wait_ge(s["dn_lo"], n + 1)

            def load_ffn(c, j):
                sp.dma_start(ring[:, j, :], a["ffn_w"][bass.ds(c * PER + j, 1)].rearrange("o p n -> (o p) n")
                             ).then_inc(ffn_full[j], 16)

            for j in range(PER):
                load_ffn(0, j)
            sp.wait_ge(s["op_ps"], 2)
            for dst, n in ((Bp, "s5_b"), (Cp, "s5_c")):
                sp.dma_start(dst.rearrange("z a b c d e -> z (a b c d e)"), a[n]).then_inc(s["s5_in"], 16)
            sp.dma_start(Dp, a["s5_d"]).then_inc(s["s5_in"], 16)
            sp.dma_start(eye16, a["eye16"]).then_inc(s["s5_in"], 16)

            def load_next(c):
                for j in range(2):
                    sp.wait_ge(s["ffn_gu_lo"], c * 2 + (3 + j))
                    load_ffn(c + 2, j)
                sp.wait_ge(s["ffn_dn_lo"], c + 1)
                load_ffn(c + 1, 2)

            def store_w2(k):
                sp.wait_ge(s["s5_w2"], k + 1)
                sp.dma_start(w2_d[bass.ds(k, 1)].rearrange("o p n -> (o p) n"),
                             w2.rearrange("z a b c d -> z (a b c d)")).then_inc(s["s5_free"], 16)

            def store_w1(k):
                sp.wait_ge(s["w1_sb"], 4 * k + 4)
                sp.dma_start(w1_d[bass.ds(k, 1)].rearrange("o p n -> (o p) n"),
                             w1.rearrange("z a b -> z (a b)")).then_inc(s["w1_out"], 16)

            def store_t(k):
                sp.wait_ge(s["kext_sb"], k + 1)
                for j in range(L):
                    dst = t_d[bass.ds(k, 1), j * CG:(j + 1) * CG].rearrange("o c (g n) -> g (o c) n", g=8)
                    sp.dma_start(dst, kext[:, L - 1 - j:2 * L - 1 - j, :]).then_inc(s["t_out"], 16)

            for j in range(2):
                sp.wait_ge(s["ffn_gu_lo"], 1 + j)
                load_ffn(1, j)
            for c in range(CHUNK_A):
                load_next(c)
            store_w2(0)
            load_next(CHUNK_A)
            with sp.Fori(1, KT - 1) as k:
                store_t(k - 1)
                store_w2(k)
                load_next(k + CHUNK_A)
                store_w1(k - 1)
            store_t(KT - 2)
            store_w2(KT - 1)
            sp.wait_ge(s["ffn_dn_lo"], NCH - 1)
            load_ffn(NCH - 1, 2)
            store_w1(KT - 2)
            store_t(KT - 1)
            store_w1(KT - 1)

            def load_glu(i):
                load_item(i, a["glu_w"][i])

            sp.wait_ge(s["ffn_gu_lo"], 2 * NCH)
            load_glu(0)
            load_glu(1)
            sp.wait_ge(s["ffn_tile"], MT)
            sp.wait_ge(s["s5_free"], 16 * KT)
            sp.wait_ge(s["w1_out"], 16 * KT)
            sp.wait_ge(s["t_out"], 16 * L * KT)

            def load_expert(turn, e, items):
                for i in items:
                    wait_split(turn, i - R)
                    load_item((MOE_ITEM0 + i) % R,
                              a["moe_w"][bass.ds(e * ITEMS + i, 1)].rearrange("o p n -> (o p) n"))

            s5_loads(sp, load_glu)
            for i in range(ITEMS):
                if i == 0:
                    sp.wait_ge(s["yt_ps"], KT)
                elif R - GLU_ITEMS <= i < R:
                    sp.wait_ge(s["glu_ps"], 2 * ((i - (R - GLU_ITEMS)) // 2 + 1))
                elif i >= R:
                    wait_split(1, i - R)
                load_item((MOE_ITEM0 + i) % R, a["moe_w"][i])
            ahead, rest = range(2), range(2, ITEMS)
            load_expert(2, 1, ahead)
            with sp.Fori(2, NE) as turn:
                load_expert(turn, turn - 1, rest)
                load_expert(turn + 1, turn, ahead)
            load_expert(NE, NE - 1, rest)
            sp.wait_ge(s["route_ok"], 1)
            n_over = sp.value_load(over_i[0:1, 0:1], min_val=0, max_val=NOV)
            load_expert(NE + 1, sp.value_load(over_i[0:1, 1:2], min_val=0, max_val=NE - 1), ahead)
            with sp.Fori(0, NOV) as i:
                with sp.If(i < n_over):
                    e = sp.value_load(over_i[0:1, bass.ds(i + 1, 1)], min_val=0, max_val=NE - 1)
                    load_expert(i + (1 + NE), e, rest)
                    e = sp.value_load(over_i[0:1, bass.ds(i + 2, 1)], min_val=0, max_val=NE - 1)
                    load_expert(i + (2 + NE), e, ahead)
            sp.wait_ge(s["fin"], 2)
            sp.dma_start(out.rearrange("(m p) d -> p m d", p=P), x_tok[:]).then_inc(s["out_sent"], 16)
            sp.wait_ge(s["out_sent"], 16)

        def ksel(v, x, k):
            return v[:, x, bass.ds(k, 1)].rearrange("z o d p n -> z (o d p) n")

        @block.gpsimd
        def _(pool):
            def ln_params(n):
                if n:
                    pool.wait_ge(s["ln_out"], 2 * n)
                for j, what in enumerate(("ln_g", "ln_b")):
                    pool.dma_start(lnp[:, j, :], a[what][n:n + 1, :].to_broadcast([P, D])).then_inc(s["ln_p"], 16)

            ln_params(0)
            ln_params(1)
            pstep = Steps(pool, s["pool_step"])

            per_turn = 10

            def w1t_pool(k, first):
                for x in range(2):
                    pool.tensor_copy(B_k[:, x], ksel(Bp, x, k)).then_inc(s["pool_step"], 1)
                    pool.tensor_copy(p1_k[:, x], ksel(p1, x, k)).then_inc(s["pool_step"], 1)
                pstep.passed(4)
                B_, Q_ = ([v[:, x] for x in (0, 1)] for v in (B_k, p1_k))
                bb = [v.unsqueeze(2).to_broadcast([P, 2 * PR, L, CG]) for v in B_]
                qb = [v.unsqueeze(3).to_broadcast([P, 2 * PR, L, CG]) for v in Q_]
                pstep(pool.tensor_tensor(tc, bb[0], qb[0], ALU.mult))
                pstep(pool.tensor_tensor(td, bb[1], qb[1], ALU.mult))
                if not first:
                    pool.wait_ge(s["w1t_ps"], 4 * k)
                pstep(pool.tensor_tensor(w1t[:, 0], tc, td, ALU.subtract))
                pstep(pool.tensor_tensor(tc, bb[0], qb[1], ALU.mult))
                pstep(pool.tensor_tensor(td, bb[1], qb[0], ALU.mult))
                pstep(pool.tensor_tensor(w1t[:, 1], tc, td, ALU.add))
                pool.sem_inc(s["s5_w1t"], 1)

            pool.wait_ge(s["s5_w2"], 1)
            w1t_pool(0, True)
            with pool.Fori(1, KT) as k:
                pstep.loop(k - 1, per_turn)
                w1t_pool(k, False)
            pstep.end_loop(KT - 1)
            pool.wait_ge(s["ln_out"], 4)
            pool.dma_start(x2_d.rearrange("(m p) d -> p m d", p=P), x_tok[:]).then_inc(s["x2_out"], 16)
            ln_params(2)
            ln_params(3)

        def products(pe, o, lhs, rhs, start, stop):
            (lh, ll), (rh, rl) = lhs, rhs
            pe.matmul(o, ll, rh, start=start, stop=False)
            pe.matmul(o, lh, rl, start=False, stop=False)
            return pe.matmul(o, lh, rh, start=False, stop=stop)

        def gate_up(pe, n):
            for j in range(2):
                pe.wait_ge(s["gu_lo"], 2 * n + (j + 1))
                if j == 0:
                    pe.wait_ge(s["h_ok"], n)
                for k in range(KT // 2):
                    kk = j * KT // 2 + k
                    w = slice(k * 2 * FC, (k + 1) * 2 * FC)
                    mm = products(pe, bank(4), (xh[:, kk, :], xl_[:, kk, :]),
                                  (wh[:, j, w], wl[:, j, w]), kk == 0, kk == KT - 1)
                mm.then_inc(s["gu_used"], 1)

        def turn_h(pe, n):
            pe.wait_ge(s["h_ok"], n + 1)
            for t in range(SUB):
                mm = pe.transpose(ps[:, 6, t * P:(t + 1) * P], h[:, 0, t * P:(t + 1) * P], ident[:])
            mm.then_inc(s["tr_ps"], 1)

        def down(pe, n, start, stop):
            pe.wait_ge(s["hT_lo"], n + 1)
            pe.wait_ge(s["dn_lo"], n + 1)
            for t in range(SUB):
                for b in range(2):
                    w = slice(t * D + b * 512, t * D + (b + 1) * 512)
                    mm = products(pe, bank(b), (hTh[:, t, :], hTl[:, t, :]),
                                  (wh[:, 2, w], wl[:, 2, w]), start and t == 0, stop and t == SUB - 1)
            mm.then_inc(s["down_ok"], 1)

        def swiglu_pe(pe, turn, after_first, before_down, before_last):
            n = turn * NCH
            gate_up(pe, n)
            after_first()
            turn_h(pe, n)
            gate_up(pe, n + 1)
            before_down()
            down(pe, n, True, False)
            turn_h(pe, n + 1)
            with pe.Fori(2, NCH) as c:
                gate_up(pe, c + n)
                down(pe, c + (n - 1), False, False)
                turn_h(pe, c + n)
            before_last()
            down(pe, n + (NCH - 1), False, True)

        def split_hi(act, n, j, slot, use):
            act.wait_ge(slot_full[slot], use)
            act.wait_ge(s["gu_used" if j < 2 else "down_ok"], 2 * n + (j - 1) if j < 2 else n)
            act.copy(wh[:, j, :], ring[:, slot, :]).then_inc(s["gu_hi" if j < 2 else "dn_hi"], 1)

        def swiglu_act(act, turn, uses):
            n = turn * NCH
            for c in range(NCH):
                for part in range(PER):
                    cc = c + (1 if part < 2 else 0)
                    i = cc * PER + part
                    split_hi(act, n + cc, part, (MOE_ITEM0 + i) % R, uses(i))
                    if part == 0:
                        act.wait_ge(s["gu_used"], 2 * (n + c) + 2)
                        act.wait_ge(s["h_ok"], n + c)
                        act.activation(sg[:, 0, :], ps[:, 4, 0:FC], ACT.Silu).then_inc(s["silu_ok"], 1)
                    elif part == 2:
                        act.wait_ge(s["tr_ps"], n + (c + 1))
                        act.copy(hTh[:].rearrange("z t n -> z (t n)"), ps[:, 6, 0:FC]).then_inc(s["hT_hi"], 1)

        def split_lo(dve, n, j, slot):
            dve.wait_ge(s["gu_hi" if j < 2 else "dn_hi"], 2 * n + (j + 1) if j < 2 else n + 1)
            dve.tensor_tensor(wl[:, j, :], ring[:, slot, :], wh[:, j, :].bitcast(F32),
                              ALU.subtract).then_inc(s["gu_lo" if j < 2 else "dn_lo"], 1)

        def swiglu_dve(dve, turn, after_chunk):
            n = turn * NCH
            for c in range(NCH):
                for part in range(PER):
                    cc = c + (1 if part < 2 else 0)
                    split_lo(dve, n + cc, part, (MOE_ITEM0 + cc * PER + part) % R)
                    if part == 0:
                        dve.wait_ge(s["silu_ok"], n + (c + 1))
                        dve.wait_ge(s["tr_ps"], n + c)
                        dve.tensor_tensor(h[:, 0, :], sg[:, 0, :], ps[:, 4, FC:2 * FC], ALU.mult).then_inc(s["h_ok"], 1)
                    elif part == 2:
                        dve.wait_ge(s["hT_hi"], n + (c + 1))
                        dve.tensor_tensor(hTl[:].rearrange("z t n -> z (t n)"), ps[:, 6, 0:FC],
                                          hTh[:].bitcast(F32).rearrange("z t n -> z (t n)"),
                                          ALU.subtract).then_inc(s["hT_lo"], 1)
                after_chunk(c)

        def turn_y(pe, k):
            pe.wait_ge(s["y_g"], 4 * (k + 1))
            if k >= 2:
                pe.wait_ge(s["yt_sb"], k - 1)
            for i in range(L):
                mm = pe.transpose(ps[:, k % 2, i * NC:(i + 1) * NC], yk[0:NC, k % 2, i, :], ident[0:NC, 0:NC])
            mm.then_inc(s["yt_ps"], 1)

        @block.tensor
        def _(pe):
            pe.wait_ge(s["ident_in"], 16)
            def turn_x(ready, count):
                for t in range(4):
                    m, half = t // 2, t % 2
                    pe.wait_ge(s["ln_out" if ready is None else ready], (count + m + 1) if ready is None else 16)
                    if t >= 2:
                        pe.wait_ge(s["xT_sb"], pe_turns[0] * 4 + t - 1)
                        if pe_turns[0] == 1:
                            pe.wait_ge(s["x1_lo"], t - 1)
                    for j in range(4):
                        mm = pe.transpose(ps[:, 6 + t % 2, j * P:(j + 1) * P],
                                          x_tok[:, m, (4 * half + j) * P:(4 * half + j + 1) * P], ident[:])
                    mm.then_inc(s["xT_ps"], 1)
                pe_turns[0] += 1

            pe_turns = [0]
            turn_x("x_in", 0)
            pe.wait_ge(s["xT_sb"], 4)
            for n in range(4):
                pe.wait_ge(s[f"win_in{n}"], 16)
                for m in range(MT):
                    for k in range(KT):
                        mm = pe.matmul(bank(4 * m + n, PROJ_N), xT[:, k, m * P:(m + 1) * P],
                                       w_in_v[:, k, n * PROJ_N:(n + 1) * PROJ_N], start=k == 0, stop=k == KT - 1)
                    mm.then_inc(s["proj_ps"], 1)
            pe.wait_ge(s["proj_sb"], 8)
            pe.wait_ge(s["rope_ok"], 2)
            for m in range(MT):
                for j in range(4):
                    pe.transpose(ps[:, j // 2, (j % 2) * SEQ + m * P:(j % 2) * SEQ + (m + 1) * P],
                                 qkr[:, m, 2 * j:2 * j + 2].rearrange("z a b c -> z (a b c)"), ident[:])
                for j in range(HKV):
                    mm = pe.transpose(ps[:, 2, j * SEQ + m * P:j * SEQ + (m + 1) * P],
                                      kd[:, m, j].rearrange("z a b -> z (a b)"), ident[:])
            mm.then_inc(s["qkT_ps"], 1)
            pe.wait_ge(s["qkT_sb"], 3)
            for hd in range(HQ):
                o = HD * (hd % 2)
                for m in range(MT):
                    mm = pe.matmul(ps[:, hd, m * SEQ:(m + 1) * SEQ], qT[o:o + HD, hd // 2, m * P:(m + 1) * P],
                                   kT[o:o + HD, hd // 4, :], start=True, stop=True)
                mm.then_inc(s["sc_ps"], 1)
            pe.wait_ge(s["p_ok"], 1)
            for hd in range(HQ):
                if hd >= 4:
                    pe.wait_ge(s["pT_sb"], hd - 3)
                for m in range(MT):
                    for kt in range(2):
                        mm = pe.transpose(ps[:, 2 + hd % 4, kt * SEQ + m * P:kt * SEQ + (m + 1) * P],
                                          pr_[:, hd, m, kt * P:(kt + 1) * P], ident[:])
                mm.then_inc(s["pT_ps"], 1)
            for hd in range(HQ):
                pe.wait_ge(s["pT_sb"], hd + 1)
                o = HD * (hd % 2)
                for kt in range(2):
                    v = hsb[:, kt, V0 + (hd // 4) * HD:V0 + (hd // 4 + 1) * HD]
                    mm = pe.matmul(ps[o:o + HD, 6 + hd // 4, (hd // 2 % 2) * SEQ:(hd // 2 % 2 + 1) * SEQ],
                                   v, pT[:, hd, kt, :], start=kt == 0, stop=kt == 1)
            mm.then_inc(s["pv_ps"], 1)
            pe.wait_ge(s["vn_ok"], 1)
            pe.wait_ge(s["sc_sb"], 8)
            pe.wait_ge(s["const_in"], 96)
            for g in range(G):
                mm = pe.matmul(ps[:, g // 4, (g % 4) * P:(g % 4 + 1) * P], sguT[:, g, :],
                               hsb[:, :, Z0 + g * HD:Z0 + (g + 1) * HD], start=True, stop=True)
            mm.then_inc(s["sv_ps"], 1)
            pe.wait_ge(s["bo_ok"], 1)
            for m in range(MT):
                for j in range(4):
                    mm = pe.transpose(ps[:, j // 2, (j % 2) * SEQ + m * P:(j % 2) * SEQ + (m + 1) * P],
                                      bout[:, m, j * P:(j + 1) * P], ident[:])
            mm.then_inc(s["bT_ps"], 1)
            pe.wait_ge(s["wout_in"], 16)
            pe.wait_ge(s["attn_ok"], 4)
            for m in range(MT):
                for n in range(2):
                    for k in range(KT):
                        mm = pe.matmul(bank(2 * m + n), mixT[:, k, m * P:(m + 1) * P],
                                       w_out_v[:, k, n * 512:(n + 1) * 512], start=k == 0, stop=k == KT - 1)
                mm.then_inc(s["op_ps"], 1)
            turn_x(None, 0)
            pe.wait_ge(s["x1_lo"], 4)

            def ffn_gate_up(c, first=False, tables=False):
                if not first:
                    pe.wait_ge(s["ffn_h"], c)
                if tables:
                    pe.wait_ge(s["w1_sb"], 4 * (c - CHUNK_A - 1))
                for j in range(2):
                    pe.wait_ge(s["ffn_gu_lo"], 2 * c + (j + 1))
                    for m in range(MT):
                        for k in range(KT // 2):
                            kk = j * KT // 2 + k
                            w = slice(k * 2 * FC, (k + 1) * 2 * FC)
                            mm = products(pe, bank(4 + m), (ffn_xh[:, m, kk, :], ffn_xl[:, m, kk, :]),
                                          (ffn_wh[:, j, w], ffn_wl[:, j, w]), kk == 0, kk == KT - 1)
                    mm.then_inc(s["ffn_used"], 1)

            def ffn_turn_h(c):
                pe.wait_ge(s["ffn_h"], c + 1)
                for m in range(MT):
                    for t in range(SUB):
                        mm = pe.transpose(ps[:, 6, (m * SUB + t) * P:(m * SUB + t + 1) * P],
                                          h[:, m, t * P:(t + 1) * P], ident[:])
                mm.then_inc(s["ffn_tr"], 1)

            def ffn_down(c, start, stop):
                pe.wait_ge(s["ffn_hT_lo"], c + 1)
                pe.wait_ge(s["ffn_dn_lo"], c + 1)
                for m in range(MT):
                    for t in range(SUB):
                        for b in range(2):
                            w = slice(t * D + b * 512, t * D + (b + 1) * 512)
                            mm = products(pe, bank(2 * m + b), (ffn_hTh[:, m, t, :], ffn_hTl[:, m, t, :]),
                                          (ffn_wh[:, 2, w], ffn_wl[:, 2, w]),
                                          start and t == 0, stop and t == SUB - 1)
                    if stop:
                        mm.then_inc(s["ffn_tile"], 1)
                if not stop:
                    mm.then_inc(s["ffn_down"], 1)

            def s5_kernels_pe(k, first):
                pe.wait_ge(s["s5_w2"], k + 1)
                pe.wait_ge(s["s5_bz"], k + 1)
                if not first:
                    pe.wait_ge(s["s5_kx"], k)
                for d in range(2):
                    for p in range(PR):
                        for ri in range(2):
                            mm = pe.matmul(ps[32 * p:32 * p + 32, 7, d * P:(d + 1) * P],
                                           Bz[:, ri, d * PR + p].rearrange("z a b -> z (a b)"),
                                           w2[:, ri, d * PR + p, d:d + L, :].rearrange("z a b -> z (a b)"),
                                           start=ri == 0, stop=ri == 1)
                mm.then_inc(s["kgen_ps"], 1)

            def s5_turn_w1(k):
                pe.wait_ge(s["s5_w1t"], k + 1)
                for t in range(16):
                    if t % 4 == 0 and t >= 8:
                        pe.wait_ge(s["w1_sb"], 4 * k + (t // 4 - 1))
                    mm = pe.transpose(ps[:, 4 + t // 4 % 2, (t % 4) * P:(t % 4 + 1) * P],
                                      w1t[:, t // 8, t % 8].rearrange("z a b -> z (a b)"), ident[:])
                    if t % 4 == 3:
                        mm.then_inc(s["w1t_ps"], 1)

            def ffn_chunk(c, tables):
                ffn_gate_up(c, tables=tables)
                ffn_down(c - 1, False, False)
                ffn_turn_h(c)

            ffn_gate_up(0, first=True)
            ffn_turn_h(0)
            ffn_gate_up(1)
            ffn_down(0, True, False)
            ffn_turn_h(1)
            ffn_chunk(CHUNK_A, False)
            s5_kernels_pe(0, True)
            ffn_chunk(CHUNK_A + 1, False)
            s5_turn_w1(0)
            s5_kernels_pe(1, False)
            with pe.Fori(2, KT) as k:
                ffn_chunk(k + CHUNK_A, True)
                s5_turn_w1(k - 1)
                s5_kernels_pe(k, False)
            ffn_chunk(NCH - 1, True)
            s5_turn_w1(KT - 1)
            ffn_down(NCH - 1, False, True)
            for k in range(KT):
                pe.wait_ge(s["xg_ok"], k // 4 + 1)
                if k == 0:
                    pe.wait_ge(s["ln_out"], 4)
                if k >= 2:
                    pe.wait_ge(s["u_sb"], k - 1)
                o = NC * (k % 4)
                for g in range(8):
                    mm = pe.transpose(ps[:, 4 + k % 2, g * NC:(g + 1) * NC],
                                      xg[o:o + NC, k // 4, g].rearrange("z a b -> z (a b)"),
                                      ident[o:o + NC, o:o + NC])
                mm.then_inc(s["uT_ps"], 1)
            for k in range(KT):
                pe.wait_ge(s["u_sb"], k + 1)
                pe.wait_ge(s[f"wk_in{k % 2}"], 16 * (k // 2 + 1))
                if k >= 2:
                    pe.wait_ge(s["s_sb"], 2 * k - 2)
                for ri in range(2):
                    for d in range(2):
                        for p in range(PR):
                            t = (ri * 2 + d) * PR + p
                            for g2 in range(2):
                                mm = pe.matmul(ps[64 * g2:64 * g2 + 64, 6 + k % 2, ((d * 2 + ri) * PR + p) * NC:((d * 2 + ri) * PR + p + 1) * NC],
                                               wb[:, k % 2, t * P + 64 * g2:t * P + 64 * g2 + 64],
                                               U[:, 8 * k + 2 * p + g2, :], start=True, stop=True)
                mm.then_inc(s["wk_used"], 1)
            def local(k):
                if k >= 2:
                    pe.wait_ge(s["y_g"], 4 * (k - 1))
                pe.wait_ge(s[f"tk_in{k % 2}"], 16 * (k // 2 + 1))
                for p in range(PR):
                    for g2 in range(2):
                        o = 64 * (p % 2) + 32 * g2
                        pe.matmul(ps[o:o + 32, 4 + k % 2, (p // 2) * P:(p // 2 + 1) * P],
                                  U[:, 8 * k + 2 * p + g2, :], Tb[:, k % 2, 2 * p + g2, :],
                                  start=p < 2, stop=False, skip_group_check=True)

            def from_states(k):
                pe.wait_ge(s[f"wk_in{k % 2}"], 16 * ((k + KT) // 2 + 1))
                w2v = wb[:, k % 2].rearrange("z (r d p l) -> z r d p l", r=2, d=2, p=PR)
                for p in range(PR):
                    o = 64 * (p % 2)
                    for d in range(2):
                        for ri in range(2):
                            lo = CG if d == 0 else 0
                            mm = pe.matmul(ps[o:o + 64, 4 + k % 2, (p // 2) * P:(p // 2 + 1) * P],
                                           Sz[:, d, ri, k * PR + p].rearrange("z a b -> z (a b)"),
                                           w2v[:, ri, d, p, lo:lo + P], start=False, stop=d + ri == 2,
                                           skip_group_check=True)
                mm.then_inc(s["y_ps"], 1)

            for half in range(2):
                k0 = half * KT // 2
                local(k0)
                if half:
                    turn_y(pe, k0 - 1)
                local(k0 + 1)
                pe.wait_ge(s["sz_ok"], 8 * (half + 1))
                for k in range(k0, k0 + KT // 2):
                    if k >= k0 + 2:
                        local(k)
                    from_states(k)
                    if k > k0:
                        turn_y(pe, k - 1)
            turn_y(pe, KT - 1)
            pe.wait_ge(s["yt_sb"], KT)
            for c in range(GLU_CH):
                for m in range(MT):
                    if c:
                        pe.wait_ge(s["glu_z"], 2 * c - 1 + m)
                    for k in range(KT):
                        item = 2 * c + k // (KT // 2)
                        if m == 0 and k % (KT // 2) == 0:
                            pe.wait_ge(slot_full[item % R], 16 * (item // R + 1))
                        kk = k % (KT // 2)
                        mm = pe.matmul(bank(m), xT[:, k, m * P:(m + 1) * P],
                                       ring[:, item % R, kk * 2 * FC:(kk + 1) * 2 * FC],
                                       start=k == 0, stop=k == KT - 1)
                    mm.then_inc(s["glu_ps"], 1)
            turn_x(None, 4)
            pe.wait_ge(s["xT_sb"], 12)
            for m in range(MT):
                for k in range(KT):
                    mm = pe.matmul(ps[:, 5, m * 8:m * 8 + 8], xT[:, k, m * P:(m + 1) * P], wr_sb[:, k, :],
                                   start=k == 0, stop=k == KT - 1)
            mm.then_inc(s["rt_ps"], 1)
            pe.wait_ge(s["sel_ok"], 1)
            pe.matmul(ps[:, 7, 0:NE], tri[:], sel[:, 0], start=True, stop=True)
            pe.matmul(ps[:, 7, NE:2 * NE], tri[:], sel[:, 1], start=True, stop=False)
            pe.matmul(ps[:, 7, NE:2 * NE], ones[:], sel[:, 0], start=False, stop=True)
            pe.matmul(ps[:, 7, 2 * NE:3 * NE], ones[:], sel[:, 0], start=True, stop=False)
            pe.matmul(ps[:, 7, 2 * NE:3 * NE], ones[:], sel[:, 1], start=False, stop=True).then_inc(s["rank_ps"], 1)
            pe.sem_inc(s["gu_used"], 2 * NCH)
            for n in ("tr_ps", "down_ok"):
                pe.sem_inc(s[n], NCH)

            def gather(turn):
                pe.wait_ge(s["hot_ok"], turn)
                for b, k0 in ((5, 0), (7, KT // 2)):
                    for k in range(k0, k0 + KT // 2):
                        for m in range(MT):
                            mm = pe.matmul(ps[:, b, (k - k0) * P:(k - k0 + 1) * P], x_tok[:, m, k * P:(k + 1) * P],
                                           pg[:, m, :], start=m == 0, stop=m == MT - 1)
                    mm.then_inc(s["gath_ps"], 1)

            def scatter(turn):
                pe.wait_ge(s["scat_sb"], turn)
                pe.wait_ge(s["ysb_ok"], turn)
                for m, b0 in ((0, 2), (1, 0)):
                    for b in range(2):
                        mm = pe.matmul(bank(b0 + b), scat[:, m * P:(m + 1) * P], ysb[:, b * 512:(b + 1) * 512],
                                       start=True, stop=True)
                    mm.then_inc(s["put_ps"], 1)

            def expert_pe(turn):
                pe.wait_ge(s["xe_lo"], 2 * turn)

                def before_down():
                    pe.wait_ge(s["acc_ok"], 2 * turn + 2)

                def before_last():
                    for m in range(MT):
                        mm = pe.transpose(ps[:, 2, m * P:(m + 1) * P], pgc[:, m, :], ident[:])
                    mm.then_inc(s["scat_ps"], 1)
                    gather(turn + 1)

                swiglu_pe(pe, turn, lambda: scatter(turn), before_down, before_last)

            pe.wait_ge(s["route_ok"], 1)
            gather(1)
            with pe.Fori(1, 1 + NE) as turn:
                expert_pe(turn)
            n_over = pe.value_load(over_i[0:1, 0:1], min_val=0, max_val=NOV)
            with pe.Fori(0, NOV) as i:
                with pe.If(i < n_over):
                    expert_pe(i + (1 + NE))
            scatter(n_over + (1 + NE))

        def copy_y(act, k):
            act.wait_ge(s["yt_ps"], k + 1)
            act.copy(xT[:, k, :].rearrange("z (n i) -> z i n", i=L),
                     ps[:, k % 2, 0:SEQ].rearrange("z (i n) -> z i n", i=L)).then_inc(s["yt_sb"], 1)

        @block.scalar
        def _(act):
            def s5_tables_act(k, first):
                if not first:
                    act.wait_ge(s["w1_out"], 16 * k)
                for t in range(4):
                    act.wait_ge(s["w1t_ps"], 4 * k + t + 1)
                    act.copy(w1[:, 4 * t:4 * t + 4].rearrange("z a b -> z (a b)"), bank(4 + t % 2)).then_inc(s["w1_sb"], 1)

            def copy_xT(turn):
                for t in range(4):
                    m, half = t // 2, t % 2
                    act.wait_ge(s["xT_ps"], 4 * turn + t + 1)
                    act.copy(ffn_xh[:, m, 4 * half:4 * half + 4, :] if turn == 1 else
                             xT[:, 4 * half:4 * half + 4, m * P:(m + 1) * P],
                             ps[:, 6 + t % 2, :].rearrange("z (a b) -> z a b", a=4)).then_inc(s["xT_sb"], 1)

            copy_xT(0)
            for n in range(4):
                for m in range(MT):
                    act.wait_ge(s["proj_ps"], MT * n + m + 1)
                    act.copy(hsb[:, m, n * PROJ_N:(n + 1) * PROJ_N], bank(4 * m + n, PROJ_N)).then_inc(s["proj_sb"], 1)
            act.wait_ge(s["qkT_ps"], 1)
            for j in range(2):
                act.copy(qT[:, 2 * j:2 * j + 2].rearrange("z a b -> z (a b)"), bank(j)).then_inc(s["qkT_sb"], 1)
            act.copy(kT.rearrange("z a b -> z (a b)"), bank(2)).then_inc(s["qkT_sb"], 1)
            act.wait_ge(s["proj_sb"], 8)
            for m in range(MT):
                act.activation(hsb[:, m, U0:IN_W], hsb[:, m, U0:IN_W], ACT.Gelu_apprx_tanh).then_inc(s["gelu_ok"], 1)
            act.wait_ge(s["mx_ok"], 1)
            for hd in range(HQ):
                for m in range(MT):
                    act.activation(pr_[:, hd, m, :], pr_[:, hd, m, :], ACT.Exp, bias=den[:, 0, 2 * hd + m:2 * hd + m + 1],
                                   accum_out=den[:, 1, 2 * hd + m:2 * hd + m + 1]).then_inc(s["exp_ok"], 1)
            act.activation(den[:, 2, :], den[:, 2, :], ACT.Exp).then_inc(s["exp_ok"], 1)
            act.wait_ge(s["ln_var"], 1)
            act.activation(gst[:, 2, :], gst[:, 2, :], ACT.Sqrt).then_inc(s["ln_std"], 1)
            for hd in range(HQ):
                act.wait_ge(s["pT_ps"], hd + 1)
                act.copy(pT[:, hd].rearrange("z a b -> z (a b)"), bank(2 + hd % 4)).then_inc(s["pT_sb"], 1)
            act.wait_ge(s["bT_ps"], 1)
            for j in range(2):
                act.copy(mixT[:, 4 + 2 * j:6 + 2 * j].rearrange("z a b -> z (a b)"), bank(j)).then_inc(s["attn_ok"], 1)
            act.wait_ge(s["pv_ps"], 1)
            for j in range(2):
                act.copy(mixT[:, 2 * j:2 * j + 2].rearrange("z a b -> z (a b)"), bank(6 + j)).then_inc(s["attn_ok"], 1)

            def norm_sqrt(n):
                for m in range(MT):
                    act.wait_ge(s["ln_var"], 1 + 2 * n + m + 1)
                    act.activation(ln_s[:, m, 1:2], ln_s[:, m, 0:1], ACT.Sqrt).then_inc(s["ln_std"], 1)

            def ffn_hi(c, j, first=False):
                act.wait_ge(ffn_full[j], 16 * (c + 1))
                if not first:
                    act.wait_ge(s["ffn_used" if j < 2 else "ffn_down"], 2 * c + (j - 1) if j < 2 else c)
                act.copy(ffn_wh[:, j, :], ring[:, j, :]).then_inc(s["ffn_gu_hi" if j < 2 else "ffn_dn_hi"], 1)

            for j in range(2):
                ffn_hi(0, j, True)
            norm_sqrt(0)
            copy_xT(1)
            def ffn_act(c, first=False, last=False):
                if not last:
                    ffn_hi(c + 1, 0)
                act.wait_ge(s["ffn_used"], 2 * c + 2)
                if not first:
                    act.wait_ge(s["ffn_h"], c)
                act.activation(sg[:], ps[:, 4:4 + MT, 0:FC], ACT.Silu).then_inc(s["ffn_silu"], 1)
                if not last:
                    ffn_hi(c + 1, 1)
                ffn_hi(c, 2, first)
                act.wait_ge(s["ffn_tr"], c + 1)
                act.copy(ffn_hTh[:].rearrange("z m t n -> z (m t n)"), ps[:, 6, 0:MT * FC]).then_inc(s["ffn_hT_hi"], 1)

            act.wait_ge(s["op_ps"], 2)
            ffn_act(0, True)
            ffn_act(1)
            ffn_act(CHUNK_A)
            ffn_act(CHUNK_A + 1)
            s5_tables_act(0, True)
            with act.Fori(1, KT - 1) as k:
                ffn_act(k + (CHUNK_A + 1))
                s5_tables_act(k, False)
            ffn_act(NCH - 1, last=True)
            s5_tables_act(KT - 1, False)
            norm_sqrt(1)
            for k in range(KT):
                act.wait_ge(s["uT_ps"], k + 1)
                act.copy(U[:, 8 * k:8 * k + 8].rearrange("z a b -> z (a b)"), ps[:, 4 + k % 2, 0:8 * NC]).then_inc(s["u_sb"], 1)
            for k in range(KT):
                act.wait_ge(s["wk_used"], k + 1)
                for d in range(2):
                    src = ps[:, 6 + k % 2, d * 256:(d + 1) * 256].rearrange("z (r p n) -> z n r p", r=2, p=PR)
                    at = slice(1, NC + 1) if d == 0 else slice(NC, 0, -1)
                    dst = S[:, 2 * k // KT, d, at].rearrange("z n (r t) -> z n r t", r=2)
                    dst = dst[:, :, :, k % (KT // 2) * PR:(k % (KT // 2) + 1) * PR]
                    act.copy(dst, src).then_inc(s["s_sb"], 1)
            for k in range(KT):
                act.wait_ge(s["y_ps"], k + 1)
                if k >= 2:
                    act.wait_ge(s["yt_ps"], k - 1)
                elif k == 0:
                    act.wait_ge(s["uT_ps"], KT)
                for q in range(4):
                    src = ps[32 * q:32 * q + 32, 4 + k % 2, 0:2 * P].rearrange("z (h i c) -> z i h c", h=2, i=L)
                    dst = yk[0:NC, k % 2].rearrange("z i (h q c) -> z i h q c", h=2, q=4)[:, :, :, q, :]
                    act.activation(dst, src, ACT.Gelu_apprx_tanh).then_inc(s["y_g"], 1)
                if k >= 1:
                    copy_y(act, k - 1)
            copy_y(act, KT - 1)
            for c in range(GLU_CH):
                for m in range(MT):
                    act.wait_ge(s["glu_ps"], 2 * c + m + 1)
                    if c:
                        act.wait_ge(s["glu_z"], 2 * c - 1 + m)
                    act.activation(sg[:, m, :], ps[:, m, FC:2 * FC], ACT.Sigmoid).then_inc(s["glu_sig"], 1)
            norm_sqrt(2)
            copy_xT(2)
            act.wait_ge(s["rt_ps"], 2)
            act.activation(rt[:, :, 1:2], rt[:, :, 0:1], ACT.Exp).then_inc(s["rt_ps"], 1)
            def xe_high(turn):
                for x, b in enumerate((5, 7)):
                    act.wait_ge(s["gath_ps"], 2 * turn + (x - 1))
                    act.copy(xh[:, x * KT // 2:(x + 1) * KT // 2].rearrange("z k n -> z (k n)"),
                             bank(b)).then_inc(s["xe_hi"], 1)

            def uses(turn, i):
                return turn * (16 * ITEMS // R) + 16 * ((MOE_ITEM0 + i) // R + 1 - ITEMS // R)

            def expert_act(turn):
                swiglu_act(act, turn, lambda i: uses(turn, i))
                act.wait_ge(s["scat_ps"], turn)
                act.copy(scat, ps[:, 2, 0:2 * P]).then_inc(s["scat_sb"], 1)
                xe_high(turn + 1)
                act.wait_ge(s["down_ok"], (turn + 1) * NCH)
                act.copy(ysb.rearrange("z (b n) -> z b n", b=2), ps[:, 0:2, :]).then_inc(s["ysb_ok"], 1)

            for n, v in (("silu_ok", 1), ("hT_hi", 1), ("dn_hi", 1), ("gu_hi", 2)):
                act.sem_inc(s[n], v * NCH)
            for j in range(2):
                split_hi(act, NCH, j, (MOE_ITEM0 + j) % R, uses(1, j))
            act.preload_act_table(ACT.Silu)
            act.wait_ge(s["route_ok"], 1)
            xe_high(1)
            with act.Fori(1, 1 + NE) as turn:
                expert_act(turn)
            n_over = act.value_load(over_i[0:1, 0:1], min_val=0, max_val=NOV)
            with act.Fori(0, NOV) as i:
                with act.If(i < n_over):
                    expert_act(i + (1 + NE))
            norm_sqrt(3)

        @block.vector
        def _(dve):
            step = Steps(dve, s["dve_step"])

            def tt(o, x, y, op):
                step(dve.tensor_tensor(o, x, y, op))

            def ts(o, x, s1, s2, op0, op1=None):
                step(dve.tensor_scalar(o, x, s1, s2, op0, op1) if op1 is not None
                     else dve.tensor_scalar(o, x, s1, None, op0))

            def stt(o, x, sc, y, op0, op1):
                step(dve.scalar_tensor_tensor(o, x, sc, y, op0, op1))

            MUL, ADD, SUB_ = ALU.mult, ALU.add, ALU.subtract

            free = iter(range(24))

            def small():
                return sm[:, next(free), :]

            q0, q1, q2, q3 = small(), small(), small(), small()

            def exp_parts(x, e, em1):
                ts(q0, x, -200.0, 200.0, ALU.max, ALU.min)
                ts(q1, q0, 1.0 / math.log(2.0), MAGIC, MUL, ADD)
                ts(q1, q1, MAGIC, None, SUB_)
                stt(q0, q1, -0.693359375, q0, MUL, ADD)
                stt(q0, q1, 2.12194440e-4, q0, MUL, ADD)
                ts(q2, q0, 1.0 / math.factorial(9), None, MUL)
                for n in range(8, 0, -1):
                    stt(q2, q2, 1.0 / math.factorial(n), q0, ADD, MUL)
                ts(q1, q1, 127.0, 0.0, ADD, ALU.max)
                step(dve.tensor_scalar(pw_i[:], q1, 255.0, None, ALU.min))
                step(dve.tensor_scalar(pw_i[:], pw_i[:], 23, None, ALU.logical_shift_left))
                pw = pw_i[:].bitcast(F32)
                stt(e, q2, 1.0, pw, ADD, MUL)
                if em1 is not None:
                    ts(q3, pw, -1.0, None, ADD)
                    tt(q0, q2, pw, MUL)
                    tt(em1, q0, q3, ADD)

            dve.wait_ge(s["lamdt_in"], 16)
            l_re, l_im, l_dt = lamdt[:, 0, :], lamdt[:, 1, :], lamdt[:, 2, :]
            dt_, la, lb, ea, em = small(), small(), small(), small(), small()
            exp_parts(l_dt, dt_, None)
            tt(la, l_re, dt_, MUL)
            tt(lb, l_im, dt_, MUL)
            exp_parts(la, ea, em)
            hh, h2, sh, ch, sb, oc = small(), small(), small(), small(), small(), small()
            ts(q0, lb, 1.0 / (2 * math.pi), MAGIC, MUL, ADD)
            ts(q0, q0, MAGIC, None, SUB_)
            stt(hh, q0, -6.28125, lb, MUL, ADD)
            stt(hh, q0, -1.93500518798828125e-3, hh, MUL, ADD)
            stt(hh, q0, -3.0199159819e-7, hh, MUL, ADD)
            ts(hh, hh, 0.5, None, MUL)
            tt(h2, hh, hh, MUL)
            f = math.factorial
            ts(sh, h2, 1.0 / f(13), None, MUL)
            for n, sign in ((11, -1), (9, 1), (7, -1), (5, 1), (3, -1)):
                stt(sh, sh, sign / f(n), h2, ADD, MUL)
            stt(sh, sh, 1.0, hh, ADD, MUL)
            ts(ch, h2, 1.0 / f(14) * -1, None, MUL)
            for n, sign in ((12, 1), (10, -1), (8, 1), (6, -1), (4, 1), (2, -1)):
                stt(ch, ch, sign / f(n), h2, ADD, MUL)
            ts(ch, ch, 1.0, None, ADD)
            stt(sb, sh, 2.0, ch, MUL, MUL)
            stt(oc, sh, 2.0, sh, MUL, MUL)
            br, bi, mr = small(), small(), small()
            tt(q0, ea, oc, MUL)
            tt(br, ea, q0, SUB_)
            tt(mr, em, q0, SUB_)
            tt(bi, ea, sb, MUL)
            cr, ci, nn = coef[:, 0, :], coef[:, 1, :], small()
            tt(q0, l_re, l_re, MUL)
            tt(q1, l_im, l_im, MUL)
            tt(q0, q0, q1, ADD)
            step(dve.reciprocal(nn, q0))
            tt(q0, mr, l_re, MUL)
            tt(q1, bi, l_im, MUL)
            tt(q0, q0, q1, ADD)
            tt(cr, q0, nn, MUL)
            tt(q0, bi, l_re, MUL)
            tt(q1, mr, l_im, MUL)
            tt(q0, q0, q1, SUB_)
            tt(ci, q0, nn, MUL)
            step(dve.memset(pa[:, 0, :, 0:1], 1.0))
            step(dve.memset(pa[:, 1, :, 0:1], 0.0))
            step(dve.tensor_copy(pa[:, 0, :, 1:2], br.unsqueeze(2)))
            step(dve.tensor_copy(pa[:, 1, :, 1:2], bi.unsqueeze(2)))
            for lo, n in ((1, 1), (2, 2), (4, 4)):
                sr, si = (pa[:, x, :, 1:1 + n] for x in (0, 1))
                mr_, mi_ = (pa[:, x, :, n:n + 1].to_broadcast([P, NT, n]) for x in (0, 1))
                dr, di = (pa[:, x, :, n + 1:2 * n + 1] for x in (0, 1))
                fa = pow_a[:, 0:NT * n].rearrange("z (a b) -> z a b", b=n)
                fb = pow_b[:, 0:NT * n].rearrange("z (a b) -> z a b", b=n)
                tt(fa, sr, mr_, MUL)
                tt(fb, si, mi_, MUL)
                tt(dr, fa, fb, SUB_)
                tt(fa, sr, mi_, MUL)
                tt(fb, si, mr_, MUL)
                tt(di, fa, fb, ADD)
            pav = pa.rearrange("z r (k d p) l -> z r k d p l", k=KT, d=2)
            for d in range(2):
                for half in range(2):
                    a8v = a8[:, half, d].rearrange("z a b (k p) -> z a b k p", k=KT // 2)
                    ks = slice(half * KT // 2, (half + 1) * KT // 2)
                    for o, i, x, sgn in ((0, 0, 0, 1.0), (0, 1, 1, -1.0), (1, 0, 1, 1.0), (1, 1, 0, 1.0)):
                        ts(a8v[:, o, i], pav[:, x, ks, d, :, L], sgn, None, MUL)
            for x in range(2):
                for i in range(L + 1):
                    step(dve.tensor_copy(p2[:, x, :, 0, :, i], pav[:, x, :, 0, :, i]))
                    step(dve.tensor_copy(p2[:, x, :, 1, :, i], pav[:, x, :, 1, :, L - i]))
                for i in range(L):
                    step(dve.tensor_copy(p1[:, x, :, 0, :, i], pav[:, x, :, 0, :, L - 1 - i]))
                    step(dve.tensor_copy(p1[:, x, :, 1, :, i], pav[:, x, :, 1, :, i]))
            dve.wait_ge(s["const_in"], 96)
            dve.wait_ge(s["proj_sb"], MT * -(-QK // PROJ_N))
            for m in range(MT):
                src = hsb[:, m, 0:QK].rearrange("z (h a b) -> z h a b", a=2, b=HD // 2)
                c_, s_ = (cs[:, m, x, :].unsqueeze(1).to_broadcast([P, HQ + HKV, HD // 2]) for x in (0, 1))
                x1, x2 = src[:, :, 0, :], src[:, :, 1, :]
                ra, rb = rtmp[:, 0], rtmp[:, 1]
                tt(ra, x1, c_, MUL)
                tt(rb, x2, s_, MUL)
                tt(qkr[:, m, :, 0, :], ra, rb, SUB_)
                tt(ra, x2, c_, MUL)
                tt(rb, x1, s_, MUL)
                tt(qkr[:, m, :, 1, :], ra, rb, ADD)
                kk = qkr[:, m, HQ:HQ + HKV].rearrange("z h a b -> z h (a b)")
                for x in range(2):
                    step(dve.tensor_copy(kd[:, m, :, x, :], kk))
                dve.sem_inc(s["rope_ok"], 1)
            for hd in range(HQ):
                dve.wait_ge(s["sc_ps"], hd + 1)
                step(dve.scalar_tensor_tensor(pr_[:, hd].rearrange("z a b -> z (a b)"), bank(hd), HD ** -0.5,
                                              mask.rearrange("z a b -> z (a b)"), MUL, ADD))
                dve.sem_inc(s["sc_sb"], 1)
            step(dve.tensor_reduce(mxs.rearrange("z a b -> z (a b)"), pr_.rearrange("z a b c -> z (a b) c"), AX.X, ALU.max))
            sinkb = sink.unsqueeze(2).to_broadcast([P, HQ, MT])
            tt(mxs, mxs, sinkb, ALU.max)
            ts(den[:, 0, :], mxs.rearrange("z a b -> z (a b)"), -1.0, None, MUL)
            tt(den[:, 2, :].rearrange("z (a b) -> z a b", b=MT), sinkb, mxs, SUB_)
            dve.sem_inc(s["mx_ok"], 1)
            dve.wait_ge(s["gelu_ok"], 2)
            vv = [hsb[:, m, Z0:IN_W].rearrange("z (g d) -> z g d", g=G) for m in range(MT)]
            sq = gsq.rearrange("z (m g d) -> z m g d", m=MT, g=G)
            mean, var, std = (gst[:, x, :] for x in (0, 1, 2))
            rs = gst[:, 3, :]
            for m in range(MT):
                step(dve.tensor_reduce(mean[:, m * G:(m + 1) * G], vv[m], AX.X, ADD))
            ts(mean, mean, 1.0 / HD, None, MUL)
            for m in range(MT):
                tt(vv[m], vv[m], mean[:, m * G:(m + 1) * G].unsqueeze(2).to_broadcast([P, G, HD]), SUB_)
                tt(sq[:, m], vv[m], vv[m], MUL)
                step(dve.tensor_reduce(var[:, m * G:(m + 1) * G], sq[:, m], AX.X, ADD))
            ts(var, var, 1.0 / HD, EPS, MUL, ADD)
            step(dve.tensor_copy(std, var))
            dve.sem_inc(s["ln_var"], 1)
            dve.wait_ge(s["exp_ok"], 2 * HQ + 1)
            tt(den[:, 3, :], den[:, 1, :], den[:, 2, :], ADD)
            step(dve.reciprocal(den[:, 1, :], den[:, 3, :]))
            pf = pr_.rearrange("z a b c -> z (a b) c")
            tt(pf, pf, den[:, 1, :].unsqueeze(2).to_broadcast([P, HQ * MT, SEQ]), MUL)
            dve.sem_inc(s["p_ok"], 1)
            dve.wait_ge(s["ln_std"], 1)

            def refine(rs_, std_, var_, t_):
                step(dve.reciprocal(rs_, std_))
                tt(t_, rs_, rs_, MUL)
                tt(t_, t_, var_, MUL)
                ts(t_, t_, -0.5, 1.5, MUL, ADD)
                tt(rs_, rs_, t_, MUL)

            refine(rs, std, var, mean)
            for m in range(MT):
                tt(vv[m], vv[m], rs[:, m * G:(m + 1) * G].unsqueeze(2).to_broadcast([P, G, HD]), MUL)
                fv = hsb[:, m, Z0:IN_W]
                tt(fv, fv, sgln[:, 0, :], MUL)
                tt(fv, fv, sgln[:, 1, :], ADD)
            dve.sem_inc(s["vn_ok"], 1)
            dve.wait_ge(s["sv_ps"], 1)
            for g in range(G):
                step(dve.scalar_tensor_tensor(
                    bout[:, :, g * HD:(g + 1) * HD],
                    ps[:, g // 4, (g % 4) * P:(g % 4 + 1) * P].rearrange("z (m d) -> z m d", m=MT), sgub[:, g:g + 1],
                    hsb[:, :, U0 + g * HD:U0 + (g + 1) * HD], ADD, MUL))
            dve.sem_inc(s["bo_ok"], 1)

            def norm(n, add_rest):
                for m in range(MT):
                    add_rest(m)
                    for x in range(2):
                        step(dve.bn_stats(stats[:, m, x, :], res[:, m, x * 512:(x + 1) * 512]))
                    step(dve.bn_aggr(mv[:, m, :], stats[:, m].rearrange("z a b -> z (a b)")))
                    ts(ln_s[:, m, 0:1], mv[:, m, 1:2], EPS, None, ADD)
                    dve.sem_inc(s["ln_var"], 1)
                for m in range(MT):
                    dve.wait_ge(s["ln_std"], 1 + 2 * n + m + 1)
                    refine(ln_s[:, m, 2:3], ln_s[:, m, 1:2], ln_s[:, m, 0:1], ln_s[:, m, 3:4])
                    dve.wait_ge(s["ln_p"], 32 * (n + 1))
                    ts(res[:, m], res[:, m], mv[:, m, 0:1], ln_s[:, m, 2:3], SUB_, MUL)
                    tt(res[:, m], res[:, m], lnp[:, 0], MUL)
                    step(dve.tensor_tensor(x_tok[:, m], res[:, m], lnp[:, 1], ADD))
                    dve.sem_inc(s["ln_out"], 1)

            def rest_of(sem_name):
                def add(m):
                    dve.wait_ge(s[sem_name], m + 1)
                    for n in range(2):
                        stt(res[:, m, n * 512:(n + 1) * 512], x_tok[:, m, n * 512:(n + 1) * 512], ALPHA,
                            bank(2 * m + n), MUL, ADD)
                return add

            def ffn_lo(c, j):
                dve.wait_ge(s["ffn_gu_hi" if j < 2 else "ffn_dn_hi"], 2 * c + (j + 1) if j < 2 else c + 1)
                dve.tensor_tensor(ffn_wl[:, j, :], ring[:, j, :], ffn_wh[:, j, :].bitcast(F32),
                                  SUB_).then_inc(s["ffn_gu_lo" if j < 2 else "ffn_dn_lo"], 1)

            for j in range(2):
                ffn_lo(0, j)
            norm(0, rest_of("op_ps"))
            def low_of(o, src, hi):
                return dve.tensor_tensor(o, src, hi.bitcast(F32), SUB_)

            for t in range(4):
                m, half = t // 2, t % 2
                dve.wait_ge(s["xT_sb"], 4 + t + 1)
                low_of(ffn_xl[:, m, 4 * half:4 * half + 4, :].rearrange("z k n -> z (k n)"), bank(6 + t % 2),
                       ffn_xh[:, m, 4 * half:4 * half + 4, :].rearrange("z k n -> z (k n)")).then_inc(s["x1_lo"], 1)

            def ffn_dve(c, first=False, last=False):
                if not last:
                    ffn_lo(c + 1, 0)
                dve.wait_ge(s["ffn_silu"], c + 1)
                if not first:
                    dve.wait_ge(s["ffn_tr"], c)
                dve.tensor_tensor(h[:], sg[:], ps[:, 4:4 + MT, FC:2 * FC], MUL).then_inc(s["ffn_h"], 1)
                if not last:
                    ffn_lo(c + 1, 1)
                ffn_lo(c, 2)
                dve.wait_ge(s["ffn_hT_hi"], c + 1)
                low_of(ffn_hTl[:].rearrange("z m t n -> z (m t n)"), ps[:, 6, 0:MT * FC],
                       ffn_hTh[:].rearrange("z m t n -> z (m t n)")).then_inc(s["ffn_hT_lo"], 1)

            ffn_dve(0, True)
            dve.wait_ge(s["s5_in"], 64)
            cf = Cp.rearrange("z x a b c d -> z x (a b c) d")
            w2f = w2.rearrange("z a b c d -> z (a b c d)")
            ta_, tb_, w2a, w2b = (v[:, 0:NT * CG].rearrange("z (a b) -> z a b", b=CG) for v in (
                ta.rearrange("z a b c -> z (a b c)"), tb.rearrange("z a b c -> z (a b c)"), w2f, w2f[:, NT * CG:]))
            crb, cib = (v.unsqueeze(2).to_broadcast([P, NT, CG]) for v in (cr, ci))
            tt(ta_, cf[:, 0], crb, MUL)
            tt(tb_, cf[:, 1], cib, MUL)
            tt(w2a, cf[:, 0], cib, MUL)
            tt(w2b, cf[:, 1], crb, MUL)
            tt(cf[:, 0], ta_, tb_, SUB_)
            tt(cf[:, 1], w2a, w2b, ADD)
            step(dve.memset(Bz.rearrange("z a b c d -> z (a b c d)"), 0.0))
            for k in range(KT):
                ts(Dd[:, k, :], eye16, Dp[:, k:k + 1], None, MUL)

            def s5_out_side(k, first):
                C_, P_ = ([ksel(v, x, k) for x in (0, 1)] for v in (Cp, p2))
                cb = [v.unsqueeze(2).to_broadcast([P, 2 * PR, L + 1, CG]) for v in C_]
                pb = [v.unsqueeze(3).to_broadcast([P, 2 * PR, L + 1, CG]) for v in P_]
                tt(ta, cb[0], pb[0], MUL)
                tt(tb, cb[1], pb[1], MUL)
                if not first:
                    dve.wait_ge(s["s5_free"], 16 * k)
                    dve.wait_ge(s["kgen_ps"], k)
                tt(w2[:, 0], ta, tb, SUB_)
                tt(ta, cb[0], pb[1], MUL)
                tt(tb, cb[1], pb[0], MUL)
                flat = lambda v: v.rearrange("z a b c -> z (a b c)")
                stt(flat(w2[:, 1]), flat(ta), -1.0, flat(tb), MUL, SUB_)
                dve.sem_inc(s["s5_w2"], 1)
                for x in range(2):
                    for g2 in range(2):
                        step(dve.tensor_copy(Bz[64 * g2:64 * g2 + 64, x, :, g2, :],
                                             ksel(Bp, x, k)[64 * g2:64 * g2 + 64]))
                dve.sem_inc(s["s5_bz"], 1)

            def s5_kernels(k, first):
                dve.wait_ge(s["kgen_ps"], k + 1)
                if not first:
                    dve.wait_ge(s["t_out"], 16 * L * k)
                kf = ps[:, 7, 0:P].rearrange("z (l c) -> z l c", c=CG)
                kb = ps[:, 7, P:2 * P].rearrange("z (l c) -> z l c", c=CG)
                step(dve.tensor_copy(kext[:, 0:L], kb))
                step(dve.tensor_copy(kext[:, L:2 * L - 1], kf[:, 1:L]))
                tt(kext[:, L - 1], kf[:, 0], kext[:, L - 1], ADD)
                step(dve.tensor_tensor(kext[:, L - 1], kext[:, L - 1],
                                       Dd[:, bass.ds(k, 1)].rearrange("z o c -> z (o c)"), ADD))
                dve.sem_inc(s["s5_kx"], 1)
                dve.sem_inc(s["kext_sb"], 1)

            ffn_dve(1)
            s5_out_side(0, True)
            ffn_dve(CHUNK_A)
            before = step.n
            s5_kernels(0, True)
            s5_out_side(1, False)
            ffn_dve(CHUNK_A + 1)
            per_turn = step.n - before
            with dve.Fori(2, KT) as k:
                step.loop(k - 2, per_turn)
                s5_kernels(k - 1, False)
                s5_out_side(k, False)
                ffn_dve(k + CHUNK_A)
            step.end_loop(KT - 2)
            s5_kernels(KT - 1, False)
            ffn_dve(NCH - 1, last=True)
            norm(1, rest_of("ffn_tile"))
            for x in range(2):
                dve.wait_ge(s[f"xk_in{x}"], 64)
                step(dve.tensor_copy(xg[:, x], xl[:, x].rearrange("z j (g c) -> z g j c", c=CG)))
                dve.sem_inc(s["xg_ok"], 1)
            step(dve.memset(Sz.rearrange("z a b c d e -> z (a b c d e)"), 0.0))
            for half in range(2):
                step(dve.memset(S[:, half, :, 0], 0.0))
            for half in range(2):
                dve.wait_ge(s["s_sb"], (half + 1) * KT)
                a8v = a8[:, half].rearrange("z d o i t -> z d o (i t)")
                for i in range(1, NC):
                    tt(pd, a8v, S[:, half, :, i].unsqueeze(2).to_broadcast([P, 2, 2, 2 * HT]), MUL)
                    for x in range(2):
                        cur = S[:, half, :, i + 1].rearrange("z d (o t) -> z d o t", o=2)
                        tt(cur, cur, pd[:, :, :, x * HT:(x + 1) * HT], ADD)
                for d in range(2):
                    for ri in range(2):
                        for g2 in range(2):
                            at = slice(0, NC) if d == 0 else slice(NC - 1, None, -1)
                            src = S[64 * g2:64 * g2 + 64, half, d, at, ri * HT:(ri + 1) * HT].rearrange("z n t -> z t n")
                            step(dve.tensor_copy(
                                Sz[64 * g2:64 * g2 + 64, d, ri, half * HT:(half + 1) * HT, g2, :], src))
                            dve.sem_inc(s["sz_ok"], 1)

            for c in range(GLU_CH):
                for m in range(MT):
                    dve.wait_ge(s["glu_sig"], 2 * c + m + 1)
                    if c == 0 and m == 0:
                        dve.wait_ge(s["yt_ps"], KT)
                    col = slice(c * FC, (c + 1) * FC)
                    step(dve.tensor_tensor(h[:, m, :], sg[:, m, :], ps[:, m, 0:FC], MUL))
                    dve.sem_inc(s["glu_z"], 1)
                    stt(res[:, m, col], x_tok[:, m, col], ALPHA, h[:, m, :], MUL, ADD)
            norm(2, lambda m: None)
            dve.wait_ge(s["rt_ps"], 1)
            lg, mx8 = rt[:, :, 8:16], rt[:, :, 16:24]
            tpf, m1, m2 = rt[:, :, 24:32], rt[:, :, 32:40], rt[:, :, 40:48]
            step(dve.tensor_copy(lg, ps[:, 5, 0:16].rearrange("z (m e) -> z m e", m=MT)))
            for m in range(MT):
                step(dve.max(mx8[:, m], lg[:, m]))
                step(dve.max_index(top_i[:, m], mx8[:, m], lg[:, m]))
                step(dve.tensor_copy(tpf[:, m], top_i[:, m]))
            tt(rt[:, :, 0:1], rt[:, :, 17:18], rt[:, :, 16:17], SUB_)
            dve.sem_inc(s["rt_ps"], 1)
            dve.wait_ge(s["rt_ps"], 3)
            ts(rt[:, :, 2:3], rt[:, :, 1:2], 1.0, None, ADD)
            step(dve.reciprocal(rt[:, :, 3:4], rt[:, :, 2:3]))
            tt(rt[:, :, 4:5], rt[:, :, 1:2], rt[:, :, 3:4], MUL)
            for m in range(MT):
                ts(m1[:, m], iota8[:], tpf[:, m, 0:1], None, ALU.is_equal)
                ts(m2[:, m], iota8[:], tpf[:, m, 1:2], None, ALU.is_equal)
                tt(sel[:, m], m1[:, m], m2[:, m], ADD)
            step(dve.memset(ones[:], 1.0))
            dve.sem_inc(s["sel_ok"], 1)
            for m in range(MT):
                ts(m1[:, m], m1[:, m], rt[:, m, 3:4], None, MUL)
                stt(comb[:, m], m2[:, m], rt[:, m, 4:5], m1[:, m], MUL, ADD)
            for v in (posx, selx, combx):
                step(dve.memset(v[:], 0.0))
            step(dve.tensor_copy(selx[:, :, 1:1 + NE], sel[:]))
            step(dve.tensor_copy(combx[:, :, 1:1 + NE], comb[:]))
            dve.wait_ge(s["rank_ps"], 1)
            pos = rt[:, :, 48:56]
            step(dve.tensor_copy(pos, ps[:, 7, 0:2 * NE].rearrange("z (m e) -> z m e", m=MT)))
            step(dve.tensor_copy(posx[:, :, 1:1 + NE], pos))
            cnt, rank, hot, tmp = (over[:, x, :] for x in range(4))
            ts(cnt, ps[:, 7, 2 * NE:3 * NE], float(P), None, ALU.is_gt)
            step(dve.memset(rank, 0.0))
            for e in range(1, NE):
                tt(rank[:, e:e + 1], rank[:, e - 1:e], cnt[:, e - 1:e], ADD)
            nf = over[:, 4, :]
            step(dve.memset(nf, 0.0))
            tt(nf[:, 0:1], rank[:, NE - 1:NE], cnt[:, NE - 1:NE], ADD)
            for i in range(NOV):
                stt(hot, rank, float(i), cnt, ALU.is_equal, MUL)
                tt(tmp, hot, iota8[:], MUL)
                step(dve.tensor_reduce(nf[:, 1 + i:2 + i], tmp, AX.X, ADD))
                for dst, src in ((posx, pos), (selx, sel[:]), (combx, comb[:])):
                    tt(m1, src, hot.unsqueeze(1).to_broadcast([P, MT, NE]), MUL)
                    step(dve.tensor_reduce(dst[:, :, 1 + NE + i:2 + NE + i], m1, AX.X, ADD))
            ts(posx[:, :, 1 + NE:TURNS], posx[:, :, 1 + NE:TURNS], -float(P), None, ADD)
            step(dve.tensor_copy(over_i[:], nf[:, 0:2 + NOV]))

            def tokens_hot(turn):
                for m in range(MT):
                    at = bass.ds(turn, 1)
                    ins = dve.tensor_scalar(pg[:, m, :], iotaP[:], posx[:, m, at], selx[:, m, at],
                                            ALU.is_equal, MUL)
                ins.then_inc(s["hot_ok"], 1)

            def add_outputs(turn):
                for m, b0 in ((0, 2), (1, 0)):
                    dve.wait_ge(s["put_ps"], 2 * turn + (m - 1))
                    dve.wait_ge(s["acc_ok"], 2 * turn + m)
                    dve.tensor_tensor(res[:, m].rearrange("z (b n) -> z b n", b=2), ps[:, b0:b0 + 2, :],
                                      res[:, m].rearrange("z (b n) -> z b n", b=2), ADD).then_inc(s["acc_ok"], 1)

            def expert_dve(turn):
                def after_chunk(c):
                    if c == 0:
                        add_outputs(turn)
                    if c == 4:
                        at = bass.ds(turn, 1)
                        for m in range(MT):
                            dve.tensor_scalar(pgc[:, m, :], iotaP[:], posx[:, m, at], combx[:, m, at],
                                              ALU.is_equal, MUL)
                        dve.wait_ge(s["gath_ps"], 2 * turn)
                        tokens_hot(turn + 1)

                swiglu_dve(dve, turn, after_chunk)
                tokens_low(turn + 1)

            def tokens_low(turn):
                for x, b in enumerate((5, 7)):
                    dve.wait_ge(s["xe_hi"], 2 * turn + (x - 1))
                    low_of(xl_[:, x * KT // 2:(x + 1) * KT // 2].rearrange("z k n -> z (k n)"), bank(b),
                           xh[:, x * KT // 2:(x + 1) * KT // 2].rearrange("z k n -> z (k n)")
                           ).then_inc(s["xe_lo"], 1)

            for n, v in (("h_ok", 1), ("hT_lo", 1), ("dn_lo", 1), ("gu_lo", 2)):
                dve.sem_inc(s[n], v * NCH)
            for j in range(2):
                split_lo(dve, NCH, j, (MOE_ITEM0 + j) % R)
            ts(res[:, 0], x_tok[:, 0], ALPHA, None, MUL)
            ts(res[:, 1], x_tok[:, 1], ALPHA, None, MUL)
            dve.sem_inc(s["acc_ok"], 2)
            step(dve.memset(scat, 0.0))
            dve.sem_inc(s["scat_sb"], 1)
            step(dve.memset(ysb, 0.0))
            dve.sem_inc(s["ysb_ok"], 1)
            tokens_hot(1)
            dve.wait_ge(s["hot_ok"], 1)
            dve.sem_inc(s["route_ok"], 1)
            tokens_low(1)
            with dve.Fori(1, 1 + NE) as turn:
                expert_dve(turn)
            n_over = dve.value_load(over_i[0:1, 0:1], min_val=0, max_val=NOV)
            with dve.Fori(0, NOV) as i:
                with dve.If(i < n_over):
                    expert_dve(i + (1 + NE))
            add_outputs(n_over + (1 + NE))
            dve.wait_ge(s["acc_ok"], 2 * n_over + (4 + 2 * NE))
            norm(3, lambda m: None)
            dve.sem_inc(s["fin"], 2)


def layouts(inp):
    g = {k: np.asarray(v) for k, v in inp.items()}
    c = np.ascontiguousarray

    def by_k(w):
        return c(w.reshape(-1, P, w.shape[1]).transpose(1, 0, 2).reshape(P, -1))

    def swiglu_chunks(wg, wu, wd):
        e = wg.shape[0]
        gu = np.stack([w.reshape(e, KT, P, NCH, FC) for w in (wg, wu)], axis=4)
        gu = gu.reshape(e, 2, KT // 2, P, NCH, 2, FC).transpose(0, 4, 1, 3, 2, 5, 6).reshape(e, NCH, 2, P, ITEM)
        dn = wd.reshape(e, NCH, 1, SUB, P, D).transpose(0, 1, 2, 4, 3, 5).reshape(e, NCH, 1, P, ITEM)
        return c(np.concatenate([gu, dn], axis=2)).reshape(e * ITEMS, P, ITEM)

    o = {"x": c(g["x"][0])}
    o["w_in"], o["w_out"] = by_k(g["mix_w_in"][0]), by_k(g["mix_w_out"][0])
    o["w_router"] = by_k(g["router_w"][0])
    o["ln_g"], o["ln_b"] = c(g["ln_g"].reshape(4, D)), c(g["ln_b"].reshape(4, D))
    o["sguT"] = c(g["sgu_w"][0].transpose(2, 0, 1).reshape(P, G * P))
    o["sgub"] = c(g["sgu_b"][0].T)
    o["sgln"] = c(np.concatenate([g["sgu_ln_g"][0].reshape(1, -1), g["sgu_ln_b"][0].reshape(1, -1)], axis=1))
    o["sink"] = c(g["attn_sink"])
    o["ffn_w"] = swiglu_chunks(g["ffn_w_gate"], g["ffn_w_up"], g["ffn_w_down"])
    o["moe_w"] = swiglu_chunks(g["moe_w_gate"][0], g["moe_w_up"][0], g["moe_w_down"][0])
    glu = np.stack([g[n][0].reshape(KT, P, GLU_CH, FC) for n in ("glu_w_val", "glu_w_gate")], axis=3)
    glu = glu.reshape(2, KT // 2, P, GLU_CH, 2, FC).transpose(3, 0, 2, 1, 4, 5)
    o["glu_w"] = c(glu).reshape(GLU_ITEMS, P, ITEM)
    def groups(w):
        return w.reshape((2, KT, PR, 2) + w.shape[2:])
    o["s5_b"] = c(np.stack([groups(g[n][0]).transpose(3, 4, 1, 0, 2, 5) for n in ("s5_b_re", "s5_b_im")], axis=2).reshape(P, -1))
    o["s5_c"] = c(np.stack([groups(g[n][0]).transpose(3, 5, 1, 0, 2, 4) for n in ("s5_c_re", "s5_c_im")], axis=2).reshape(P, -1))
    ldt = np.broadcast_to(g["s5_log_dt"][0][:, :, None], (2, 64, PS))
    o["s5_lamdt"] = c(np.stack([groups(v).transpose(3, 4, 1, 0, 2) for v in (g["s5_lam_re"][0], g["s5_lam_im"][0], ldt)], axis=2).reshape(P, 3, NT))
    o["s5_d"] = c(g["s5_d"][0].reshape(KT, P).T)
    o["ident"] = np.eye(P, dtype=np.float32)
    o["eye16"] = c(np.tile(np.eye(CG, dtype=np.float32), (8, 1)))
    o["iota8"] = c(np.tile(np.arange(NE, dtype=np.float32), (P, 1)))
    o["iotaP"] = c(np.tile(np.arange(P, dtype=np.float32), (P, 1)))
    o["tri"] = np.triu(np.ones((P, P), np.float32), 1)
    pos = np.arange(SEQ, dtype=np.float32)
    inv = (10000.0 ** (-np.arange(0, HD, 2, dtype=np.float32) / HD)).astype(np.float32)
    ang = pos[:, None] * inv[None, :]
    o["cossin"] = c(np.stack([np.cos(ang), np.sin(ang)], 1).reshape(MT, P, 2, HD // 2).transpose(1, 0, 2, 3).reshape(P, -1))
    dist = np.abs(pos[:, None] - pos[None, :])
    o["mask"] = c(np.where(dist <= 128, 0.0, NEG).astype(np.float32).reshape(MT, P, SEQ).transpose(1, 0, 2).reshape(P, -1))
    return o


def kernel(**inputs):
    import concourse.bacc as _bacc
    from concourse import bass_utils as _bu

    nc = _bacc.Bacc("TRN2", target_bir_lowering=False, num_devices=1)
    arrays = layouts(inputs)
    aps = {n: nc.dram_tensor("in_" + n, v.shape, mybir.dt.from_np(v.dtype), kind="ExternalInput").ap() for n, v in arrays.items()}
    out = nc.dram_tensor("out", (SEQ, D), F32, kind="ExternalOutput").ap()
    build(nc, aps, out)
    got = _bu.run_bass_kernel_spmd(nc, [{"in_" + n: v for n, v in arrays.items()}], core_ids=[0])
    return got.results[0]["out"].reshape(1, SEQ, D)
```
